# Optimizing a Trainium2 kernel written in Bass

```python
import math
import jax, jax.numpy as jnp
from jax import lax
import numpy as np

D_MODEL = 2048
BATCH = 1
SEQ = 512
DEPTH = 2
DEC_BATCH = 8
DEC_SEQ = 4
PAST_LEN = 1024
PAGE_SIZE = 128

N_EVEN = (DEPTH + 1) // 2
N_ODD = DEPTH // 2
WINDOW = 128
HD_A = 64
H_A = (D_MODEL // 2) // HD_A
H_A_KV = max(1, H_A // 8)
G_A = H_A // H_A_KV
W_A = H_A * HD_A
NUM_BUCKETS = 32
MAX_DISTANCE = 128
H_B = 4
DV_B = (D_MODEL // 2) // H_B
DK_B = DV_B // 2
W_B = H_B * DV_B
GLA_RANK = 16
GLA_TAU = 16.0
GLA_CHUNK = 64
H_C = 8
DK_C = D_MODEL // H_C
DV_C = 2 * DK_C
W_C = H_C * DV_C
RET_CHUNK = 128
ROPE_BASE = 10000.0
EPS = 1e-6
NEG_INF = -1e30
EVEN_SPLITS = (W_A, H_A_KV * HD_A, H_A_KV * HD_A, W_A, H_B * DK_B, H_B * DK_B, W_B, W_B, GLA_RANK)
ODD_SPLITS = (H_C * DK_C, H_C * DK_C, W_C, W_C)

kernel_name = "hybrid_swa_gla_retention_decode_step"

def rms_norm(x, g):
    xf = x.astype(jnp.float32)
    y = xf * lax.rsqrt(jnp.mean(xf * xf, axis=-1, keepdims=True) + EPS)
    return (y * g.astype(jnp.float32)).astype(x.dtype)

def split_cols(x, sizes):
    idx = [int(i) for i in np.cumsum(sizes)[:-1]]
    return jnp.split(x, idx, axis=-1)

def ada_norm(x, c, ada_w, ada_b, norm_g):
    mod = jax.nn.silu(c) @ ada_w + ada_b
    shift, scale, gate = jnp.split(mod, 3, axis=-1)
    h = rms_norm(x, norm_g) * (1 + scale[:, None]) + shift[:, None]
    return h, gate[:, None]

def t5_bucket(dist):
    dist = jnp.maximum(dist, 0)
    max_exact = NUM_BUCKETS // 2
    log_ratio = jnp.log(jnp.maximum(dist, 1).astype(jnp.float32) / max_exact) / math.log(MAX_DISTANCE / max_exact)
    large = max_exact + (log_ratio * (NUM_BUCKETS - max_exact)).astype(jnp.int32)
    large = jnp.minimum(large, NUM_BUCKETS - 1)
    return jnp.where(dist < max_exact, dist, large)

def rel_bias_for(dist, rel_bias):
    b = rel_bias[t5_bucket(dist)].astype(jnp.float32)
    return jnp.moveaxis(b, -1, 0).reshape(H_A_KV, G_A, *dist.shape)

def sink_attention(q, k, v, bias, mask, sinks):
    s = jnp.einsum('...qkgd,...skd->...kgqs', q, k).astype(jnp.float32) * HD_A ** -0.5 + bias
    s = jnp.where(mask, s, NEG_INF)
    sink = sinks.astype(jnp.float32).reshape(H_A_KV, G_A)[:, :, None, None]
    m = jnp.maximum(jnp.max(s, axis=-1, keepdims=True), sink)
    p = jnp.exp(s - m)
    denom = jnp.sum(p, axis=-1, keepdims=True) + jnp.exp(sink - m)
    return jnp.einsum('...kgqs,...skd->...qkgd', (p / denom).astype(v.dtype), v)

def swa_prompt(q, k, v, sinks, rel_bias):
    b, length = q.shape[:2]
    nb = length // WINDOW
    qb = q.reshape(b, nb, WINDOW, H_A_KV, G_A, HD_A)
    kb = k.reshape(b, nb, WINDOW, H_A_KV, HD_A)
    vb = v.reshape(b, nb, WINDOW, H_A_KV, HD_A)
    pad = ((0, 0), (1, 0), (0, 0), (0, 0), (0, 0))
    kk = jnp.concatenate([jnp.pad(kb[:, :-1], pad), kb], axis=2)
    vv = jnp.concatenate([jnp.pad(vb[:, :-1], pad), vb], axis=2)
    i = jnp.arange(WINDOW)
    s = jnp.arange(2 * WINDOW)
    dist = WINDOW + i[:, None] - s[None, :]
    kpos = (jnp.arange(nb)[:, None] - 1) * WINDOW + s[None, :]
    mask = ((dist >= 0) & (dist <= WINDOW))[None] & (kpos >= 0)[:, None, :]
    bias = rel_bias_for(dist, rel_bias)
    o = sink_attention(qb, kk, vv, bias, mask[:, None, None], sinks)
    return o.reshape(b, length, W_A)

def swa_sample(q, k, v, win_k, win_v, sinks, rel_bias):
    bd, length = q.shape[:2]
    w_buf = win_k.shape[1]
    kk = jnp.concatenate([win_k, k], axis=1)
    vv = jnp.concatenate([win_v, v], axis=1)
    qpos = PAST_LEN + jnp.arange(length)
    kpos = PAST_LEN - w_buf + jnp.arange(w_buf + length)
    dist = qpos[:, None] - kpos[None, :]
    mask = (dist >= 0) & (dist <= WINDOW)
    bias = rel_bias_for(dist, rel_bias)
    o = sink_attention(q.reshape(bd, length, H_A_KV, G_A, HD_A), kk, vv, bias, mask, sinks)
    return o.reshape(bd, length, W_A), kk[:, -w_buf:], vv[:, -w_buf:]

def pick_chunk(length, chunk):
    return chunk if length % chunk == 0 else length

def run_chunks(step, s0, xs, chunk):
    b, length = xs[0].shape[:2]
    n = length // chunk
    xs_c = tuple(jnp.moveaxis(a.reshape(b, n, chunk, *a.shape[2:]), 1, 0) for a in xs)
    s, ys = lax.scan(lambda carry, blk: step(carry, *blk), s0, xs_c)
    ys = jnp.moveaxis(ys, 0, 1)
    return ys.reshape(b, length, *ys.shape[3:]), s

def gla_step(s, q, k, v, la):
    c = q.shape[1]
    bcum = jnp.cumsum(la, axis=1)
    qt = q * jnp.exp(bcum)
    kt = k * jnp.exp(-bcum)
    causal = jnp.tril(jnp.ones((c, c), dtype=bool))
    a = jnp.where(causal, jnp.einsum('bqhd,bshd->bhqs', qt, kt), 0.0)
    o = jnp.einsum('bhqs,bshe->bqhe', a, v) + jnp.einsum('bqhd,bhde->bqhe', qt, s)
    blast = bcum[:, -1]
    k_dec = k * jnp.exp(blast[:, None] - bcum)
    s_new = jnp.exp(blast)[..., None] * s + jnp.einsum('bshd,bshe->bhde', k_dec, v)
    return s_new, o

def retention_step(s, q, k, v, log_gamma):
    c = q.shape[1]
    i = jnp.arange(c, dtype=jnp.float32)
    dist = i[:, None] - i[None, :]
    decay = jnp.where(dist >= 0, jnp.exp(jnp.maximum(dist, 0.0)[None] * log_gamma[:, None, None]), 0.0)
    a = jnp.einsum('bqhd,bshd->bhqs', q, k) * decay
    inner = jnp.exp((i + 1.0)[:, None] * log_gamma[None, :])[None, :, :, None]
    o = jnp.einsum('bhqs,bshe->bqhe', a, v) + inner * jnp.einsum('bqhd,bhde->bqhe', q, s)
    k_dec = k * jnp.exp((c - 1.0 - i)[:, None] * log_gamma[None, :])[None, :, :, None]
    s_new = jnp.exp(c * log_gamma)[None, :, None, None] * s + jnp.einsum('bshd,bshe->bhde', k_dec, v)
    return s_new, o

def rotary(x, pos):
    half = x.shape[-1] // 2
    inv = ROPE_BASE ** (-jnp.arange(half, dtype=jnp.float32) / half)
    ang = pos.astype(jnp.float32)[:, None] * inv[None, :]
    cos = jnp.cos(ang)[None, :, None]
    sin = jnp.sin(ang)[None, :, None]
    xf = x.astype(jnp.float32)
    x1, x2 = xf[..., :half], xf[..., half:]
    return jnp.concatenate([x1 * cos - x2 * sin, x2 * cos + x1 * sin], axis=-1)

def even_layer(x, c, win_k, win_v, gla_s0, rel_bias, ada_w, ada_b, norm_g, w_in, w_lr, b_lr, qn_g, kn_g, sinks, gla_g, w_out):
    b, length = x.shape[:2]
    h, gate = ada_norm(x, c, ada_w, ada_b, norm_g)
    qa, ka, va, ga, qb, kb, vb, gb, lr = split_cols(h @ w_in, EVEN_SPLITS)
    qa = rms_norm(qa.reshape(b, length, H_A, HD_A), qn_g)
    ka = rms_norm(ka.reshape(b, length, H_A_KV, HD_A), kn_g)
    va = va.reshape(b, length, H_A_KV, HD_A)
    qb = qb.reshape(b, length, H_B, DK_B).astype(jnp.float32) * DK_B ** -0.5
    kb = kb.reshape(b, length, H_B, DK_B).astype(jnp.float32)
    vb = vb.reshape(b, length, H_B, DV_B).astype(jnp.float32)
    la = (jax.nn.log_sigmoid((lr @ w_lr + b_lr).astype(jnp.float32)) / GLA_TAU).reshape(b, length, H_B, DK_B)
    if win_k is None:
        oa = swa_prompt(qa, ka, va, sinks, rel_bias)
        new_k, new_v = ka[:, -WINDOW:], va[:, -WINDOW:]
        s0 = jnp.zeros((b, H_B, DK_B, DV_B), jnp.float32)
        state_dtype = x.dtype
    else:
        oa, new_k, new_v = swa_sample(qa, ka, va, win_k, win_v, sinks, rel_bias)
        s0 = gla_s0.astype(jnp.float32)
        state_dtype = gla_s0.dtype
    ob, s_new = run_chunks(gla_step, s0, (qb, kb, vb, la), pick_chunk(length, GLA_CHUNK))
    ob = rms_norm(ob, gla_g).astype(x.dtype).reshape(b, length, W_B)
    mixed = jnp.concatenate([oa * jax.nn.silu(ga), ob * jax.nn.silu(gb)], axis=-1)
    return x + gate * (mixed @ w_out), new_k, new_v, s_new.astype(state_dtype)

def odd_layer(x, c, ret_s0, pos, ada_w, ada_b, norm_g, w_in, ret_g, w_out):
    b, length = x.shape[:2]
    h, gate = ada_norm(x, c, ada_w, ada_b, norm_g)
    q, k, v, g = split_cols(h @ w_in, ODD_SPLITS)
    q = rotary(q.reshape(b, length, H_C, DK_C), pos)
    k = rotary(k.reshape(b, length, H_C, DK_C), pos) * DK_C ** -0.5
    v = v.reshape(b, length, H_C, DV_C).astype(jnp.float32)
    log_gamma = jnp.log1p(-jnp.exp2(-5.0 - jnp.arange(H_C, dtype=jnp.float32)))
    if ret_s0 is None:
        s0 = jnp.zeros((b, H_C, DK_C, DV_C), jnp.float32)
        state_dtype = x.dtype
    else:
        s0 = ret_s0.astype(jnp.float32)
        state_dtype = ret_s0.dtype
    step = lambda s, qc, kc, vc: retention_step(s, qc, kc, vc, log_gamma)
    o, s_new = run_chunks(step, s0, (q, k, v), pick_chunk(length, RET_CHUNK))
    o = rms_norm(o, ret_g).astype(x.dtype).reshape(b, length, W_C) * jax.nn.silu(g)
    return x + gate * (o @ w_out), s_new.astype(state_dtype)

def setup_inputs(seed: int = 0) -> dict:
    key = jax.random.key(seed)
    ks = iter(jax.random.split(key, 32))

    def nrm(shape, scale=1.0):
        return jax.random.normal(next(ks), shape, jnp.float32) * scale

    def gain(shape):
        return 1.0 + nrm(shape, 0.02)

    w_buf = min(WINDOW, PAST_LEN)
    d_in_even = sum(EVEN_SPLITS)
    d_in_odd = sum(ODD_SPLITS)
    return {
        "x_prompt": nrm((BATCH, SEQ, D_MODEL)),
        "x_sample": nrm((DEC_BATCH, DEC_SEQ, D_MODEL)),
        "cache_swa_k": nrm((N_EVEN, DEC_BATCH, w_buf, H_A_KV, HD_A)),
        "cache_swa_v": nrm((N_EVEN, DEC_BATCH, w_buf, H_A_KV, HD_A)),
        "state_gla": nrm((N_EVEN, DEC_BATCH, H_B, DK_B, DV_B), 0.5),
        "state_ret": nrm((N_ODD, DEC_BATCH, H_C, DK_C, DV_C), 0.5),
        "c_prompt": nrm((BATCH, D_MODEL)),
        "c_sample": nrm((DEC_BATCH, D_MODEL)),
        "rel_bias": nrm((NUM_BUCKETS, H_A), 0.5),
        "ada_w_even": nrm((N_EVEN, D_MODEL, 3 * D_MODEL), 0.5 * D_MODEL ** -0.5),
        "ada_b_even": nrm((N_EVEN, 3 * D_MODEL), 0.02),
        "norm_g_even": gain((N_EVEN, D_MODEL)),
        "w_in_even": nrm((N_EVEN, D_MODEL, d_in_even), D_MODEL ** -0.5),
        "w_lr_even": nrm((N_EVEN, GLA_RANK, H_B * DK_B), GLA_RANK ** -0.5),
        "b_lr_even": nrm((N_EVEN, H_B * DK_B), 0.02),
        "qn_g_even": gain((N_EVEN, HD_A)),
        "kn_g_even": gain((N_EVEN, HD_A)),
        "sinks_even": nrm((N_EVEN, H_A), 0.5),
        "gla_g_even": gain((N_EVEN, DV_B)),
        "w_out_even": nrm((N_EVEN, W_A + W_B, D_MODEL), (W_A + W_B) ** -0.5),
        "ada_w_odd": nrm((N_ODD, D_MODEL, 3 * D_MODEL), 0.5 * D_MODEL ** -0.5),
        "ada_b_odd": nrm((N_ODD, 3 * D_MODEL), 0.02),
        "norm_g_odd": gain((N_ODD, D_MODEL)),
        "w_in_odd": nrm((N_ODD, D_MODEL, d_in_odd), D_MODEL ** -0.5),
        "ret_g_odd": gain((N_ODD, DV_C)),
        "w_out_odd": nrm((N_ODD, W_C, D_MODEL), W_C ** -0.5),
    }

def reference(x_prompt, x_sample, cache_swa_k, cache_swa_v, state_gla, state_ret, c_prompt, c_sample, rel_bias,
              ada_w_even, ada_b_even, norm_g_even, w_in_even, w_lr_even, b_lr_even, qn_g_even, kn_g_even,
              sinks_even, gla_g_even, w_out_even, ada_w_odd, ada_b_odd, norm_g_odd, w_in_odd, ret_g_odd, w_out_odd):
    pos_prompt = jnp.arange(x_prompt.shape[1])
    pos_sample = PAST_LEN + jnp.arange(x_sample.shape[1])
    y_prompt, y_sample = x_prompt, x_sample
    swa_k_p, swa_v_p, gla_p, ret_p = [], [], [], []
    swa_k_s, swa_v_s, gla_s, ret_s = [], [], [], []
    for layer in range(DEPTH):
        j = layer // 2
        if layer % 2 == 0:
            ew = (ada_w_even[j], ada_b_even[j], norm_g_even[j], w_in_even[j], w_lr_even[j], b_lr_even[j],
                  qn_g_even[j], kn_g_even[j], sinks_even[j], gla_g_even[j], w_out_even[j])
            y_prompt, kp, vp, sp = even_layer(y_prompt, c_prompt, None, None, None, rel_bias, *ew)
            y_sample, ksm, vsm, ssm = even_layer(y_sample, c_sample, cache_swa_k[j], cache_swa_v[j], state_gla[j], rel_bias, *ew)
            swa_k_p.append(kp); swa_v_p.append(vp); gla_p.append(sp)
            swa_k_s.append(ksm); swa_v_s.append(vsm); gla_s.append(ssm)
        else:
            ow = (ada_w_odd[j], ada_b_odd[j], norm_g_odd[j], w_in_odd[j], ret_g_odd[j], w_out_odd[j])
            y_prompt, rp = odd_layer(y_prompt, c_prompt, None, pos_prompt, *ow)
            y_sample, rsm = odd_layer(y_sample, c_sample, state_ret[j], pos_sample, *ow)
            ret_p.append(rp); ret_s.append(rsm)
    return (y_prompt, y_sample, jnp.stack(swa_k_p), jnp.stack(swa_v_p), jnp.stack(gla_p), jnp.stack(ret_p),
            jnp.stack(swa_k_s), jnp.stack(swa_v_s), jnp.stack(gla_s), jnp.stack(ret_s))


_drawn_inputs = setup_inputs


def setup_inputs(seed=0):
    import zlib

    import numpy as np

    out = dict(_drawn_inputs(seed))
    spreads = {}
    factors = {'rel_bias': 5.401,
     'b_lr_even': 6.316,
     'qn_g_even': 174.958,
     'sinks_even': 200.0,
     'gla_g_even': 8.0,
     'norm_g_odd': 2.81,
     'ret_g_odd': 70.353}
    for name, (base, spread) in spreads.items():
        noise = np.random.default_rng([zlib.crc32(name.encode()), seed]).standard_normal(out[name].shape)
        drawn = base * np.exp(spread * noise) if base else spread * noise
        out[name] = __import__('jax').numpy.asarray(drawn.astype(out[name].dtype))
    for name, factor in factors.items():
        out[name] = (out[name] * factor).astype(out[name].dtype)
    return out
```

```python
from contextlib import ExitStack
import math

import numpy as np
import concourse.bass as bass
from concourse import mybir

ALU = mybir.AluOpType
ACT = mybir.ActivationFunctionType
AX = mybir.AxisListType.X
F32 = mybir.dt.float32
F32R = mybir.dt.float32r

D = 2048
KT = D // 128
SEQ, NB, NQ = 512, 8, 4
NS = NB * NQ
T = SEQ + NS
HALF = T // 2
WIN = 128
NEG = -1.0e30
EPS = 1e-6

C_QA, C_KA, C_VA, C_GA = 0, 1024, 1152, 1280
C_QB, C_KB, C_VB, C_GB, C_LR = 2304, 2816, 3328, 4352, 5376
C_QC, C_KC, C_VC, C_GC = 0, 2048, 4096, 8192
HA, HB, HC = 16, 4, 8
RANK = 16

N_KV = 0
N_A = 3
N_B = N_A + 2 * 8
N_W0 = N_B + 6 * HB
N_C = N_W0 + KT
N_WA = N_C + 12 * HC
N_WB = N_WA + KT
N_END = N_WB + KT

RT_W = T + NS + NB + 5


def shape_constants():
    c = {}
    c["ident"] = np.eye(128, dtype=np.float32)
    c["ones"] = np.ones((128, 128), np.float32)
    i = np.arange(128)
    c["blk64"] = (i[:, None] // 64 == i[None, :] // 64).astype(np.float32)
    same = i[:, None] // 64 == i[None, :] // 64
    c["gmask"] = (same & (i[:, None] <= i[None, :])).astype(np.float32)
    j = np.arange(NS)
    sm = (j[:, None] // NQ == j[None, :] // NQ) & (j[:, None] <= j[None, :])
    smask = np.zeros((128, NS + NB), np.float32)
    smask[:NS, :NS] = sm
    smask[:NS, NS:] = (j[:, None] // NQ == np.arange(NB)[None, :])
    c["smask"] = smask
    dist = 255 - np.arange(384)
    ok = (dist >= 0) & (dist <= WIN)
    dd = np.clip(dist, 0, WIN)
    ratio = np.log(np.maximum(dd, 1).astype(np.float32) / np.float32(16)) / math.log(128 / 16)
    large = np.minimum(16 + (ratio * 16).astype(np.int32), 31)
    bucket = np.where(dd < 16, dd, large)
    hot = np.zeros((33, 384), np.float32)
    hot[bucket[ok], np.nonzero(ok)[0]] = 1.0
    hot[32, ~ok] = NEG
    c["hot"] = hot
    pos = np.concatenate([np.arange(SEQ), 1024 + np.tile(np.arange(NQ), NB)]).astype(np.float32)
    inv = (np.float32(10000.0) ** (-np.arange(128, dtype=np.float32) / np.float32(128))).astype(np.float32)
    ang = (inv[:, None] * pos[None, :]).astype(np.float32).astype(np.float64)
    c["rope"] = np.stack([np.cos(ang), np.sin(ang)], 1).astype(np.float32)
    ret = np.zeros((HC + 1, 128, RT_W), np.float32)
    p = np.arange(128)[:, None].astype(np.float64)
    for h in range(HC):
        lg = math.log1p(-2.0 ** (-5.0 - h))
        dcol = np.arange(SEQ)[None, :] - p
        ret[h, :, :SEQ] = np.where(dcol >= 0, np.exp(np.maximum(dcol, 0) * lg), 0) / 16
        ds = j[None, :] - j[:, None]
        ret[h, :NS, SEQ:T] = np.where(sm, np.exp(np.maximum(ds, 0) * lg), 0) / 16
        ret[h, :, T:T + NS] = np.exp((j % NQ + 1.0) * lg)[None, :]
        ret[h, :NS, T + NS:T + NS + NB] = smask[:NS, NS:] * np.exp((NQ - 1.0 - j % NQ) * lg)[:, None] / 16
        for t in range(4):
            ret[h, :, T + NS + NB + t] = np.exp((SEQ - 1.0 - 128 * t - p[:, 0]) * lg) / 16
        ret[h, :, T + NS + NB + 4] = math.exp(NQ * lg)
    c["ret"] = ret
    return c


def build(nc, I, O, C):
    ctx = ExitStack()
    with ctx:
        def sb(name, shape, dt=F32):
            return ctx.enter_context(nc.sbuf_tensor(name, shape, dt))

        def sem(name):
            return ctx.enter_context(nc.semaphore(name))

        ds = bass.ds
        ident, ones = sb("ident", [128, 128]), sb("ones", [128, 128])
        vecT = sb("vecT", [128, 128])
        vecT2 = sb("vecT2", [128, 24])
        eps = sb("eps", [128, 8])
        mod = [sb("mod_even", [128, 48, 9]), sb("mod_odd", [128, 48, 9])]
        cs = sb("cs", [128, KT, 9])
        G = sb("G", [128, KT, 9])
        WR = sb("W_raw", [128, 4 * KT * 128])
        WH = sb("W_hi", [128, 2, KT, 128], F32R)
        WL = sb("W_lo", [128, 2, KT, 128], F32R)
        AH = sb("act_hi", [128, KT, T], F32R)
        AL = sb("act_lo", [128, KT, T], F32R)
        R3 = sb("tiles", [128, KT, T])
        U = sb("work", [128, 9120])
        U2 = WR[:, 2 * KT * 128:4 * KT * 128]
        slot = [WR[:, s * 2048:(s + 1) * 2048].rearrange("p (k n) -> p k n", k=KT) for s in range(4)]
        slab = [WR[:, s * 4096:(s + 1) * 4096].rearrange("p (k n) -> p k n", k=KT) for s in range(2)]

        def u(at, *shape, base=None):
            n = int(np.prod(shape))
            v = (U if base is None else base)[:, at:at + n]
            if len(shape) == 2:
                v = v.rearrange("p (a b) -> p a b", a=shape[0])
            elif len(shape) == 3:
                v = v.rearrange("p (a b c) -> p a b c", a=shape[0], b=shape[1])
            return v

        PJ = ctx.enter_context(nc.psum_tensor("PJ", [128, 2, 512], F32))
        AD = ctx.enter_context(nc.psum_tensor("AD", [128, 512], F32))
        X = ctx.enter_context(nc.psum_tensor("X", [128, 5, 512], F32))

        def dram(name, shape):
            return nc.dram_tensor(name, shape, F32).ap()

        res_d = [dram("resid0", (KT, 128, T)), dram("resid1", (KT, 128, T)), dram("resid2", (KT, 128, T))]
        mix_d = dram("mixed_odd", (2 * KT, 128, T))
        rel_d = dram("rel_rows", (HA, 384))
        bias_d = dram("bias_tiles", (HA, 128, 256))

        xs = u(0, 2, 2048)
        ssum, sq, rstd = u(4096, T), u(4640, 2, T), u(5728, T)
        tk, ts, hs = u(6272, 2, 512), u(7296, KT, NS), u(7808, KT, NS)
        vr, vr2, vc = u(8320, 128), u(8448, 128), u(8576, 128)
        craw, cexp = u(8704, KT, 9), u(8848, KT, 9)
        KC, PT, PTs, PTn = u(0, NB, 128), u(0, 4, 2, 128), u(0, 4, 128), u(512, 4, 128)
        VCc, KCT = u(1024, NB, 128), u(2048, NB, 128)
        kdup = [u(3072, T), u(3616, T)]
        vtok, vtok_s = u(4160, 4, 128), u(4672, 128)
        blk64, LR, gmask, smask = u(4800, 128), u(4928, T), u(5472, 128), u(5600, NS + NB)
        bmask = smask[:, NS:NS + NB]
        qsT = u(5640, NB, 8, NQ)
        sk, skrow, sk2 = u(5896, 16), u(5912, 1), u(5914, 2)
        mx, nm, den, es, rec = (u(5920 + 4 * n, 4) for n in range(5))
        qg8 = u(5944, 1)
        QT, QN, E = u(5952, T), u(6496, T), u(7040, T)
        S, kn, biasT = u(7584, 4, 256), u(7584, T), u(8608, 2, 256)
        SS, biasS, OSm = u(7584, 4, 160), u(5952, 4, 160), u(7040, 8, NS)
        relb, hot = u(8608, 16), u(2048, 384)
        relS = u(8640, 384)
        BP = u(0, 4, T)
        ST = u(2176, 8, 256)
        LAt, LAs, AT, ATs = u(4224, 4, 128), u(4736, 128), u(4224, 4, 128), u(4736, NS)
        sq1 = u(4224, T)
        WLR = u(5640, 512)
        WLH = u(8808, 128)
        EBP, T1, T2 = u(6152, T), u(6696, T), u(7240, T)
        KDT, KDTs, kdm = u(6152, 4, 128), u(7240, 128), u(7368, 2, 128)
        VTB, VTBs = u(7784, 4, 256), u(8808, 256)
        ebl, blast = u(4864, 16), u(4880, 16)
        resb, yst, wsq = u(0, 2, T), u(1088, 2, T), u(2176, T)
        smp = u(2720, NS)
        ost = u(2760, 2, 5, 128)
        cos, sin = u(0, T), u(544, T)
        CT, CTs, KTK, KTKs = u(1088, 4, 512), u(3136, 512), u(3648, 4, 256), u(4672, 256)
        RT = u(4928, RT_W)
        r1, r2 = u(5520, T), u(6064, T)
        qi = u(6608, 2, NS)
        ckdm = u(6672, 2, 256)
        CST = u(7184, 2, 512)
        r3 = u(8208, T)
        SB = u(0, 4, 2, 512, base=U2)
        RAT, RATs = R3[:, 0:4, :].rearrange("p a b -> p (a b)")[:, 0:1280], \
            R3[:, 0:4, :].rearrange("p a b -> p (a b)")[:, 1280:1280 + NS]
        RAOFF = [0, 512, 896, 1152]

        names = ("vld vld2 xT_ready vec_ps vec_sb xa xd sqd ms rb tset sset hi_t nl nls "
                 "ad_done ad_ev hi lo half ev "
                 "c_exp v_chain a_chain res_st "
                 "kv_ps kv_ms kv_rb kn_ready kdup_ready kv_out_sb kv_st kct_ps kct_sb rel_sb "
                 "rel_st bias_ld "
                 "a_ms a_rb a_qn a_qs a_sc a_sadd a_mxd a_exp a_p a_tp a_ptA a_ptV a_pv a_eg a_gate "
                 "bs_ld s_sc s_mx s_exp s_p s_tp s_pt s_pv s_os s_gate swa_st "
                 "b_wl b_z b_ln b_la b_bc b_eb b_dif b_kdx b_qk b_kd b_at b_vt b_vta b_kt b_kta b_atm b_dS b_st "
                 "b_o b_oe b_so b_sld b_stf b_sup b_ssb b_ms b_rb b_eg b_gate b_kdm b_pst b_sq1 "
                 "wy wssq wsqa wtp wotp "
                 "c_tab c_rot c_sc c_scv c_kt c_kta c_vt c_vta c_vtv c_st c_stv c_o c_oe c_os "
                 "c_km c_up c_upv c_ms c_rb c_eg c_gate c_mst c_ssq c_pst m_hi pool_passed act_passed b_free c_mfree c_pfree ost_free ")
        s = {}
        for n in names.split():
            s[n] = sem(n)
        wld = [sem(f"w_loaded{n}") for n in range(2)]
        adl = [sem(f"ada_tile_loaded{n}") for n in range(2)]
        xld = [sem(f"x_loaded{n}") for n in range(2)]
        rld = [sem(f"resid_loaded{n}") for n in range(2)]
        sld = [sem(f"state_loaded{n}") for n in range(4)]
        sst = [sem(f"state_stored{n}") for n in range(4)]
        yst_s = [sem(f"y_stored{n}") for n in range(2)]
        ost_s = [sem(f"out_stored{n}") for n in range(2)]
        raw = [sem(f"mixed_loaded{n}") for n in range(4)]

        class Chain:

            def __init__(self, eng, sm):
                self.eng, self.sm, self.base, self.total, self.k, self.per = eng, sm, 0, 0, 0, None

            def loop(self, i, per):
                assert self.per is None
                self.total += self.k
                self.base, self.k, self.per = i * per + self.total, 0, per

            def end(self, trips):
                assert self.k == self.per, f"{self.sm}: {self.k} links in the loop, {self.per} declared"
                self.total += self.per * trips
                self.base, self.k, self.per = self.total, 0, None

            def __call__(self, ins):
                self.k += 1
                ins.then_inc(self.sm, 1)
                self.eng.wait_ge(self.sm, self.base + self.k)

        block = ctx.enter_context(nc.Block())

        @block.sync
        def _(sp):
            def load(n, par, src, cols=128):
                if not isinstance(n, int) or n >= 2:
                    sp.wait_ge(s["lo"], n - 1)
                sp.dma_start(slot[par][:, :, 0:cols], src).then_inc(wld[par], 16)

            wie = I["w_in_even"][0].rearrange("(k p) n -> p k n", p=128)
            woe = I["w_out_even"][0].rearrange("(k p) n -> p k n", p=128)
            wio = I["w_in_odd"][0].rearrange("(k p) n -> p k n", p=128)
            woo = I["w_out_odd"][0].rearrange("(k p) n -> p k n", p=128)
            ae = I["ada_w_even"][0].rearrange("(k p) n -> p k n", p=128)
            ao = I["ada_w_odd"][0].rearrange("(k p) n -> p k n", p=128)
            xp = I["x_prompt"][0]
            xsm = I["x_sample"].rearrange("b t d -> (b t) d")
            for t in range(5):
                if t >= 2:
                    sp.wait_ge(s["xT_ready"], 4 * (t - 1))
                if t < 4:
                    sp.dma_start(xs[:, t % 2], xp[t * 128:(t + 1) * 128, :]).then_inc(xld[t % 2], 16)
                else:
                    sp.dma_start(xs[0:NS, 0], xsm).then_inc(xld[0], 16)
                if t == 1:
                    for sl in range(2):
                        sp.dma_start(slab[sl], ae[:, :, sl * 256:(sl + 1) * 256]).then_inc(adl[sl], 16)
            with sp.Fori(1, 8) as i:
                for sl in range(2):
                    sp.wait_ge(s["ad_done"], i * 2 + (sl - 1))
                    sp.dma_start(slab[sl], ae[:, :, ds(i * 512 + sl * 256, 256)]).then_inc(adl[sl], 16)
            sp.wait_ge(s["ad_done"], 15)
            load(0, 0, wie[:, :, C_KA:C_KA + 128])
            load(1, 1, wie[:, :, C_VA:C_VA + 128])
            load(2, 0, wie[:, :, C_LR:C_LR + RANK], RANK)

            def ada_pair(unit, w, col):
                sp.wait_ge(s["ad_done"], unit)
                for e in range(2):
                    sp.dma_start(slot[2 + e], w[:, :, ds(col + 128 * e, 128)]).then_inc(adl[e], 16)

            with sp.Fori(0, 8) as i:
                load(i * 2 + N_A, N_A % 2, wie[:, :, ds(i * 128 + C_QA, 128)])
                ada_pair(i * 1 + 16, ae, i * 256 + 4096)
                load(i * 2 + (N_A + 1), (N_A + 1) % 2, wie[:, :, ds(i * 128 + C_GA, 128)])
            with sp.Fori(0, HB) as h:
                src = (ds(h * 128 + C_QB, 128), ds(h * 128 + C_KB, 128), ds(h * 256 + C_VB, 128),
                       ds(h * 256 + (C_VB + 128), 128), ds(h * 256 + C_GB, 128), ds(h * 256 + (C_GB + 128), 128))
                for j in range(6):
                    load(h * 6 + (N_B + j), (N_B + j) % 2, wie[:, :, src[j]])
                    ada_pair(h * 6 + (24 + j), ao, h * 1536 + 256 * j)

            def out_product(base, w):
                with sp.Fori(0, KT // 2) as m:
                    for j in range(2):
                        load(m * 2 + (base + j), (base + j) % 2, w[:, :, ds(m * 256 + 128 * j, 128)])

            out_product(N_W0, woe)
            with sp.Fori(0, HC) as h:
                src = [ds(h * 256 + (c + 128 * e), 128) for c in (C_QC, C_KC) for e in range(2)] + \
                    [ds(h * 512 + (c + 128 * e), 128) for c in (C_VC, C_GC) for e in range(4)]
                for j in range(12):
                    load(h * 12 + (N_C + j), (N_C + j) % 2, wio[:, :, src[j]])
            out_product(N_WA, woo[:, 0:KT, :])
            out_product(N_WB, woo[:, KT:2 * KT, :])

        @block.gpsimd
        def _(pool):
            def wait_for(sm, value, tell="pool_passed"):
                pool.wait_ge(sm, value)
                pool.sem_inc(s[tell], 1)

            pool.sem_inc(s["b_free"], 1)
            pool.sem_inc(s["c_mfree"], 1)
            pool.sem_inc(s["c_pfree"], 1)
            pool.sem_inc(s["ost_free"], 2)
            for dst, src in ((ident[:, :], C["ident"]), (ones[:, :], C["ones"])):
                pool.dma_start(dst, src).then_inc(s["vld"], 16)
            be, bo = (I[k][0].rearrange("(r c) -> r c", c=128) for k in ("ada_b_even", "ada_b_odd"))
            ge, go = (I[k][0].rearrange("(r c) -> r c", c=128) for k in ("norm_g_even", "norm_g_odd"))
            for a, b, src in ((0, 48, be), (48, 96, bo), (96, 112, ge), (112, 128, go)):
                pool.dma_start(vr[a:b, :], src).then_inc(s["vld"], 16)
            for a, b, src in ((0, 16, I["c_prompt"][0].rearrange("(r c) -> r c", c=128)),
                              (16, 18, I["gla_g_even"][0].rearrange("(r c) -> r c", c=128)),
                              (18, 22, I["ret_g_odd"][0].rearrange("(r c) -> r c", c=128))):
                pool.dma_start(vr2[a:b, :], src).then_inc(s["vld"], 16)
            for e in range(2):
                pool.dma_start(vr2[22:23, 64 * e:64 * e + 64], I["qn_g_even"]).then_inc(s["vld"], 16)
                pool.dma_start(vr2[23:24, 64 * e:64 * e + 64], I["kn_g_even"]).then_inc(s["vld"], 16)
            pool.dma_start(vc[:, :], I["c_sample"].rearrange("b (r c) -> (b r) c", c=128)).then_inc(s["vld"], 16)
            pool.wait_ge(s["xa"], 10)
            pool.wait_ge(s["xd"], 10)
            pool.dma_start(res_d[0].rearrange("k p t -> p k t"), R3[:, :, :]).then_inc(s["res_st"], 16)
            pool.wait_ge(s["nl"], KT)
            pool.wait_ge(s["nls"], 1)
            kc = I["cache_swa_k"][0].rearrange("b s k d -> s b (k d)")
            vcc = I["cache_swa_v"][0].rearrange("b s k d -> s b (k d)")
            pool.dma_start(KC, kc).then_inc(s["vld2"], 16)
            pool.dma_start(VCc, vcc).then_inc(s["vld2"], 16)
            pool.dma_start(blk64, C["blk64"]).then_inc(s["vld2"], 16)
            pool.dma_start(gmask, C["gmask"]).then_inc(s["vld2"], 16)
            pool.dma_start(smask, C["smask"]).then_inc(s["vld2"], 16)
            pool.dma_start(hot[0:33], C["hot"]).then_inc(s["vld2"], 16)
            pool.dma_start(relb[0:32], I["rel_bias"]).then_inc(s["vld2"], 16)
            sinks = I["sinks_even"]
            pool.dma_start(sk[:, :], bass.AP(sinks.tensor, 0, [[0, 128], [1, HA]])).then_inc(s["vld2"], 16)
            with nc.allow_non_contiguous_dma(reason="one sink per row"):
                for e in range(2):
                    pool.dma_start(skrow[64 * e:64 * e + 64, :],
                                   bass.AP(sinks.tensor, 0, [[1, HA], [0, NQ], [1, 1]])).then_inc(s["vld2"], 16)
            for k, src in ((6, I["cache_swa_k"]), (7, I["cache_swa_v"])):
                pool.dma_start(O[k][0][:, 0:WIN - NQ], src[0][:, NQ:WIN]).then_inc(s["swa_st"], 16)
            pool.wait_ge(s["rel_sb"], 1)
            pool.dma_start(rel_d, relS[0:HA, :]).then_inc(s["rel_st"], 16)
            pool.wait_ge(s["rel_st"], 16)
            pool.dma_start(bias_d, bass.AP(rel_d.tensor, 127, [[384, HA], [-1, 128], [1, 256]])).then_inc(s["rel_st"], 16)
            pool.wait_ge(s["kv_out_sb"], 2)
            pool.dma_start(O[2][0, 0].rearrange("s k d -> s (k d)"), E[:, 0:128]).then_inc(s["kv_st"], 16)
            pool.dma_start(O[6][0][:, WIN - NQ:WIN].rearrange("b t k d -> b t (k d)"), E[0:NS, 128:256]).then_inc(s["kv_st"], 16)
            pool.dma_start(O[3][0, 0].rearrange("s k d -> s (k d)"), vtok[:, 3]).then_inc(s["kv_st"], 16)
            pool.dma_start(O[7][0][:, WIN - NQ:WIN].rearrange("b t k d -> b t (k d)"), vtok_s[0:NS]).then_inc(s["kv_st"], 16)
            pool.wait_ge(s["rel_st"], 32)
            pool.wait_ge(s["kv_st"], 64)

            def load_bias(i):
                pool.dma_start(biasT, bias_d[ds(i * 2, 2)].rearrange("h i s -> i h s")).then_inc(s["bias_ld"], 16)

            load_bias(0)
            with pool.Fori(1, 8) as i:
                wait_for(s["a_sadd"], i * 2)
                load_bias(i)
            pool.wait_ge(s["bs_ld"], 1)
            with nc.allow_non_contiguous_dma(reason="small bias rows"):
                for e in range(2):
                    for p in range(4):
                        r = slice(64 * e, 64 * e + 64)
                        pool.dma_start(biasS[r, p, 0:128],
                                       bass.AP(rel_d.tensor, 127, [[384, HA], [-1, NQ], [1, 128]])).then_inc(s["rel_st"], 16)
                        b = 2 * p + e
                        pool.dma_start(biasS[r, p, 128 + NQ * b:128 + NQ * b + NQ],
                                       bass.AP(rel_d.tensor, 255, [[384, HA], [-1, NQ], [1, NQ]])).then_inc(s["rel_st"], 16)
            pool.wait_ge(s["s_gate"], 1)
            pool.dma_start(WLR[0:RANK], I["w_lr_even"][0]).then_inc(s["vld2"], 16)
            pool.dma_start(WLR[RANK:RANK + 1], I["b_lr_even"]).then_inc(s["vld2"], 16)
            with pool.Fori(0, HB) as h:
                wait_for(s["b_st"], h * 8 + 8)
                pool.dma_start(O[4][0, 0, ds(h, 1)].rearrange("h p e -> p (h e)"), ST[:, 7]).then_inc(s["b_pst"], 16)
                wait_for(s["b_pst"], h * 16 + 16)
                wait_for(s["b_o"], h * 2 + 2)
                pool.dma_start(ST, I["state_gla"][0][:, ds(h, 1)].rearrange("b h p e -> p (b h) e")).then_inc(s["b_sld"], 16)
                wait_for(s["b_sup"], h * 8 + 8)
                pool.dma_start(O[8][0][:, ds(h, 1)].rearrange("b h p e -> p (b h) e"), ST).then_inc(s["b_stf"], 16)
                wait_for(s["b_stf"], h * 16 + 16, "b_free")

            def out_product(w, src, dst):
                def load(m, j):
                    pool.dma_start(resb[:, j], src[ds(m * 2 + j, 1)].rearrange("k p t -> p (k t)")).then_inc(rld[j], 16)

                def store(m, j):
                    if w < 2:
                        wait_for(s["wy"], m * 2 + (16 * w + j + 1))
                        y = R3[:, ds(m * 2 + j, 1), :].rearrange("p k t -> p (k t)") if w == 0 else yst[:, j]
                        pool.dma_start(dst[ds(m * 2 + j, 1)].rearrange("k p t -> p (k t)"), y).then_inc(yst_s[j], 16)
                    else:
                        wait_for(s["wotp"], m * 4 + (2 * j + 2))
                        pool.dma_start(O[0][0].rearrange("(t p) n -> p t n", p=128)[:, :, ds(m * 256 + 128 * j, 128)],
                                       ost[:, j, 0:4]).then_inc(ost_s[j], 16)
                        pool.dma_start(O[1].rearrange("b t n -> (b t) n")[:, ds(m * 256 + 128 * j, 128)],
                                       ost[0:NS, j, 4]).then_inc(ost_s[j], 16)
                        wait_for(ost_s[j], m * 32 + 32, "ost_free")

                load(0, 0)
                load(0, 1)
                with pool.Fori(0, KT // 2 - 1) as m:
                    for j in range(2):
                        wait_for(s["wy"], m * 2 + (16 * w + j + 1))
                        load(m + 1, j)
                        store(m, j)
                for j in range(2):
                    store(KT // 2 - 1, j)

            pool.wait_ge(s["b_gate"], 2 * HB)
            pool.wait_ge(s["nl"], 2 * KT)
            pool.wait_ge(s["res_st"], 16)
            out_product(0, res_d[0], res_d[1])
            pool.wait_ge(s["nl"], 3 * KT)
            pool.wait_ge(s["nls"], 2)

            def load_table(h):
                pool.dma_start(RT, C["ret"][ds(h, 1)].rearrange("h p w -> p (h w)")).then_inc(s["c_tab"], 16)

            load_table(0)
            pool.dma_start(u(0, 2 * T), C["rope"].rearrange("p a t -> p (a t)")).then_inc(s["c_tab"], 16)
            with pool.Fori(0, HC) as h:
                def load_state(b):
                    pool.dma_start(SB[:, b % 4], I["state_ret"][0][b, ds(h, 1)].rearrange(
                        "h (k p) e -> p (h k) e", p=128)).then_inc(sld[b % 4], 16)

                def store_state(b):
                    wait_for(s["c_upv"], h * 16 + (2 * b + 2))
                    pool.dma_start(O[9][0][b, ds(h, 1)].rearrange("h (k p) e -> p (h k) e", p=128),
                                   SB[:, b % 4]).then_inc(sst[b % 4], 16)

                for b in range(4):
                    load_state(b)
                for kk in range(2):
                    wait_for(s["c_stv"], h * 2 + (kk + 1))
                    pool.dma_start(O[5][0, 0, ds(h, 1), 128 * kk:128 * kk + 128].rearrange("h p e -> p (h e)"),
                                   CST[:, kk]).then_inc(s["c_pst"], 16)
                for b in range(4, NB):
                    store_state(b - 4)
                    wait_for(sst[b - 4], h * 32 + 16)
                    load_state(b)
                for b in range(4, NB):
                    store_state(b)
                wait_for(s["c_pst"], h * 32 + 32, "c_pfree")
                load_table(h + 1)
                for e in range(4):
                    wait_for(s["c_gate"], h * 4 + (e + 1))
                    pool.dma_start(mix_d[ds(h * 4 + e, 1)].rearrange("k p t -> p (k t)"), R3[:, 12 + e]).then_inc(s["c_mst"], 16)
                wait_for(s["c_mst"], h * 64 + 64, "c_mfree")
                for b in range(4):
                    wait_for(sst[b], h * 32 + 32)

            def reload(w):
                for q in range(4):
                    pool.dma_start(R3[:, 4 * q:4 * q + 4],
                                   mix_d[KT * w + 4 * q:KT * w + 4 * q + 4].rearrange("k p t -> p k t")).then_inc(raw[q], 16)

            pool.wait_ge(s["c_mst"], 16 * 4 * HC)
            reload(0)
            out_product(1, res_d[1], res_d[2])
            reload(1)
            for j in range(2):
                pool.wait_ge(yst_s[j], 16 * 16)
            out_product(2, res_d[2], None)
            for j in range(2):
                pool.wait_ge(ost_s[j], 32 * 8)
            for b in range(4):
                pool.wait_ge(sst[b], 32 * HC)
            pool.wait_ge(s["b_pst"], 16 * HB)
            pool.wait_ge(s["b_stf"], 16 * HB)
            pool.wait_ge(s["swa_st"], 32)
            pool.wait_ge(s["kv_st"], 64)
            pool.wait_ge(s["c_pst"], 32 * HC)
            pool.wait_ge(s["c_tab"], 16 * HC + 32)
            pool.wait_ge(s["res_st"], 16)

        @block.scalar
        def _(act):
            link = Chain(act, s["a_chain"])
            A = nc.scalar.activation

            def wait_for(sm, value):
                act.wait_ge(sm, value)
                act.sem_inc(s["act_passed"], 1)

            def split_hi(n, par):
                if isinstance(n, int) and n >= N_END:
                    return
                act.wait_ge(wld[par], (n - par) * 8 + 16)
                if not (isinstance(n, int) and n < 2):
                    act.wait_ge(s["half"], n * 2 - 2)
                A(WH[:, par], slot[par], ACT.Copy).then_inc(s["hi"], 1)

            def evac(n, c, dst, rows=128):
                (act.wait_ge if isinstance(n, int) else wait_for)(s["half"], n * 2 + (c + 1))
                return A(dst, PJ[0:rows, c, 0:HALF], ACT.Copy).then_inc(s["ev"], 1)

            def halves(v):
                return v.rearrange("p (c t) -> p c t", c=2)

            def rsqrt_mean(dst, count, n):
                link(A(halves(dst), X[:, 0:2, 0:HALF], ACT.Ln, bias=eps[:, 0:1], scale=1.0 / n))
                return A(dst, dst, ACT.Exp, scale=-0.5)

            act.wait_ge(s["vec_sb"], 1)
            A(cexp, craw, ACT.Exp, scale=-1.0).then_inc(s["c_exp"], 1)
            for t in range(5):
                w = 128 if t < 4 else NS
                for q in (0, 2):
                    act.wait_ge(s["xT_ready"], 4 * t + q + 1)
                    A(R3[:, 4 * q:4 * q + 4, t * 128:t * 128 + w], X[:, q, 0:4 * w].rearrange("p (a b) -> p a b", a=4),
                      ACT.Copy).then_inc(s["xa"], 1)
            act.wait_ge(s["xa"], 10)
            act.wait_ge(s["xd"], 10)
            for k in range(KT):
                if k >= 2:
                    act.wait_ge(s["sqd"], k)
                A(sq[:, k % 2], R3[:, k], ACT.Square).then_inc(s["xa"], 1)

            def norm(l):
                act.wait_ge(s["ms"], l + 1)
                rsqrt_mean(rstd, 0, D).then_inc(s["rb"], 1)
                for k in range(KT):
                    act.wait_ge(s["tset"], KT * l + k + 1)
                    A(AH[:, k, 0:SEQ], tk[:, k % 2], ACT.Identity, bias=mod[l][:, k, 0:1]).then_inc(s["hi_t"], 1)
                    if k == 0:
                        act.wait_ge(s["sset"], l + 1)
                        A(AH[:, :, SEQ:T], hs, ACT.Copy).then_inc(s["hi_t"], 1)

            split_hi(0, 0)
            norm(0)
            split_hi(1, 1)
            for c in range(2):
                evac(0, c, QT[:, c * HALF:(c + 1) * HALF])
            split_hi(2, 0)
            act.wait_ge(s["ev"], 2)
            A(E, QT, ACT.Square).then_inc(s["kv_rb"], 1)
            for c in range(2):
                evac(1, c, QN[:, c * HALF:(c + 1) * HALF])
            split_hi(3, 1)
            act.wait_ge(s["kv_ms"], 1)
            rsqrt_mean(E, 0, 64).then_inc(s["kv_rb"], 1)
            act.wait_ge(s["kn_ready"], 2)
            for kv in range(2):
                for e in range(2):
                    A(kdup[kv][64 * e:64 * e + 64], kn[64 * kv:64 * kv + 64], ACT.Copy).then_inc(s["kdup_ready"], 1)
            act.wait_ge(s["kct_ps"], 2)
            A(KCT, X[:, 0:2, :].rearrange("p a (b c) -> p (a b) c", c=128), ACT.Copy).then_inc(s["kct_sb"], 1)
            for c in range(2):
                act.wait_ge(s["half"], 5 + c)
                A(LR[0:RANK, c * HALF:(c + 1) * HALF], PJ[0:RANK, c, 0:HALF], ACT.Copy).then_inc(s["ev"], 1)

            def pair_of_heads(i, kv, i0):
                n = i * 2 + N_A
                split_hi(n + 1, 0)
                for c in range(2):
                    evac(n, c, QT[:, c * HALF:(c + 1) * HALF])
                act.wait_ge(s["ev"], n * 2 + 2)
                act.wait_ge(s["a_gate"], i * 1 + 1)
                A(E, QT, ACT.Square).then_inc(s["a_rb"], 1)
                split_hi(n + 2, 1)
                act.wait_ge(s["a_ms"], i * 1 + 1)
                rsqrt_mean(E, 0, 64).then_inc(s["a_rb"], 1)
                wait_for(s["a_qn"], i * 1 + 1)
                for e in range(2):
                    A(qsT[64 * kv:64 * kv + 64, :, ds(i * 2 + (e - 2 * i0), 1), :].rearrange("p b g t -> p b (g t)"),
                      QN[64 * e:64 * e + 64, SEQ:T].rearrange("p (b t) -> p b t", t=NQ), ACT.Copy).then_inc(s["a_qs"], 1)
                for e in range(2):
                    act.wait_ge(s["a_mxd"], i * 2 + (e + 1))
                    for b in range(4):
                        A(S[:, b], S[:, b], ACT.Exp, bias=nm[:, b:b + 1], accum_out=den[:, b:b + 1]).then_inc(s["a_exp"], 1)
                    A(es, nm, ACT.Exp, bias=sk2[:, e:e + 1]).then_inc(s["a_exp"], 1)
                    act.wait_ge(s["a_tp"], i * 2 + (e + 1))
                    A(PT[:, 2:4].rearrange("p b h q -> p (b h q)"), X[:, 3, :], ACT.Copy).then_inc(s["a_ptA"], 1)
                for c in range(2):
                    evac(n + 1, c, R3[:, ds(i, 1), c * HALF:(c + 1) * HALF].rearrange("p a t -> p (a t)"))
                wait_for(s["ev"], n * 2 + 4)
                A(E, R3[:, ds(i, 1), :].rearrange("p a t -> p (a t)"), ACT.Exp, scale=-1.0).then_inc(s["a_eg"], 1)

            act.wait_ge(s["kv_st"], 64)
            for kv in range(2):
                with act.Fori(4 * kv, 4 * kv + 4) as i:
                    link.loop(i - 4 * kv, 1)
                    pair_of_heads(i, kv, 4 * kv)
                    link.end(4)
            act.wait_ge(s["s_mx"], 1)
            for p in range(4):
                A(SS[:, p], SS[:, p], ACT.Exp, bias=nm[:, p:p + 1], accum_out=den[:, p:p + 1]).then_inc(s["s_exp"], 1)
            A(es, nm, ACT.Exp, bias=skrow).then_inc(s["s_exp"], 1)
            act.wait_ge(s["s_tp"], 2)
            A(PTs.rearrange("p a b -> p (a b)"), X[:, 2, :], ACT.Copy).then_inc(s["s_pt"], 1)
            A(PTn[0:NS].rearrange("p a b -> p (a b)"), X[0:NS, 3, :], ACT.Copy).then_inc(s["s_pt"], 1)
            act.wait_ge(s["s_pv"], 1)
            for kv in range(2):
                for e in range(2):
                    for b in range(NB):
                        A(OSm[64 * e:64 * e + 64, 4 * kv:4 * kv + 4, NQ * b:NQ * b + NQ],
                          X[64 * kv:64 * kv + 64, 4, 32 * b:32 * b + 32].rearrange("p (g u t) -> p g u t", u=2, t=NQ)[:, :, e],
                          ACT.Copy).then_inc(s["s_os"], 1)

            with act.Fori(0, HB) as h:
                link.loop(h, 5)
                n = h * 6 + N_B
                act.wait_ge(s["b_z"], h * 2 + 2)
                link(A(T1[:, 0:SEQ], X[:, 0, :], ACT.Abs))
                link(A(T2[0:NS, 0:128], X[0:NS, 1, 0:128], ACT.Abs))
                link(A(T1[:, 0:SEQ], T1[:, 0:SEQ], ACT.Exp, scale=-1.0))
                link(A(T2[0:NS, 0:128], T2[0:NS, 0:128], ACT.Exp, scale=-1.0))
                A(T1[:, 0:SEQ], T1[:, 0:SEQ], ACT.Ln, bias=1.0).then_inc(s["b_ln"], 1)
                A(T2[0:NS, 0:128], T2[0:NS, 0:128], ACT.Ln, bias=1.0).then_inc(s["b_ln"], 1)
                split_hi(n + 1, 0)
                act.wait_ge(s["b_bc"], h * 1 + 1)
                A(EBP[:, 0:SEQ], X[:, 2, :], ACT.Exp, scale=1.0 / 16).then_inc(s["b_eb"], 1)
                A(EBP[:, SEQ:T], X[:, 3, 0:NS], ACT.Exp, scale=1.0 / 16).then_inc(s["b_eb"], 1)
                A(T2[:, 0:SEQ], X[:, 2, :], ACT.Exp, scale=-1.0 / 16).then_inc(s["b_eb"], 1)
                A(T2[:, SEQ:T], X[:, 3, 0:NS], ACT.Exp, scale=-1.0 / 16).then_inc(s["b_eb"], 1)
                act.wait_ge(s["b_dif"], h * 1 + 1)
                A(T1, T1, ACT.Exp, scale=1.0 / 16).then_inc(s["b_kdx"], 1)
                for j in range(4):
                    for c in range(2):
                        evac(n + j, c, BP[:, j, c * HALF:(c + 1) * HALF])
                    split_hi(n + j + 2, (j + 1) % 2)
                    if j == 2:
                        act.wait_ge(s["b_kt"], h * 1 + 1)
                        A(KDT.rearrange("p a b -> p (a b)"), X[:, 2, :], ACT.Copy).then_inc(s["b_kta"], 1)
                        A(KDTs[0:NS], X[0:NS, 3, 0:128], ACT.Copy).then_inc(s["b_kta"], 1)
                act.wait_ge(s["b_vt"], h * 1 + 1)
                A(VTB.rearrange("p (x a) e -> p x (a e)", x=2), X[:, 0:2, :], ACT.Copy).then_inc(s["b_vta"], 1)
                A(VTBs[0:NS], X[0:NS, 2, 0:256], ACT.Copy).then_inc(s["b_vta"], 1)
                for j in range(4, 6):
                    for c in range(2):
                        evac(n + j, c, R3[:, ds(h * 2 + (4 + j), 1), c * HALF:(c + 1) * HALF].rearrange("p a t -> p (a t)"))
                    if j < 5:
                        split_hi(n + j + 2, (j + 1) % 2)
                act.wait_ge(s["b_o"], h * 2 + 2)
                A(BP[:, 2:4, 0:SEQ], X[:, 0:2, :], ACT.Copy).then_inc(s["b_oe"], 1)
                act.wait_ge(s["b_so"], h * 1 + 1)
                A(BP[:, 2:4, SEQ:T], X[:, 4, 0:2 * NS].rearrange("p (e t) -> p e t", e=2), ACT.Copy).then_inc(s["b_oe"], 1)
                act.wait_ge(s["b_oe"], h * 2 + 2)
                A(T1, BP[:, 2], ACT.Square).then_inc(s["b_rb"], 1)
                A(sq1, BP[:, 3], ACT.Square).then_inc(s["b_rb"], 1)
                act.wait_ge(s["b_ms"], h * 1 + 1)
                rsqrt_mean(T1, 0, 256).then_inc(s["b_rb"], 1)
                wait_for(s["ev"], n * 2 + 12)
                for e in range(2):
                    if e == 1:
                        wait_for(s["b_gate"], h * 2 + 1)
                    A(sq1, R3[:, ds(h * 2 + (8 + e), 1), :].rearrange("p a t -> p (a t)"), ACT.Exp, scale=-1.0).then_inc(s["b_eg"], 1)
                link.end(HB)

            def out_product(w, base):
                def tiles(m, last=False):
                    for j in range(2):
                        if not (last and j == 1):
                            split_hi(m * 2 + (base + j + 1), (base + j + 1) % 2)
                        if w == 0:
                            wait_for(s["wy"], m * 2 + (j + 1))
                            A(wsq, R3[:, ds(m * 2 + j, 1), :].rearrange("p a t -> p (a t)"), ACT.Square).then_inc(s["wsqa"], 1)
                            act.wait_ge(s["wssq"], m * 2 + (j + 1))
                        if w == 2:
                            act.wait_ge(s["wtp"], m * 2 + (j + 3))
                            act.wait_ge(s["ost_free"], m * 2 + (j + 1))
                            A(ost[:, j, 0:4].rearrange("p a b -> p (a b)"), X[:, j, :], ACT.Copy).then_inc(s["wotp"], 1)
                            A(ost[0:NS, j, 4], X[0:NS, 2 + j, 0:128], ACT.Copy).then_inc(s["wotp"], 1)

                with act.Fori(0, KT // 2 - 1) as m:
                    tiles(m)
                tiles(KT // 2 - 1, last=(w == 2))

            def split_mixed(w):
                for k in range(KT):
                    if w > 0:
                        act.wait_ge(raw[k // 4], 16 * w)
                    if w == 2:
                        act.wait_ge(s["half"], 2 * (N_WA + KT))
                    if w == 0:
                        act.wait_ge(s["b_gate"], 2 * HB)
                        act.wait_ge(s["s_gate"], 1)
                    A(AH[:, k], R3[:, k], ACT.Copy).then_inc(s["m_hi"], 1)

            split_mixed(0)
            out_product(0, N_W0)
            norm(1)
            with act.Fori(0, HC) as h:
                n = h * 12 + N_C
                for j in range(12):
                    split_hi(n + (j + 1), (N_C + j + 1) % 2)
                    if j == 6:
                        act.wait_ge(s["c_tab"], h * 16 + 32)
                        act.wait_ge(s["c_kt"], h * 1 + 1)
                        for t in range(4):
                            A(KTK[:, t], X[:, 3 + t // 2, (t % 2) * 256:(t % 2) * 256 + 256], ACT.Copy,
                              scale=RT[:, T + NS + NB + t:T + NS + NB + t + 1]).then_inc(s["c_kta"], 1)
                        A(KTKs[0:NS], AD[0:NS, 0:256], ACT.Copy).then_inc(s["c_kta"], 1)
                    if j == 8:
                        act.wait_ge(s["c_vt"], h * 1 + 1)
                        A(CT[:, 0:2], X[:, 0:2, :], ACT.Copy).then_inc(s["c_vta"], 1)
                        A(CTs[0:NS], X[0:NS, 4, :], ACT.Copy).then_inc(s["c_vta"], 1)
                    if j in (9, 10):
                        act.wait_ge(s["c_o"], h * 2 + (j - 8))
                        act.wait_ge(s["c_mfree"], h * 1 + 1)
                        A(R3[:, 12 + 2 * (j - 9):14 + 2 * (j - 9), 0:SEQ], X[:, 2:4, :], ACT.Copy).then_inc(s["c_oe"], 1)
                    for c in range(2):
                        evac(n + j, c, R3[:, j, c * HALF:(c + 1) * HALF])
                act.wait_ge(s["c_os"], h * 1 + 1)
                A(R3[:, 12:16, SEQ:T], X[:, 4, 0:4 * NS].rearrange("p (e t) -> p e t", e=4), ACT.Copy).then_inc(s["c_oe"], 1)
                act.wait_ge(s["c_oe"], h * 3 + 3)
                for e in range(4):
                    if e >= 2:
                        act.wait_ge(s["c_ssq"], h * 4 + (e - 1))
                    A((r1, r2)[e % 2], R3[:, 12 + e], ACT.Square).then_inc(s["c_rb"], 1)
                act.wait_ge(s["c_ms"], h * 1 + 1)
                A(halves(r1), X[:, 2:4, 0:HALF], ACT.Ln, bias=eps[:, 0:1], scale=1.0 / 512).then_inc(s["c_rb"], 1)
                act.wait_ge(s["c_rb"], h * 6 + 5)
                A(r1, r1, ACT.Exp, scale=-0.5).then_inc(s["c_rb"], 1)
                act.wait_ge(s["ev"], n * 2 + 24)
                for e in range(4):
                    if e >= 1:
                        act.wait_ge(s["c_gate"], h * 4 + e)
                    A(r2, R3[:, 8 + e], ACT.Exp, scale=-1.0).then_inc(s["c_eg"], 1)
            split_mixed(1)
            out_product(1, N_WA)
            split_mixed(2)
            out_product(2, N_WB)

        @block.vector
        def _(dve):
            link = Chain(dve, s["v_chain"])
            V = nc.vector
            TT, TS, STT = V.tensor_tensor, V.tensor_scalar, V.scalar_tensor_tensor

            def split_lo(n, par):
                dve.wait_ge(s["hi"], n + 1)
                TT(WL[:, par], slot[par], WH[:, par].bitcast(F32), ALU.subtract).then_inc(s["lo"], 1)

            link(V.memset(eps[:, :], EPS))
            V.memset(ssum, 0.0).then_inc(s["sqd"], 1)
            dve.wait_ge(s["vec_ps"], 3)
            link(V.tensor_copy(vecT[:, :], X[:, 0, 0:128]))
            link(V.tensor_copy(vecT2[:, :], X[:, 0, 128:152]))
            link(V.tensor_copy(craw[:, :, 0], X[:, 0, 128:144]))
            V.tensor_copy(craw[:, :, 1:9], X[:, 0, 256:384].rearrange("p (b k) -> p k b", b=NB)).then_inc(s["vec_sb"], 1)
            dve.wait_ge(s["c_exp"], 1)
            link(V.tensor_scalar_add(cexp, cexp, 1.0))
            link(V.reciprocal(cexp, cexp))
            TT(cs[:, :, :], craw, cexp, ALU.mult).then_inc(s["vec_sb"], 1)
            for t in range(5):
                w = 128 if t < 4 else NS
                for q in (1, 3):
                    dve.wait_ge(s["xT_ready"], 4 * t + q + 1)
                    V.tensor_copy(R3[:, 4 * q:4 * q + 4, t * 128:t * 128 + w],
                                  X[:, q, 0:4 * w].rearrange("p (a b) -> p a b", a=4)).then_inc(s["xd"], 1)
            for k in range(KT):
                dve.wait_ge(s["xa"], k + 11)
                dve.wait_ge(s["sqd"], k + 1)
                TT(ssum, ssum, sq[:, k % 2], ALU.add).then_inc(s["sqd"], 1)

            with dve.Fori(0, 8) as i:
                for sl in range(2):
                    dve.wait_ge(s["ad_done"], i * 2 + (sl + 1))
                    src = (AD[:, 0:32] if sl == 0 else X[:, 4, 0:32]).rearrange("p (a b) -> p a b", b=16)[:, :, 0:9]
                    TT(mod[0][:, ds(i * 4 + 2 * sl, 2), :], src,
                       vecT[:, ds(i * 4 + 2 * sl, 2)].unsqueeze(2).to_broadcast([128, 2, 9]), ALU.add).then_inc(s["ad_ev"], 1)

            def norm(l):
                if l == 0:
                    dve.wait_ge(s["ad_ev"], 16)
                else:
                    dve.wait_ge(s["ad_ev"], 48)
                link(V.tensor_scalar_add(G[:, :, :], mod[l][:, KT:2 * KT, :], 1.0))
                link(TT(G[:, :, :], G[:, :, :], vecT[:, 96 + 16 * l:112 + 16 * l].unsqueeze(2).to_broadcast([128, KT, 9]), ALU.mult))
                dve.wait_ge(s["rb"], l + 1)

                def low(k):
                    dve.wait_ge(s["hi_t"], 17 * l + k + 1 + (k > 0))
                    STT(AL[:, k, 0:SEQ], tk[:, k % 2], mod[l][:, k, 0:1], AH[:, k, 0:SEQ].bitcast(F32),
                        ALU.add, ALU.subtract).then_inc(s["nl"], 1)

                for k in range(KT):
                    if k >= 2:
                        dve.wait_ge(s["nl"], 2 * KT * l + k - 1)
                    STT(tk[:, k % 2], R3[:, k, 0:SEQ], G[:, k, 0:1], rstd[:, 0:SEQ], ALU.mult, ALU.mult).then_inc(s["tset"], 1)
                    if k == 0:
                        link(TT(ts, R3[:, :, SEQ:T], rstd[:, SEQ:T].unsqueeze(1).to_broadcast([128, KT, NS]), ALU.mult))
                        t4 = ts.rearrange("p k (b t) -> p k b t", t=NQ)
                        h4 = hs.rearrange("p k (b t) -> p k b t", t=NQ)
                        link(TT(t4, t4, G[:, :, 1:9].unsqueeze(3).to_broadcast([128, KT, NB, NQ]), ALU.mult))
                        TT(h4, t4, mod[l][:, 0:KT, 1:9].unsqueeze(3).to_broadcast([128, KT, NB, NQ]), ALU.add).then_inc(s["sset"], 1)
                        dve.wait_ge(s["hi_t"], 17 * l + 2)
                        TT(AL[:, :, SEQ:T], hs, AH[:, :, SEQ:T].bitcast(F32), ALU.subtract).then_inc(s["nls"], 1)
                    if k > 0:
                        low(k - 1)
                low(KT - 1)

            norm(0)
            split_lo(0, 0)
            split_lo(1, 1)
            link(V.memset(relb[32:33], 1.0))
            V.memset(LR[0:32], 1.0).then_inc(s["kn_ready"], 1)
            split_lo(2, 0)
            link(TS(qg8, vecT2[:, 22:23], 0.125, None, ALU.mult))
            dve.wait_ge(s["kv_ms"], 2)
            V.tensor_copy(relS[0:HA], X[0:HA, 2, 0:384]).then_inc(s["rel_sb"], 1)
            dve.wait_ge(s["kv_rb"], 2)
            STT(kn, QT, vecT2[:, 23:24], E, ALU.mult, ALU.mult).then_inc(s["kn_ready"], 1)
            dve.wait_ge(s["kv_ps"], 1)
            link(V.tensor_copy(vtok.rearrange("p a b -> p (a b)"), X[:, 3, :]))
            V.tensor_copy(vtok_s[0:NS], X[0:NS, 4, 0:128]).then_inc(s["kv_out_sb"], 1)
            dve.wait_ge(s["kv_ps"], 2)
            link(V.tensor_copy(E[:, 0:128], X[:, 2, 0:128]))
            V.tensor_copy(E[0:NS, 128:256], X[0:NS, 2, 128:256]).then_inc(s["kv_out_sb"], 1)
            split_lo(3, 1)
            dve.wait_ge(s["kdup_ready"], 4)
            dve.wait_ge(s["kv_ps"], 2)
            link(V.memset(S[:, 0, 0:128], NEG))
            dve.sem_inc(s["a_gate"], 1)
            dve.wait_ge(s["kv_st"], 64)

            def ada_sum(unit, dst, bias):
                dve.wait_ge(s["ad_done"], unit)
                TT(dst, AD[:, 0:32].rearrange("p (a b) -> p a b", b=16)[:, :, 0:9],
                   vecT[:, bias].unsqueeze(2).to_broadcast([128, 2, 9]), ALU.add).then_inc(s["ad_ev"], 1)

            def pair_of_heads(i, kv):
                n = i * 2 + N_A
                split_lo(n + 1, 0)
                ada_sum(i * 1 + 17, mod[0][:, ds(i * 2 + 32, 2), :], ds(i * 2 + 32, 2))
                dve.wait_ge(s["a_rb"], i * 2 + 2)
                STT(QN, QT, qg8, E, ALU.mult, ALU.mult).then_inc(s["a_qn"], 1)
                link(V.tensor_copy(sk2, sk[:, ds(i * 2, 2)]))
                split_lo(n + 2, 1)
                dve.wait_ge(s["bias_ld"], i * 16 + 16)
                for e in range(2):
                    dve.wait_ge(s["a_sc"], i * 2 + (e + 1))
                    link(TT(S[:, 0, 128:256], X[:, 0, 128:256], biasT[:, e, 128:256], ALU.add))
                    link(TT(S[:, 1], X[:, 0, 256:512], biasT[:, e], ALU.add))
                    TT(S[:, 2:4], X[:, 1, :].rearrange("p (a b) -> p a b", a=2),
                       biasT[:, e].unsqueeze(1).to_broadcast([128, 2, 256]), ALU.add).then_inc(s["a_sadd"], 1)
                    dve.wait_ge(s["a_sadd"], i * 2 + (e + 1))
                    link(V.tensor_reduce(mx, S, AX, ALU.max))
                    TS(nm, mx, sk2[:, e:e + 1], -1.0, ALU.max, ALU.mult).then_inc(s["a_mxd"], 1)
                    dve.wait_ge(s["a_exp"], i * 10 + (5 * e + 5))
                    link(TT(rec, den, es, ALU.add))
                    link(V.reciprocal(rec, rec))
                    TT(S, S, rec.unsqueeze(2).to_broadcast([128, 4, 256]), ALU.mult).then_inc(s["a_p"], 1)
                    dve.wait_ge(s["a_tp"], i * 2 + (e + 1))
                    V.tensor_copy(PT[:, 0:2].rearrange("p b h q -> p (b h q)")[:, 128:512], X[:, 2, 128:512]).then_inc(s["a_ptV"], 1)
                    if e == 0:
                        link(V.memset(S[:, 0, 0:128], NEG))
                dve.wait_ge(s["a_eg"], i * 1 + 1)
                g = R3[:, ds(i, 1), :].rearrange("p a t -> p (a t)")
                link(V.tensor_scalar_add(E, E, 1.0))
                link(V.reciprocal(E, E))
                link(TT(g, g, E, ALU.mult))
                dve.wait_ge(s["a_pv"], i * 2 + 2)
                TT(g[:, 0:SEQ], g[:, 0:SEQ], X[:, 4, :], ALU.mult).then_inc(s["a_gate"], 1)
                link(V.memset(S[:, 0, 0:128], NEG))

            for kv in range(2):
                with dve.Fori(4 * kv, 4 * kv + 4) as i:
                    link.loop(i - 4 * kv, 16)
                    pair_of_heads(i, kv)
                    link.end(4)
            dve.wait_ge(s["a_qn"], 8)
            dve.wait_ge(s["a_qs"], 16)
            V.memset(biasS, NEG).then_inc(s["bs_ld"], 1)
            dve.wait_ge(s["rel_st"], 16 * 18)
            dve.wait_ge(s["s_sc"], 1)
            dve.wait_ge(s["bs_ld"], 1)
            link(TT(SS.rearrange("p (x a) b -> p x (a b)", x=2), X[:, 0:2, 0:320],
                    biasS.rearrange("p (x a) b -> p x (a b)", x=2), ALU.add))
            link(V.tensor_reduce(mx, SS, AX, ALU.max))
            TS(nm, mx, skrow, -1.0, ALU.max, ALU.mult).then_inc(s["s_mx"], 1)
            dve.wait_ge(s["s_exp"], 5)
            link(TT(rec, den, es, ALU.add))
            link(V.reciprocal(rec, rec))
            TT(SS, SS, rec.unsqueeze(2).to_broadcast([128, 4, 160]), ALU.mult).then_inc(s["s_p"], 1)
            dve.wait_ge(s["s_os"], 4 * NB)
            TT(R3[:, 0:8, SEQ:T], R3[:, 0:8, SEQ:T], OSm, ALU.mult).then_inc(s["s_gate"], 1)

            dve.wait_ge(s["vld2"], 16 * 12)
            with dve.Fori(0, HB) as h:
                link.loop(h, 14)
                n = h * 6 + N_B
                V.tensor_copy(WLH[0:RANK + 1], WLR[0:RANK + 1, ds(h * 128, 128)]).then_inc(s["b_wl"], 1)
                split_lo(n + 1, 0)
                dve.wait_ge(s["b_ln"], h * 2 + 2)
                STT(LAt.rearrange("p a b -> p (a b)"), X[:, 0, :], 0.0, T1[:, 0:SEQ], ALU.min, ALU.subtract).then_inc(s["b_la"], 1)
                STT(LAs[0:NS], X[0:NS, 1, 0:128], 0.0, T2[0:NS, 0:128], ALU.min, ALU.subtract).then_inc(s["b_la"], 1)
                ada_sum(h * 6 + 25, mod[1][:, ds(h * 12, 2), :], ds(h * 12 + 48, 2))
                dve.wait_ge(s["b_bc"], h * 1 + 1)
                dve.wait_ge(s["b_eb"], h * 4 + 4)
                dve.wait_ge(s["b_la"], h * 2 + 2)
                bl = X[:, 2, :].rearrange("p (c t) -> p c t", t=64)
                bs = X[:, 3, 0:NS].rearrange("p (b t) -> p b t", t=NQ)
                link(V.tensor_copy(blast[:, 0:8], bl[:, :, 63]))
                link(V.tensor_copy(blast[:, 8:16], bs[:, :, NQ - 1]))
                link(TT(T1[:, 0:SEQ].rearrange("p (c t) -> p c t", t=64), blast[:, 0:8].unsqueeze(2).to_broadcast([128, 8, 64]),
                        bl, ALU.subtract))
                TT(T1[:, SEQ:T].rearrange("p (b t) -> p b t", t=NQ), blast[:, 8:16].unsqueeze(2).to_broadcast([128, NB, NQ]),
                   bs, ALU.subtract).then_inc(s["b_dif"], 1)
                link(V.tensor_copy(ebl[:, 0:8], EBP[:, 0:SEQ].rearrange("p (c t) -> p c t", t=64)[:, :, 63]))
                link(V.tensor_copy(ebl[:, 8:16], EBP[:, SEQ:T].rearrange("p (b t) -> p b t", t=NQ)[:, :, NQ - 1]))
                dve.wait_ge(s["ev"], n * 2 + 2)
                split_lo(n + 2, 1)
                STT(BP[:, 0], BP[:, 0], 128.0 ** -0.5, EBP, ALU.mult, ALU.mult).then_inc(s["b_qk"], 1)
                dve.wait_ge(s["ev"], n * 2 + 4)
                dve.wait_ge(s["b_kdx"], h * 1 + 1)
                TT(T1, T1, BP[:, 1], ALU.mult).then_inc(s["b_kd"], 1)
                dve.wait_ge(s["b_kd"], h * 1 + 1)
                TT(BP[:, 1], BP[:, 1], T2, ALU.mult).then_inc(s["b_qk"], 1)
                split_lo(n + 3, 0)
                ada_sum(h * 6 + 26, mod[1][:, ds(h * 12 + 2, 2), :], ds(h * 12 + 50, 2))
                split_lo(n + 4, 1)
                ada_sum(h * 6 + 27, mod[1][:, ds(h * 12 + 4, 2), :], ds(h * 12 + 52, 2))
                dve.wait_ge(s["b_at"], h * 1 + 1)
                link(TT(AT, X[:, 0, :].rearrange("p (a b) -> p a b", a=4), gmask.unsqueeze(1).to_broadcast([128, 4, 128]), ALU.mult))
                TT(ATs[0:NS], X[0:NS, 1, 0:NS], smask[0:NS, 0:NS], ALU.mult).then_inc(s["b_atm"], 1)
                split_lo(n + 5, 0)
                ada_sum(h * 6 + 28, mod[1][:, ds(h * 12 + 6, 2), :], ds(h * 12 + 54, 2))
                split_lo(n + 6, 1)
                ada_sum(h * 6 + 29, mod[1][:, ds(h * 12 + 8, 2), :], ds(h * 12 + 56, 2))
                for c in range(8):
                    dS = X[:, (c % 2) * 2 + c // 4, (c // 2 % 2) * 256:(c // 2 % 2) * 256 + 256]
                    if c == 0:
                        dve.wait_ge(s["b_dS"], h * 1 + 1)
                        dve.wait_ge(s["b_free"], h * 1 + 1)
                        V.tensor_copy(ST[:, 0], dS).then_inc(s["b_st"], 1)
                    else:
                        dve.wait_ge(s["b_st"], h * 8 + c)
                        STT(ST[:, c], ST[:, c - 1], ebl[:, c:c + 1], dS, ALU.mult, ALU.add).then_inc(s["b_st"], 1)
                ada_sum(h * 6 + 30, mod[1][:, ds(h * 12 + 10, 2), :], ds(h * 12 + 58, 2))
                dve.wait_ge(s["b_kta"], h * 2 + 2)
                for b in range(NB):
                    if b >= 2:
                        dve.wait_ge(s["b_ssb"], h * 8 + (b - 1))
                    TS(kdm[0:NS, b % 2], KDTs[0:NS], bmask[0:NS, b:b + 1], None, ALU.mult).then_inc(s["b_kdm"], 1)
                    dve.wait_ge(s["b_ssb"], h * 8 + (b + 1))
                    STT(ST[:, b], ST[:, b], ebl[:, 8 + b:9 + b], X[:, 2 + b % 2, 0:256], ALU.mult, ALU.add).then_inc(s["b_sup"], 1)
                dve.wait_ge(s["b_rb"], h * 3 + 2)
                TT(T1, T1, sq1, ALU.add).then_inc(s["b_sq1"], 1)
                dve.wait_ge(s["b_rb"], h * 3 + 3)
                for e in range(2):
                    g = R3[:, ds(h * 2 + (8 + e), 1), :].rearrange("p a t -> p (a t)")
                    dve.wait_ge(s["b_eg"], h * 2 + (e + 1))
                    link(V.tensor_scalar_add(sq1, sq1, 1.0))
                    link(V.reciprocal(sq1, sq1))
                    link(TT(g, g, sq1, ALU.mult))
                    link(STT(BP[:, 2 + e], BP[:, 2 + e], vecT2[:, 16 + e:17 + e], T1, ALU.mult, ALU.mult))
                    TT(g, g, BP[:, 2 + e], ALU.mult).then_inc(s["b_gate"], 1)
                link.end(HB)

            def split_mixed(w):
                for k in range(KT):
                    dve.wait_ge(s["m_hi"], KT * w + k + 1)
                    TT(AL[:, k], R3[:, k], AH[:, k].bitcast(F32), ALU.subtract).then_inc(s["nl"], 1)

            def out_product(w, base, l):
                if w == 0:
                    dve.wait_ge(s["b_free"], HB + 1)
                    link(V.memset(ssum, 0.0))
                if w == 2:
                    for j in range(2):
                        dve.wait_ge(yst_s[j], 256)
                def tiles(m, last=False):
                    for j in range(2):
                        n = m * 2 + (base + j)
                        if not (last and j == 1):
                            split_lo(n + 1, (base + j + 1) % 2)
                        dve.wait_ge(rld[j], m * 16 + (128 * w + 16))
                        y = R3[:, ds(m * 2 + j, 1), :].rearrange("p a t -> p (a t)") if w == 0 else yst[:, j]
                        gp = mod[l][:, ds(m * 2 + (32 + j), 1), 0:1].rearrange("p a b -> p (a b)")
                        gs = mod[l][:, ds(m * 2 + (32 + j), 1), 1:9].rearrange("p a b -> p (a b)")
                        link(V.tensor_copy(eps[:, 6:7], gp))
                        if w == 1:
                            dve.wait_ge(yst_s[j], m * 16 + 128)
                        if w == 2:
                            dve.wait_ge(s["wtp"], m * 2 + (j + 1))
                        dve.wait_ge(s["half"], n * 2 + 1)
                        STT(y[:, 0:HALF], PJ[:, 0, 0:HALF], eps[:, 6:7], resb[:, j, 0:HALF], ALU.mult, ALU.add).then_inc(s["ev"], 1)
                        dve.wait_ge(s["half"], n * 2 + 2)
                        link(STT(y[:, HALF:SEQ], PJ[:, 1, 0:SEQ - HALF], eps[:, 6:7], resb[:, j, HALF:SEQ], ALU.mult, ALU.add))
                        TT(smp.rearrange("p (b t) -> p b t", t=NQ), PJ[:, 1, SEQ - HALF:HALF].rearrange("p (b t) -> p b t", t=NQ),
                           gs.unsqueeze(2).to_broadcast([128, NB, NQ]), ALU.mult).then_inc(s["ev"], 1)
                        dve.wait_ge(s["ev"], n * 2 + 2)
                        TT(y[:, SEQ:T], smp, resb[:, j, SEQ:T], ALU.add).then_inc(s["wy"], 1)
                        if w == 0:
                            dve.wait_ge(s["wsqa"], m * 2 + (j + 1))
                            TT(ssum, ssum, wsq, ALU.add).then_inc(s["wssq"], 1)
                            dve.wait_ge(s["wssq"], m * 2 + (j + 1))

                with dve.Fori(0, KT // 2 - 1) as m:
                    link.loop(m, 4)
                    tiles(m)
                    link.end(KT // 2 - 1)
                tiles(KT // 2 - 1, last=(w == 2))

            split_mixed(0)
            out_product(0, N_W0, 0)
            norm(1)
            dve.wait_ge(s["c_tab"], 32)
            with dve.Fori(0, HC) as h:
                link.loop(h, 32)
                n = h * 12 + N_C
                split_lo(n + 1, (N_C + 1) % 2)
                split_lo(n + 2, N_C % 2)
                split_lo(n + 3, (N_C + 1) % 2)
                for x in range(2):
                    dve.wait_ge(s["ev"], n * 2 + (4 + 4 * x))
                    x1, x2 = R3[:, 2 * x], R3[:, 2 * x + 1]
                    if x == 1:
                        dve.wait_ge(s["c_rot"], h * 2 + 1)
                    link(TT(r3, x1, sin, ALU.mult))
                    link(TT(r2, x2, sin, ALU.mult))
                    link(TT(x1, x1, cos, ALU.mult))
                    link(TT(x1, x1, r2, ALU.subtract))
                    link(TT(x2, x2, cos, ALU.mult))
                    TT(x2, x2, r3, ALU.add).then_inc(s["c_rot"], 1)
                    if x == 0:
                        split_lo(n + 4, N_C % 2)
                split_lo(n + 5, (N_C + 1) % 2)
                split_lo(n + 6, N_C % 2)
                dve.wait_ge(s["c_tab"], h * 16 + 32)
                dve.wait_ge(s["c_rot"], h * 2 + 2)
                for kk in range(2):
                    link(TT(qi[:, kk], R3[:, kk, SEQ:T], RT[:, T:T + NS], ALU.mult))
                dve.wait_ge(s["c_sc"], h * 1 + 1)
                dve.wait_ge(s["c_kt"], h * 1 + 1)
                for t, src in enumerate((X[:, 0, 0:512], X[:, 1, 0:384], X[:, 2, 0:256], X[:, 1, 384:512])):
                    link(TT(RAT[:, RAOFF[t]:RAOFF[t] + SEQ - 128 * t], src, RT[:, 0:SEQ - 128 * t], ALU.mult))
                TT(RATs[0:NS], X[0:NS, 2, 256:256 + NS], RT[0:NS, SEQ:T], ALU.mult).then_inc(s["c_scv"], 1)
                split_lo(n + 7, (N_C + 1) % 2)
                split_lo(n + 8, N_C % 2)
                dve.wait_ge(s["c_vt"], h * 1 + 1)
                V.tensor_copy(CT[:, 2:4], X[:, 2:4, :]).then_inc(s["c_vtv"], 1)
                split_lo(n + 9, (N_C + 1) % 2)
                dve.wait_ge(s["c_pfree"], h * 1 + 1)
                for kk in range(2):
                    dve.wait_ge(s["c_st"], h * 2 + (kk + 1))
                    V.tensor_copy(CST[:, kk], X[:, kk, :]).then_inc(s["c_stv"], 1)
                split_lo(n + 10, N_C % 2)
                split_lo(n + 11, (N_C + 1) % 2)
                split_lo(n + 12, N_C % 2)
                for b in range(NB):
                    if b >= 2:
                        dve.wait_ge(s["c_up"], h * 16 + 2 * (b - 1))
                    TS(ckdm[0:NS, b % 2], KTKs[0:NS], RT[0:NS, T + NS + b:T + NS + b + 1], None, ALU.mult).then_inc(s["c_km"], 1)
                    for kk in range(2):
                        dve.wait_ge(s["c_up"], h * 16 + (2 * b + kk + 1))
                        STT(SB[:, b % 4, kk], SB[:, b % 4, kk], RT[:, T + NS + NB + 4:T + NS + NB + 5],
                            X[:, kk, :], ALU.mult, ALU.add).then_inc(s["c_upv"], 1)
                for e in range(4):
                    dve.wait_ge(s["c_rb"], h * 6 + (e + 1))
                    if e == 0:
                        V.tensor_copy(r3, r1).then_inc(s["c_ssq"], 1)
                    else:
                        dve.wait_ge(s["c_ssq"], h * 4 + e)
                        TT(r3, r3, (r1, r2)[e % 2], ALU.add).then_inc(s["c_ssq"], 1)
                dve.wait_ge(s["c_rb"], h * 6 + 6)
                for e in range(4):
                    g, o = R3[:, 8 + e], R3[:, 12 + e]
                    dve.wait_ge(s["c_eg"], h * 4 + (e + 1))
                    link(V.tensor_scalar_add(r2, r2, 1.0))
                    link(V.reciprocal(r2, r2))
                    link(TT(g, g, r2, ALU.mult))
                    link(STT(o, o, vecT2[:, 18 + e:19 + e], r1, ALU.mult, ALU.mult))
                    TT(o, o, g, ALU.mult).then_inc(s["c_gate"], 1)
                link.end(HC)
            split_mixed(1)
            out_product(1, N_WA, 1)
            split_mixed(2)
            out_product(2, N_WB, 1)

        @block.tensor
        def _(pe):
            mm = nc.tensor.matmul

            def tr(out, in_, rows=128):
                return nc.tensor.transpose(out, in_, ident[0:rows, 0:rows])

            def product(n, par, ready=None):
                for c in range(2):
                    product_half(n, par, c, ready)

            def product_half(n, par, c, ready=None):
                if c == 0:
                    pe.wait_ge(s["lo"], n + 1)
                if not (isinstance(n, int) and n == 0):
                    pe.wait_ge(s["ev"], n * 2 + (c - 1))
                for k in range(KT):
                    if ready is not None and c == 0:
                        pe.wait_ge(s["nl"], ready + k + 1)
                    for a, (w, x) in enumerate(((WH, AH), (WH, AL), (WL, AH))):
                        last = mm(PJ[:, c, 0:HALF], w[:, par, k], x[:, k, c * HALF:(c + 1) * HALF],
                                  start=(k == 0 and a == 0), stop=(k == KT - 1 and a == 2))
                last.then_inc(s["half"], 1)

            def sum_rows(lhs, src, banks=(0, 1)):
                for c in range(2):
                    last = mm(X[:, banks[c], 0:HALF], lhs, src[:, c * HALF:(c + 1) * HALF], start=True, stop=True)
                return last

            def ada_tile(w, at):
                for k in range(KT):
                    last = mm(at, w[:, k], cs[:, k, :], start=(k == 0), stop=(k == KT - 1))
                return last

            pe.wait_ge(s["vld"], 16 * 14)
            tr(X[:, 0, 0:128], vr).then_inc(s["vec_ps"], 1)
            tr(X[:, 0, 128:152], vr2[0:24], 24).then_inc(s["vec_ps"], 1)
            tr(X[:, 0, 256:384], vc).then_inc(s["vec_ps"], 1)
            pe.wait_ge(s["vec_sb"], 1)
            for t in range(5):
                w = 128 if t < 4 else NS
                pe.wait_ge(xld[t % 2], 16 * (t // 2 + 1))
                for q in range(4):
                    if t > 0:
                        pe.wait_ge(s["xa" if q % 2 == 0 else "xd"], 2 * (t - 1) + q // 2 + 1)
                    for a in range(4):
                        last = tr(X[:, q, a * w:(a + 1) * w], xs[0:w, t % 2, (4 * q + a) * 128:(4 * q + a + 1) * 128], w)
                    last.then_inc(s["xT_ready"], 1)
            pe.wait_ge(s["vec_sb"], 2)

            def ada_slab(i, sl):
                pe.wait_ge(adl[sl], i * 16 + 16)
                for e in range(2):
                    bank = AD[:, 16 * e:16 * e + 9] if sl == 0 else X[:, 4, 16 * e:16 * e + 9]
                    last = ada_tile(slab[sl][:, :, 128 * e:128 * e + 128], bank)
                last.then_inc(s["ad_done"], 1)

            ada_slab(0, 0)
            ada_slab(0, 1)
            with pe.Fori(1, 8) as i:
                for sl in range(2):
                    pe.wait_ge(s["ad_ev"], i * 2 + (sl - 1))
                    ada_slab(i, sl)
            pe.wait_ge(s["sqd"], KT + 1)
            pe.wait_ge(s["xa"], 10)
            pe.wait_ge(s["xd"], 10)
            sum_rows(ones[:, :], ssum).then_inc(s["ms"], 1)
            pe.wait_ge(s["nls"], 1)
            product(0, 0, ready=0)
            product(1, 1)
            pe.wait_ge(s["vld2"], 16 * 10)
            pe.wait_ge(s["kv_rb"], 1)
            sum_rows(blk64, E).then_inc(s["kv_ms"], 1)
            pe.wait_ge(s["kn_ready"], 1)
            mm(X[0:HA, 2, 0:384], relb[0:33], hot[0:33], start=True, stop=True).then_inc(s["kv_ms"], 1)
            pe.wait_ge(s["ev"], 4)
            for t in range(4):
                tr(X[:, 3, 128 * t:128 * t + 128], QN[:, 128 * t:128 * t + 128])
            tr(X[0:NS, 4, 0:128], QN[:, SEQ:T]).then_inc(s["kv_ps"], 1)
            product(2, 0)
            pe.wait_ge(s["kn_ready"], 2)
            pe.wait_ge(s["rel_sb"], 1)
            tr(X[:, 2, 0:128], kn[:, SEQ - 128:SEQ])
            tr(X[0:NS, 2, 128:256], kn[:, SEQ:T]).then_inc(s["kv_ps"], 1)
            pe.wait_ge(s["kv_rb"], 2)
            for b in range(NB):
                last = tr(X[:, b // 4, (b % 4) * 128:(b % 4) * 128 + 128], KC[:, b])
                if b % 4 == 3:
                    last.then_inc(s["kct_ps"], 1)
            pe.wait_ge(s["kdup_ready"], 4)
            pe.wait_ge(s["kv_out_sb"], 2)
            pe.wait_ge(s["kct_sb"], 1)

            def ada_pair(unit, loaded):
                pe.wait_ge(s["ad_ev"], unit)
                for e in range(2):
                    pe.wait_ge(adl[e], loaded)
                    last = ada_tile(slot[2 + e], AD[:, 16 * e:16 * e + 9])
                last.then_inc(s["ad_done"], 1)

            def pair_of_heads(i, kv):
                n = i * 2 + N_A
                product(n, 1)
                ada_pair(i * 1 + 16, i * 16 + 144)
                pe.wait_ge(s["a_rb"], i * 2 + 1)
                sum_rows(blk64, E).then_inc(s["a_ms"], 1)
                pe.wait_ge(s["a_qn"], i * 1 + 1)
                for e in range(2):
                    r = slice(64 * e, 64 * e + 64)
                    if e == 1:
                        pe.wait_ge(s["a_mxd"], i * 2 + 1)
                    for b in range(4):
                        bank = X[:, b // 2, (b % 2) * 256:(b % 2) * 256 + 256]
                        if b == 0:
                            last = mm(bank[:, 128:256], QN[r, 0:128], kdup[kv][r, 0:128], start=True, stop=True)
                        else:
                            last = mm(bank, QN[r, 128 * b:128 * b + 128], kdup[kv][r, 128 * b - 128:128 * b + 128],
                                      start=True, stop=True)
                    last.then_inc(s["a_sc"], 1)
                    product_half(n + 1, 0, e)
                    pe.wait_ge(s["a_p"], i * 2 + (e + 1))
                    for b in range(4):
                        for f in range(2):
                            if b == 0 and f == 0:
                                continue
                            last = tr(X[:, 2 + b // 2, (b % 2) * 256 + f * 128:(b % 2) * 256 + f * 128 + 128],
                                      S[:, b, f * 128:f * 128 + 128])
                    last.then_inc(s["a_tp"], 1)
                    pe.wait_ge(s["a_ptA"], i * 2 + (e + 1))
                    pe.wait_ge(s["a_ptV"], i * 2 + (e + 1))
                    if e == 0:
                        pe.wait_ge(s["a_gate"], i * 1 + 1)
                    for b in range(4):
                        out = X[r, 4, 128 * b:128 * b + 128]
                        if b > 0:
                            mm(out, vtok[:, b - 1, 64 * kv:64 * kv + 64], PT[:, b, 0], start=True, stop=False)
                        last = mm(out, vtok[:, b, 64 * kv:64 * kv + 64], PT[:, b, 1], start=(b == 0), stop=True)
                    last.then_inc(s["a_pv"], 1)

            for kv in range(2):
                with pe.Fori(4 * kv, 4 * kv + 4) as i:
                    pair_of_heads(i, kv)
            pe.wait_ge(s["a_gate"], 9)
            pe.wait_ge(s["a_qs"], 16)
            for p in range(4):
                for e in range(2):
                    for kv in range(2):
                        b = 2 * p + e
                        r = slice(64 * kv, 64 * kv + 64)
                        rows = slice(64 * e + 32 * kv, 64 * e + 32 * kv + 32)
                        q = qsT[r, b].rearrange("p g t -> p (g t)")
                        at = (p % 2) * 160
                        mm(X[rows, p // 2, at:at + 128], q, KCT[r, b], start=True, stop=True)
                        last = mm(X[rows, p // 2, at + 128:at + 160], q, kdup[kv][r, SEQ:T], start=True, stop=True)
            last.then_inc(s["s_sc"], 1)
            pe.wait_ge(s["s_p"], 1)
            for p in range(4):
                last = tr(X[:, 2, 128 * p:128 * p + 128], SS[:, p, 0:128])
            last.then_inc(s["s_tp"], 1)
            for p in range(4):
                last = tr(X[0:NS, 3, 128 * p:128 * p + 128], SS[:, p, 128:160])
            last.then_inc(s["s_tp"], 1)
            pe.wait_ge(s["s_pt"], 2)
            for b in range(NB):
                for kv in range(2):
                    cols = slice(64 * (b % 2) + 32 * kv, 64 * (b % 2) + 32 * kv + 32)
                    out = X[64 * kv:64 * kv + 64, 4, 32 * b:32 * b + 32]
                    mm(out, VCc[:, b, 64 * kv:64 * kv + 64], PTs[:, b // 2, cols], start=True, stop=False)
                    last = mm(out, vtok_s[0:NS, 64 * kv:64 * kv + 64], PTn[0:NS, b // 2, cols], start=False, stop=True)
            last.then_inc(s["s_pv"], 1)

            pe.wait_ge(s["s_gate"], 1)
            pe.wait_ge(s["vld2"], 16 * 12)
            pe.wait_ge(s["ev"], 6)
            with pe.Fori(0, HB) as h:
                n = h * 6 + N_B

                def ada(j):
                    ada_pair(h * 6 + (24 + j), h * 96 + (272 + 16 * j))

                pe.wait_ge(s["b_wl"], h * 1 + 1)
                for t in range(4):
                    last = mm(X[:, 0, 128 * t:128 * t + 128], LR[0:RANK + 1, 128 * t:128 * t + 128],
                              WLH[0:RANK + 1], start=True, stop=True)
                last.then_inc(s["b_z"], 1)
                mm(X[0:NS, 1, 0:128], LR[0:RANK + 1, SEQ:T], WLH[0:RANK + 1],
                   start=True, stop=True).then_inc(s["b_z"], 1)
                product(n, 1)
                ada(0)
                pe.wait_ge(s["b_la"], h * 2 + 2)
                for t in range(4):
                    mm(X[:, 2, 128 * t:128 * t + 128], LAt[:, t], gmask, start=True, stop=True)
                mm(X[:, 3, 0:NS], LAs[0:NS], smask[0:NS, 0:NS], start=True, stop=True).then_inc(s["b_bc"], 1)
                product(n + 1, 0)
                ada(1)
                product(n + 2, 1)
                ada(2)
                pe.wait_ge(s["b_qk"], h * 2 + 2)
                for t in range(4):
                    mm(X[:, 0, 128 * t:128 * t + 128], BP[:, 1, 128 * t:128 * t + 128], BP[:, 0, 128 * t:128 * t + 128],
                       start=True, stop=True)
                mm(X[0:NS, 1, 0:NS], BP[:, 1, SEQ:T], BP[:, 0, SEQ:T], start=True, stop=True).then_inc(s["b_at"], 1)
                pe.wait_ge(s["b_kd"], h * 1 + 1)
                for t in range(4):
                    tr(X[:, 2, 128 * t:128 * t + 128], T1[:, 128 * t:128 * t + 128])
                tr(X[0:NS, 3, 0:128], T1[:, SEQ:T]).then_inc(s["b_kt"], 1)
                product(n + 3, 0)
                ada(3)
                pe.wait_ge(s["ev"], n * 2 + 8)
                pe.wait_ge(s["b_atm"], h * 1 + 1)
                pe.wait_ge(s["b_kta"], h * 2 + 2)
                for t in range(4):
                    for e in range(2):
                        tr(X[:, t // 2, (t % 2) * 256 + 128 * e:(t % 2) * 256 + 128 * e + 128],
                           BP[:, 2 + e, 128 * t:128 * t + 128])
                tr(X[0:NS, 2, 0:128], BP[:, 2, SEQ:T])
                tr(X[0:NS, 2, 128:256], BP[:, 3, SEQ:T]).then_inc(s["b_vt"], 1)
                product(n + 4, 1)
                ada(4)
                pe.wait_ge(s["b_vta"], h * 2 + 2)
                for c in range(8):
                    r = slice(64 * (c % 2), 64 * (c % 2) + 64)
                    last = mm(X[:, (c % 2) * 2 + c // 4, (c // 2 % 2) * 256:(c // 2 % 2) * 256 + 256], KDT[r, c // 2], VTB[r, c // 2],
                              start=True, stop=True)
                last.then_inc(s["b_dS"], 1)
                product(n + 5, 0)
                ada(5)
                pe.wait_ge(s["b_st"], h * 8 + 8)
                for e in range(2):
                    ec = slice(128 * e, 128 * e + 128)
                    for t in range(4):
                        mm(X[:, e, 128 * t:128 * t + 128], VTB[:, t, ec], AT[:, t], start=True, stop=False)
                        for c in (2 * t, 2 * t + 1):
                            if c > 0:
                                last = mm(X[:, e, 64 * c:64 * c + 64], ST[:, c - 1, ec], BP[:, 0, 64 * c:64 * c + 64],
                                          start=False, stop=(c % 2 == 1))
                    last.then_inc(s["b_o"], 1)
                pe.wait_ge(s["b_sld"], h * 16 + 16)
                for e in range(2):
                    ec = slice(128 * e, 128 * e + 128)
                    mm(X[:, 4, NS * e:NS * e + NS], VTBs[0:NS, ec], ATs[0:NS], start=True, stop=False)
                    for b in range(NB):
                        last = mm(X[:, 4, NS * e + NQ * b:NS * e + NQ * b + NQ], ST[:, b, ec],
                                  BP[:, 0, SEQ + NQ * b:SEQ + NQ * b + NQ], start=False, stop=(b == NB - 1))
                last.then_inc(s["b_so"], 1)
                for b in range(NB):
                    pe.wait_ge(s["b_kdm"], h * 8 + (b + 1))
                    if b >= 2:
                        pe.wait_ge(s["b_sup"], h * 8 + (b - 1))
                    mm(X[:, 2 + b % 2, 0:256], kdm[0:NS, b % 2], VTBs[0:NS], start=True, stop=True).then_inc(s["b_ssb"], 1)
                pe.wait_ge(s["b_sq1"], h * 1 + 1)
                sum_rows(ones[:, :], T1).then_inc(s["b_ms"], 1)
                pe.wait_ge(s["b_gate"], h * 2 + 2)
                pe.wait_ge(s["b_sup"], h * 8 + 8)

            def transposed(r, j):
                pe.wait_ge(s["wy"], r + 33)
                if not (isinstance(r, int) and r == 0):
                    pe.wait_ge(s["wotp"], r * 2)
                for t in range(4):
                    tr(X[:, j, 128 * t:128 * t + 128], yst[:, j, 128 * t:128 * t + 128])
                tr(X[0:NS, 2 + j, 0:128], yst[:, j, SEQ:T]).then_inc(s["wtp"], 1)

            def out_product(w, base, ready):
                p0, p1 = base % 2, (base + 1) % 2
                product(base, p0, ready=ready)
                product(base + 1, p1)
                if w == 2:
                    transposed(0, 0)
                with pe.Fori(1, KT // 2) as m:
                    product(m * 2 + base, p0)
                    if w == 2:
                        transposed(m * 2 - 1, 1)
                    product(m * 2 + (base + 1), p1)
                    if w == 2:
                        transposed(m * 2, 0)
                if w == 2:
                    transposed(KT - 1, 1)

            out_product(0, N_W0, KT)
            pe.wait_ge(s["wssq"], KT)
            sum_rows(ones[:, :], ssum).then_inc(s["ms"], 1)
            pe.wait_ge(s["nls"], 2)
            pe.wait_ge(s["nl"], 3 * KT)
            with pe.Fori(0, HC) as h:
                n = h * 12 + N_C
                for j in range(6):
                    product(n + j, (N_C + j) % 2)
                pe.wait_ge(s["c_rot"], h * 2 + 2)
                for t, out in enumerate((X[:, 0, 0:512], X[:, 1, 0:384], X[:, 2, 0:256], X[:, 1, 384:512])):
                    for kk in range(2):
                        mm(out, R3[:, 2 + kk, 128 * t:128 * t + 128], R3[:, kk, 128 * t:SEQ], start=(kk == 0), stop=(kk == 1))
                for kk in range(2):
                    last = mm(X[0:NS, 2, 256:256 + NS], R3[:, 2 + kk, SEQ:T], R3[:, kk, SEQ:T], start=(kk == 0), stop=(kk == 1))
                last.then_inc(s["c_sc"], 1)
                for t in range(4):
                    for kk in range(2):
                        tr(X[:, 3 + t // 2, (t % 2) * 256 + 128 * kk:(t % 2) * 256 + 128 * kk + 128],
                           R3[:, 2 + kk, 128 * t:128 * t + 128])
                for kk in range(2):
                    last = tr(AD[0:NS, 128 * kk:128 * kk + 128], R3[:, 2 + kk, SEQ:T])
                last.then_inc(s["c_kt"], 1)
                product(n + 6, N_C % 2)
                product(n + 7, (N_C + 1) % 2)
                pe.wait_ge(s["ev"], n * 2 + 16)
                pe.wait_ge(s["c_scv"], h * 1 + 1)
                pe.wait_ge(s["c_kta"], h * 5 + 5)
                for t in range(4):
                    for e in range(4):
                        tr(X[:, t, 128 * e:128 * e + 128], R3[:, 4 + e, 128 * t:128 * t + 128])
                for e in range(4):
                    last = tr(X[0:NS, 4, 128 * e:128 * e + 128], R3[:, 4 + e, SEQ:T])
                last.then_inc(s["c_vt"], 1)
                product(n + 8, N_C % 2)
                pe.wait_ge(s["c_vta"], h * 2 + 2)
                pe.wait_ge(s["c_vtv"], h * 1 + 1)
                for kk in range(2):
                    for t in range(4):
                        last = mm(X[:, kk, :], KTK[:, t, 128 * kk:128 * kk + 128], CT[:, t], start=(t == 0), stop=(t == 3))
                    last.then_inc(s["c_st"], 1)

                def outputs(g):
                    for e in (2 * g, 2 * g + 1):
                        for t in range(4):
                            last = mm(X[:, 2 + e % 2, 128 * t:SEQ], CT[:, t, 128 * e:128 * e + 128],
                                      RAT[:, RAOFF[t]:RAOFF[t] + SEQ - 128 * t], start=(t == 0), stop=(t == 3))
                    last.then_inc(s["c_o"], 1)

                outputs(0)
                product(n + 9, (N_C + 1) % 2)
                pe.wait_ge(s["c_oe"], h * 3 + 1)
                outputs(1)
                product(n + 10, N_C % 2)
                product(n + 11, (N_C + 1) % 2)
                pe.wait_ge(s["c_stv"], h * 2 + 2)
                for e in range(4):
                    last = mm(X[:, 4, NS * e:NS * e + NS], CTs[0:NS, 128 * e:128 * e + 128], RATs[0:NS],
                              start=(e == 0), stop=False, skip_group_check=True)
                for b in range(NB):
                    pe.wait_ge(sld[b % 4], h * 32 + (16 * (b // 4) + 16))
                    for e in range(4):
                        for kk in range(2):
                            last = mm(X[:, 4, NS * e + NQ * b:NS * e + NQ * b + NQ], SB[:, b % 4, kk, 128 * e:128 * e + 128],
                                      qi[:, kk, NQ * b:NQ * b + NQ], start=False, stop=(b == NB - 1 and kk == 1 and e == 3),
                                      skip_group_check=True)
                    if b == NB - 1:
                        last.then_inc(s["c_os"], 1)
                    pe.wait_ge(s["c_km"], h * 8 + (b + 1))
                    for kk in range(2):
                        if b >= 1:
                            pe.wait_ge(s["c_upv"], h * 16 + (2 * b - 1 + kk))
                        mm(X[:, kk, :], ckdm[0:NS, b % 2, 128 * kk:128 * kk + 128], CTs[0:NS], start=True, stop=True)\
                            .then_inc(s["c_up"], 1)
                pe.wait_ge(s["c_oe"], h * 3 + 2)
                pe.wait_ge(s["c_ssq"], h * 4 + 4)
                sum_rows(ones[:, :], r3, banks=(2, 3)).then_inc(s["c_ms"], 1)
                pe.wait_ge(s["c_upv"], h * 16 + 16)
                pe.wait_ge(s["c_rb"], h * 6 + 5)
            out_product(1, N_WA, 3 * KT)
            pe.sem_inc(s["wtp"], 2)
            out_product(2, N_WB, 4 * KT)


_OUTS = [(1, SEQ, D), (NB, NQ, D), (1, 1, WIN, 2, 64), (1, 1, WIN, 2, 64), (1, 1, HB, 128, 256), (1, 1, HC, 256, 512),
         (1, NB, WIN, 2, 64), (1, NB, WIN, 2, 64), (1, NB, HB, 128, 256), (1, NB, HC, 256, 512)]


def kernel(**inputs):
    import concourse.bacc as _bacc
    from concourse.bass_utils import run_bass_kernel_spmd as _run

    nc = _bacc.Bacc("TRN2", target_bir_lowering=False, num_devices=1)
    arrays, ins, consts = {}, {}, {}
    for name in inputs:
        a = np.ascontiguousarray(inputs[name])
        arrays[f"in_{name}"] = a
        ins[name] = nc.dram_tensor(f"in_{name}", a.shape, mybir.dt.from_np(a.dtype), kind="ExternalInput").ap()
    for name, a in shape_constants().items():
        arrays[f"const_{name}"] = a
        consts[name] = nc.dram_tensor(f"const_{name}", a.shape, F32, kind="ExternalInput").ap()
    outs = [nc.dram_tensor(f"out_{i}", shape, F32, kind="ExternalOutput").ap() for i, shape in enumerate(_OUTS)]
    build(nc, ins, outs, consts)
    r = _run(nc, [arrays], core_ids=[0])
    return tuple(r.results[0][f"out_{i}"] for i in range(len(_OUTS)))
```

```python
from contextlib import ExitStack
import math

import numpy as np
import concourse.bass as bass
from concourse import mybir

ALU = mybir.AluOpType
ACT = mybir.ActivationFunctionType
AX = mybir.AxisListType.X
F32 = mybir.dt.float32
F32R = mybir.dt.float32r

D = 2048
KT = D // 128
SEQ, NB, NQ = 512, 8, 4
NS = NB * NQ
T = SEQ + NS
HALF = T // 2
WIN = 128
NEG = -1.0e30
EPS = 1e-6

C_QA, C_KA, C_VA, C_GA = 0, 1024, 1152, 1280
C_QB, C_KB, C_VB, C_GB, C_LR = 2304, 2816, 3328, 4352, 5376
C_QC, C_KC, C_VC, C_GC = 0, 2048, 4096, 8192
HA, HB, HC = 16, 4, 8
RANK = 16

N_KV = 0
N_A = 3
N_B = N_A + 2 * 8
N_W0 = N_B + 6 * HB
N_C = N_W0 + KT
N_WA = N_C + 12 * HC
N_WB = N_WA + KT
N_END = N_WB + KT

RT_W = T + NS + NB + 6


def shape_constants():
    c = {}
    c["ident"] = np.eye(128, dtype=np.float32)
    c["ones"] = np.ones((128, 128), np.float32)
    i = np.arange(128)
    c["blk64"] = (i[:, None] // 64 == i[None, :] // 64).astype(np.float32)
    same = i[:, None] // 64 == i[None, :] // 64
    c["gmask"] = (same & (i[:, None] <= i[None, :])).astype(np.float32)
    j = np.arange(NS)
    sm = (j[:, None] // NQ == j[None, :] // NQ) & (j[:, None] <= j[None, :])
    smask = np.zeros((128, NS + NB), np.float32)
    smask[:NS, :NS] = sm
    smask[:NS, NS:] = (j[:, None] // NQ == np.arange(NB)[None, :])
    c["smask"] = smask
    dist = 255 - np.arange(384)
    ok = (dist >= 0) & (dist <= WIN)
    dd = np.clip(dist, 0, WIN)
    ratio = np.log(np.maximum(dd, 1).astype(np.float32) / np.float32(16)) / math.log(128 / 16)
    large = np.minimum(16 + (ratio * 16).astype(np.int32), 31)
    bucket = np.where(dd < 16, dd, large)
    hot = np.zeros((33, 384), np.float32)
    hot[bucket[ok], np.nonzero(ok)[0]] = 1.0
    hot[32, ~ok] = NEG
    c["hot"] = hot
    pos = np.concatenate([np.arange(SEQ), 1024 + np.tile(np.arange(NQ), NB)]).astype(np.float32)
    inv = (np.float32(10000.0) ** (-np.arange(128, dtype=np.float32) / np.float32(128))).astype(np.float32)
    ang = (inv[:, None] * pos[None, :]).astype(np.float32).astype(np.float64)
    c["rope"] = np.stack([np.cos(ang), np.sin(ang)], 1).astype(np.float32)
    ret = np.zeros((HC, 128, RT_W), np.float32)
    p = np.arange(128)[:, None].astype(np.float64)
    for h in range(HC):
        lg = math.log1p(-2.0 ** (-5.0 - h))
        dcol = np.arange(SEQ)[None, :] - p
        ret[h, :, :SEQ] = np.where(dcol >= 0, np.exp(np.maximum(dcol, 0) * lg), 0) / 16
        ds = j[None, :] - j[:, None]
        ret[h, :NS, SEQ:T] = np.where(sm, np.exp(np.maximum(ds, 0) * lg), 0) / 16
        ret[h, :, T:T + NS] = np.exp((j % NQ + 1.0) * lg)[None, :]
        ret[h, :3 * NS, T + NS:T + NS + NB] = np.tile(smask[:NS, NS:], (3, 1))
        for t in range(4):
            ret[h, :, T + NS + NB + t] = np.exp((SEQ - 1.0 - 128 * t - p[:, 0]) * lg) / 16
        ret[h, :, T + NS + NB + 4] = math.exp(NQ * lg)
        ret[h, :NS, T + NS + NB + 5] = np.exp((NQ - 1.0 - j % NQ) * lg) / 16
    c["ret"] = ret
    c["sel"] = (i[:, None] % 32 == np.arange(32)[None, :]).astype(np.float32)
    return c


def build(nc, I, O, C):
    ctx = ExitStack()
    with ctx:
        def sb(name, shape, dt=F32):
            return ctx.enter_context(nc.sbuf_tensor(name, shape, dt))

        def sem(name):
            return ctx.enter_context(nc.semaphore(name))

        ds = bass.ds
        ident, ones = sb("ident", [128, 128]), sb("ones", [128, 128])
        vecT = sb("vecT", [128, 128])
        vecT2 = sb("vecT2", [128, 24])
        eps = sb("eps", [128, 8])
        mod = [sb("mod_even", [128, 48, 9]), sb("mod_odd", [128, 48, 9])]
        cs = sb("cs", [128, KT * 9 + 23])
        sel = sb("sel", [128, 32])
        WR = sb("W_raw", [128, 4 * KT * 128])
        WH = sb("W_hi", [128, 2, KT, 128], F32R)
        WL = sb("W_lo", [128, 2, KT, 128], F32R)
        AH = sb("act_hi", [128, KT, T], F32R)
        AL = sb("act_lo", [128, KT, T], F32R)
        R3 = sb("tiles", [128, KT, T])
        U = sb("work", [128, 8424])
        STK = sb("row_stacks", [128, 768], F32R)
        U2 = WR[:, 2 * KT * 128:4 * KT * 128]
        slot = [WR[:, s * 2048:(s + 1) * 2048].rearrange("p (k n) -> p k n", k=KT) for s in range(4)]
        slab = [WR[:, s * 4096:(s + 1) * 4096].rearrange("p (k n) -> p k n", k=KT) for s in range(2)]

        def u(at, *shape, base=None):
            n = int(np.prod(shape))
            v = (U if base is None else base)[:, at:at + n]
            if len(shape) == 2:
                v = v.rearrange("p (a b) -> p a b", a=shape[0])
            elif len(shape) == 3:
                v = v.rearrange("p (a b c) -> p a b c", a=shape[0], b=shape[1])
            return v

        PJ = ctx.enter_context(nc.psum_tensor("PJ", [128, 2, 512], F32))
        AD = ctx.enter_context(nc.psum_tensor("AD", [128, 512], F32))
        X = ctx.enter_context(nc.psum_tensor("X", [128, 5, 512], F32))

        def dram(name, shape):
            return nc.dram_tensor(name, shape, F32).ap()

        res_d = [dram("resid0", (KT, 128, T)), dram("resid1", (KT, 128, T)), dram("resid2", (KT, 128, T))]
        mix_d = dram("mixed_odd", (2 * KT, 128, T))
        rel_d = dram("rel_rows", (HA, 384))
        bias_d = dram("bias_tiles", (HA, 128, 256))

        xs = u(0, 2, 2048)
        ssum, sq, rstd = u(4096, T), u(4640, 2, T), u(5728, T)
        tk, ts, hs = u(6272, 2, 512), u(0, KT, NS), u(512, KT, NS)
        vr, vr2, vc = u(7296, 128), u(7424, 128), u(7552, 128)
        craw, cexp = u(7680, KT, 9), u(7824, KT, 9)
        G = u(7680, KT, 9)
        arow0 = u(6272, 2, 256)
        arow = R3[:, 15, 288:544]
        KC, PT, PTs, PTn = u(0, NB, 128), u(0, 4, 2, 128), u(0, 4, 128), u(512, 4, 128)
        VCc, KCT = u(1024, NB, 128), u(2048, NB, 128)
        kdup = [u(3072, T), u(3616, T)]
        vtok, vtok_s = u(4160, 4, 128), u(4672, 128)
        blk64, LR, smask = u(4800, 128), u(4928, T), u(5472, NS + NB)
        gmask = R3[:, 15, 0:128]
        bmask = smask[:, NS:NS + NB]
        qsT = u(5640, NB, 8, NQ)
        sk, skrow, sk2 = u(5896, 16), u(5912, 1), u(5914, 2)
        mx, nm, den, es, rec = (u(5920 + 4 * n, 4) for n in range(5))
        qg8 = u(5944, 1)
        QT, QN, E = u(5952, T), u(6496, T), u(7040, T)
        tiles8 = R3[:, 8:10].rearrange("p a b -> p (a b)")
        S, SS = (tiles8[:, 0:4 * w].rearrange("p (a b) -> p a b", a=4) for w in (256, 160))
        kn, biasT = R3[:, 8], R3[:, 10, 0:512].rearrange("p (a b) -> p a b", a=2)
        biasS, OSm = u(5952, 4, 160), u(7040, 8, NS)
        relS, relb, hot = R3[:, 11, 0:384], R3[:, 11, 384:400], u(2048, 384)
        BP = u(0, 4, T)
        ST = u(2176, 8, 256)
        LAt, LAs, AT, ATs = u(4224, 4, 128), u(4736, 128), u(4224, 4, 128), u(4736, NS)
        sq1 = u(4224, T)
        WLR = R3[:, 14, 0:512]
        WLH = u(8168, 128)
        EBP, T1, T2 = u(5512, T), u(6056, T), u(6600, T)
        KDT, KDTs, kdm = u(5512, 4, 128), u(6600, 128), u(6728, 2, 128)
        VTB, VTBs = u(7144, 4, 256), u(8168, 256)
        ebl, blast = u(4864, 16), u(4880, 16)
        resb, yst, wsq = u(0, 2, T), u(1088, 2, T), u(2176, T)
        smp = u(2720, NS)
        ost = u(2760, 2, 5, 128)
        cos, sin = u(0, T), u(544, T)
        CT, CTs, KTK, KTKs = u(1088, 4, 512), u(3136, 512), u(3648, 4, 256), u(4672, 256)
        RT = u(4928, RT_W)
        r1, r2 = u(5520, T), u(6064, T)
        qi = u(6608, 2, NS)
        CST = u(6672, 2, 512)
        r3 = u(7696, T)
        SB = u(0, 4, 2, 512, base=U2)
        qk_flat = R3[:, 0:4, :].rearrange("p a b -> p (a b)")
        RAT, RATs = qk_flat[:, 0:1280], qk_flat[:, 1280:1280 + NS]
        Qpad = qk_flat[:, 1632:2144].rearrange("p (k b t) -> p k b t", k=2, b=NB)
        VS, KM = STK[0:3 * NS, 0:512], STK[0:3 * NS, 512:768]
        SR = R3[:, 5, 0:512]
        KS = R3[0:3 * NS, 6, 0:256]
        RAOFF = [0, 512, 896, 1152]

        names = ("vld vld2 xT_ready vec_ps vec_sb xa xd sqd ms rb tset sset hi_t nl nls "
                 "ad_done ad_ev hi lo half ev "
                 "c_exp v_chain a_chain res_st "
                 "kv_ps kv_ms kv_rb kn_ready kdup_ready kv_out_sb kv_st kct_ps kct_sb rel_sb "
                 "rel_st bias_ld "
                 "a_ms a_rb a_qn a_qs a_sc a_sadd a_mxd a_exp a_p a_tp a_ptA a_ptV a_pv a_eg a_gate "
                 "bs_ld s_sc s_mx s_exp s_p s_tp s_pt s_pv s_os s_gate swa_st "
                 "b_wl b_z b_ln b_la b_bc b_eb b_dif b_kdx b_qk b_kd b_at b_vt b_vta b_kt b_kta b_atm b_dS b_st "
                 "b_o b_oe b_so b_sld b_stf b_sup b_ssb b_ms b_rb b_eg b_gate b_kdm b_pst b_sq1 "
                 "wy wssq wsqa wtp wotp "
                 "c_tab c_rot c_sc c_scv c_kt c_kta c_vt c_vta c_vtv c_st c_stv c_o c_oe c_os "
                 "c_km c_up c_upv c_ms c_rb c_eg c_gate c_mst c_ssq c_pst m_hi pool_passed act_passed ad_rows ad_sel b_free c_mfree c_pfree ost_free ")
        s = {}
        for n in names.split():
            s[n] = sem(n)
        wld = [sem(f"w_loaded{n}") for n in range(2)]
        adl = [sem(f"ada_tile_loaded{n}") for n in range(2)]
        xld = [sem(f"x_loaded{n}") for n in range(2)]
        rld = [sem(f"resid_loaded{n}") for n in range(2)]
        sld = [sem(f"state_loaded{n}") for n in range(4)]
        sst = [sem(f"state_stored{n}") for n in range(4)]
        yst_s = [sem(f"y_stored{n}") for n in range(2)]
        ost_s = [sem(f"out_stored{n}") for n in range(2)]
        raw = [sem(f"mixed_loaded{n}") for n in range(4)]

        class Chain:

            def __init__(self, eng, sm):
                self.eng, self.sm, self.base, self.total, self.k, self.per = eng, sm, 0, 0, 0, None

            def loop(self, i, per):
                assert self.per is None
                self.total += self.k
                self.base, self.k, self.per = i * per + self.total, 0, per

            def end(self, trips):
                assert self.k == self.per, f"{self.sm}: {self.k} links in the loop, {self.per} declared"
                self.total += self.per * trips
                self.base, self.k, self.per = self.total, 0, None

            def __call__(self, ins):
                self.k += 1
                ins.then_inc(self.sm, 1)
                self.eng.wait_ge(self.sm, self.base + self.k)

        block = ctx.enter_context(nc.Block())

        @block.sync
        def _(sp):
            def load(n, par, src, cols=128):
                if not isinstance(n, int) or n >= 2:
                    sp.wait_ge(s["lo"], n - 1)
                sp.dma_start(slot[par][:, :, 0:cols], src).then_inc(wld[par], 16)

            wie = I["w_in_even"][0].rearrange("(k p) n -> p k n", p=128)
            woe = I["w_out_even"][0].rearrange("(k p) n -> p k n", p=128)
            wio = I["w_in_odd"][0].rearrange("(k p) n -> p k n", p=128)
            woo = I["w_out_odd"][0].rearrange("(k p) n -> p k n", p=128)
            ae = I["ada_w_even"][0].rearrange("(k p) n -> p k n", p=128)
            ao = I["ada_w_odd"][0].rearrange("(k p) n -> p k n", p=128)
            xp = I["x_prompt"][0]
            xsm = I["x_sample"].rearrange("b t d -> (b t) d")
            for t in range(5):
                if t >= 2:
                    sp.wait_ge(s["xT_ready"], 4 * (t - 1))
                if t < 4:
                    sp.dma_start(xs[:, t % 2], xp[t * 128:(t + 1) * 128, :]).then_inc(xld[t % 2], 16)
                else:
                    sp.dma_start(xs[0:NS, 0], xsm).then_inc(xld[0], 16)
                if t == 1:
                    for sl in range(2):
                        sp.dma_start(slab[sl], ae[:, :, sl * 256:(sl + 1) * 256]).then_inc(adl[sl], 16)
            with sp.Fori(1, 8) as i:
                for sl in range(2):
                    sp.wait_ge(s["ad_done"], i * 2 + (sl - 1))
                    sp.dma_start(slab[sl], ae[:, :, ds(i * 512 + sl * 256, 256)]).then_inc(adl[sl], 16)
            sp.wait_ge(s["ad_done"], 15)
            load(0, 0, wie[:, :, C_KA:C_KA + 128])
            load(1, 1, wie[:, :, C_VA:C_VA + 128])
            load(2, 0, wie[:, :, C_LR:C_LR + RANK], RANK)

            def ada_pair(unit, w, col):
                sp.wait_ge(s["ad_done"], unit)
                sp.dma_start(slab[1], w[:, :, ds(col, 256)]).then_inc(adl[1], 16)

            with sp.Fori(0, 8) as i:
                load(i * 2 + N_A, N_A % 2, wie[:, :, ds(i * 128 + C_QA, 128)])
                ada_pair(i * 1 + 16, ae, i * 256 + 4096)
                load(i * 2 + (N_A + 1), (N_A + 1) % 2, wie[:, :, ds(i * 128 + C_GA, 128)])
            with sp.Fori(0, HB) as h:
                src = (ds(h * 128 + C_QB, 128), ds(h * 128 + C_KB, 128), ds(h * 256 + C_VB, 128),
                       ds(h * 256 + (C_VB + 128), 128), ds(h * 256 + C_GB, 128), ds(h * 256 + (C_GB + 128), 128))
                for j in range(6):
                    load(h * 6 + (N_B + j), (N_B + j) % 2, wie[:, :, src[j]])
                    ada_pair(h * 6 + (24 + j), ao, h * 1536 + 256 * j)

            def out_product(base, w):
                with sp.Fori(0, KT // 2) as m:
                    for j in range(2):
                        load(m * 2 + (base + j), (base + j) % 2, w[:, :, ds(m * 256 + 128 * j, 128)])

            out_product(N_W0, woe)
            with sp.Fori(0, HC) as h:
                src = [ds(h * 256 + (c + 128 * e), 128) for c in (C_QC, C_KC) for e in range(2)] + \
                    [ds(h * 512 + (c + 128 * e), 128) for c in (C_VC, C_GC) for e in range(4)]
                for j in range(12):
                    load(h * 12 + (N_C + j), (N_C + j) % 2, wio[:, :, src[j]])
            out_product(N_WA, woo[:, 0:KT, :])
            out_product(N_WB, woo[:, KT:2 * KT, :])

        @block.gpsimd
        def _(pool):
            def wait_for(sm, value, tell="pool_passed"):
                pool.wait_ge(sm, value)
                pool.sem_inc(s[tell], 1)

            pool.sem_inc(s["b_free"], 1)
            pool.sem_inc(s["c_mfree"], 1)
            pool.sem_inc(s["c_pfree"], 1)
            pool.sem_inc(s["ost_free"], 2)
            for dst, src in ((ident[:, :], C["ident"]), (ones[:, :], C["ones"]), (sel[:, :], C["sel"])):
                pool.dma_start(dst, src).then_inc(s["vld"], 16)
            be, bo = (I[k][0].rearrange("(r c) -> r c", c=128) for k in ("ada_b_even", "ada_b_odd"))
            ge, go = (I[k][0].rearrange("(r c) -> r c", c=128) for k in ("norm_g_even", "norm_g_odd"))
            for a, b, src in ((0, 48, be), (48, 96, bo), (96, 112, ge), (112, 128, go)):
                pool.dma_start(vr[a:b, :], src).then_inc(s["vld"], 16)
            for a, b, src in ((0, 16, I["c_prompt"][0].rearrange("(r c) -> r c", c=128)),
                              (16, 18, I["gla_g_even"][0].rearrange("(r c) -> r c", c=128)),
                              (18, 22, I["ret_g_odd"][0].rearrange("(r c) -> r c", c=128))):
                pool.dma_start(vr2[a:b, :], src).then_inc(s["vld"], 16)
            for e in range(2):
                pool.dma_start(vr2[22:23, 64 * e:64 * e + 64], I["qn_g_even"]).then_inc(s["vld"], 16)
                pool.dma_start(vr2[23:24, 64 * e:64 * e + 64], I["kn_g_even"]).then_inc(s["vld"], 16)
            pool.dma_start(vc[:, :], I["c_sample"].rearrange("b (r c) -> (b r) c", c=128)).then_inc(s["vld"], 16)
            pool.wait_ge(s["xa"], 10)
            pool.wait_ge(s["xd"], 10)
            pool.dma_start(res_d[0].rearrange("k p t -> p k t"), R3[:, :, :]).then_inc(s["res_st"], 16)
            pool.wait_ge(s["res_st"], 16)
            pool.wait_ge(s["nl"], KT)
            pool.wait_ge(s["nls"], 1)
            kc = I["cache_swa_k"][0].rearrange("b s k d -> s b (k d)")
            vcc = I["cache_swa_v"][0].rearrange("b s k d -> s b (k d)")
            pool.dma_start(KC, kc).then_inc(s["vld2"], 16)
            pool.dma_start(VCc, vcc).then_inc(s["vld2"], 16)
            pool.dma_start(blk64, C["blk64"]).then_inc(s["vld2"], 16)
            pool.dma_start(gmask, C["gmask"]).then_inc(s["vld2"], 16)
            pool.dma_start(smask, C["smask"]).then_inc(s["vld2"], 16)
            pool.dma_start(hot[0:33], C["hot"]).then_inc(s["vld2"], 16)
            pool.dma_start(relb[0:32], I["rel_bias"]).then_inc(s["vld2"], 16)
            sinks = I["sinks_even"]
            pool.dma_start(sk[:, :], bass.AP(sinks.tensor, 0, [[0, 128], [1, HA]])).then_inc(s["vld2"], 16)
            with nc.allow_non_contiguous_dma(reason="one sink per row"):
                for e in range(2):
                    pool.dma_start(skrow[64 * e:64 * e + 64, :],
                                   bass.AP(sinks.tensor, 0, [[1, HA], [0, NQ], [1, 1]])).then_inc(s["vld2"], 16)
            for k, src in ((6, I["cache_swa_k"]), (7, I["cache_swa_v"])):
                pool.dma_start(O[k][0][:, 0:WIN - NQ], src[0][:, NQ:WIN]).then_inc(s["swa_st"], 16)
            pool.wait_ge(s["rel_sb"], 1)
            pool.dma_start(rel_d, relS[0:HA, :]).then_inc(s["rel_st"], 16)
            pool.wait_ge(s["rel_st"], 16)
            pool.dma_start(bias_d, bass.AP(rel_d.tensor, 127, [[384, HA], [-1, 128], [1, 256]])).then_inc(s["rel_st"], 16)
            pool.wait_ge(s["kv_out_sb"], 2)
            pool.dma_start(O[2][0, 0].rearrange("s k d -> s (k d)"), E[:, 0:128]).then_inc(s["kv_st"], 16)
            pool.dma_start(O[6][0][:, WIN - NQ:WIN].rearrange("b t k d -> b t (k d)"), E[0:NS, 128:256]).then_inc(s["kv_st"], 16)
            pool.dma_start(O[3][0, 0].rearrange("s k d -> s (k d)"), vtok[:, 3]).then_inc(s["kv_st"], 16)
            pool.dma_start(O[7][0][:, WIN - NQ:WIN].rearrange("b t k d -> b t (k d)"), vtok_s[0:NS]).then_inc(s["kv_st"], 16)
            pool.wait_ge(s["rel_st"], 32)
            pool.wait_ge(s["kv_st"], 64)

            def load_bias(i):
                pool.dma_start(biasT, bias_d[ds(i * 2, 2)].rearrange("h i s -> i h s")).then_inc(s["bias_ld"], 16)

            load_bias(0)
            with pool.Fori(1, 8) as i:
                wait_for(s["a_sadd"], i * 2)
                load_bias(i)
            pool.wait_ge(s["bs_ld"], 1)
            with nc.allow_non_contiguous_dma(reason="small bias rows"):
                for e in range(2):
                    for p in range(4):
                        r = slice(64 * e, 64 * e + 64)
                        pool.dma_start(biasS[r, p, 0:128],
                                       bass.AP(rel_d.tensor, 127, [[384, HA], [-1, NQ], [1, 128]])).then_inc(s["rel_st"], 16)
                        b = 2 * p + e
                        pool.dma_start(biasS[r, p, 128 + NQ * b:128 + NQ * b + NQ],
                                       bass.AP(rel_d.tensor, 255, [[384, HA], [-1, NQ], [1, NQ]])).then_inc(s["rel_st"], 16)
            pool.wait_ge(s["s_gate"], 1)
            pool.dma_start(WLR[0:RANK], I["w_lr_even"][0]).then_inc(s["vld2"], 16)
            pool.dma_start(WLR[RANK:RANK + 1], I["b_lr_even"]).then_inc(s["vld2"], 16)
            with pool.Fori(0, HB) as h:
                wait_for(s["b_st"], h * 8 + 8)
                pool.dma_start(O[4][0, 0, ds(h, 1)].rearrange("h p e -> p (h e)"), ST[:, 7]).then_inc(s["b_pst"], 16)
                wait_for(s["b_pst"], h * 16 + 16)
                wait_for(s["b_o"], h * 2 + 2)
                pool.dma_start(ST, I["state_gla"][0][:, ds(h, 1)].rearrange("b h p e -> p (b h) e")).then_inc(s["b_sld"], 16)
                wait_for(s["b_sup"], h * 8 + 8)
                pool.dma_start(O[8][0][:, ds(h, 1)].rearrange("b h p e -> p (b h) e"), ST).then_inc(s["b_stf"], 16)
                wait_for(s["b_stf"], h * 16 + 16, "b_free")

            def out_product(w, src, dst):
                def load(m, j):
                    pool.dma_start(resb[:, j], src[ds(m * 2 + j, 1)].rearrange("k p t -> p (k t)")).then_inc(rld[j], 16)

                def store(m, j):
                    if w < 2:
                        wait_for(s["wy"], m * 2 + (16 * w + j + 1))
                        y = R3[:, ds(m * 2 + j, 1), :].rearrange("p k t -> p (k t)") if w == 0 else yst[:, j]
                        pool.dma_start(dst[ds(m * 2 + j, 1)].rearrange("k p t -> p (k t)"), y).then_inc(yst_s[j], 16)
                    else:
                        wait_for(s["wotp"], m * 4 + (2 * j + 2))
                        pool.dma_start(O[0][0].rearrange("(t p) n -> p t n", p=128)[:, :, ds(m * 256 + 128 * j, 128)],
                                       ost[:, j, 0:4]).then_inc(ost_s[j], 16)
                        pool.dma_start(O[1].rearrange("b t n -> (b t) n")[:, ds(m * 256 + 128 * j, 128)],
                                       ost[0:NS, j, 4]).then_inc(ost_s[j], 16)
                        wait_for(ost_s[j], m * 32 + 32, "ost_free")

                load(0, 0)
                load(0, 1)
                with pool.Fori(0, KT // 2 - 1) as m:
                    for j in range(2):
                        wait_for(s["wy"], m * 2 + (16 * w + j + 1))
                        load(m + 1, j)
                        store(m, j)
                for j in range(2):
                    store(KT // 2 - 1, j)

            pool.wait_ge(s["b_gate"], 2 * HB)
            pool.wait_ge(s["nl"], 2 * KT)
            pool.wait_ge(s["res_st"], 16)
            out_product(0, res_d[0], res_d[1])
            pool.wait_ge(s["nl"], 3 * KT)
            pool.wait_ge(s["nls"], 2)

            def load_table(h):
                pool.dma_start(RT, C["ret"][ds(h, 1)].rearrange("h p w -> p (h w)")).then_inc(s["c_tab"], 16)

            load_table(0)
            pool.dma_start(u(0, 2 * T), C["rope"].rearrange("p a t -> p (a t)")).then_inc(s["c_tab"], 16)

            def load_state(h, b):
                pool.dma_start(SB[:, b % 4], I["state_ret"][0][b, ds(h, 1)].rearrange(
                    "h (k p) e -> p (h k) e", p=128)).then_inc(sld[b % 4], 16)

            def store_state(h, b):
                wait_for(s["c_upv"], h * 16 + (2 * b + 2))
                pool.dma_start(O[9][0][b, ds(h, 1)].rearrange("h (k p) e -> p (h k) e", p=128),
                               SB[:, b % 4]).then_inc(sst[b % 4], 16)

            def store_mixed(h):
                for e in range(4):
                    wait_for(s["c_gate"], h * 4 + (e + 1))
                    pool.dma_start(mix_d[ds(h * 4 + e, 1)].rearrange("k p t -> p (k t)"), R3[:, 12 + e]).then_inc(s["c_mst"], 16)
                wait_for(s["c_mst"], h * 64 + 64, "c_mfree")

            def head_transfers(h, first, last):
                if not first:
                    store_mixed(h - 1)
                for kk in range(2):
                    wait_for(s["c_stv"], h * 2 + (kk + 1))
                    pool.dma_start(O[5][0, 0, ds(h, 1), 128 * kk:128 * kk + 128].rearrange("h p e -> p (h e)"),
                                   CST[:, kk]).then_inc(s["c_pst"], 16)
                for b in range(4):
                    store_state(h, b)
                for b in range(4):
                    wait_for(sst[b], h * 32 + 16)
                    load_state(h, b + 4)
                wait_for(s["c_pst"], h * 32 + 32, "c_pfree")
                for b in range(4, NB):
                    store_state(h, b)
                for b in range(4):
                    wait_for(sst[b], h * 32 + 32)
                    if not last:
                        load_state(h + 1, b)
                if not last:
                    load_table(h + 1)

            for b in range(4):
                load_state(0, b)
            head_transfers(0, True, False)
            with pool.Fori(1, HC - 1) as h:
                head_transfers(h, False, False)
            head_transfers(HC - 1, False, True)
            store_mixed(HC - 1)

            def reload(w):
                for q in range(4):
                    pool.dma_start(R3[:, 4 * q:4 * q + 4],
                                   mix_d[KT * w + 4 * q:KT * w + 4 * q + 4].rearrange("k p t -> p k t")).then_inc(raw[q], 16)

            pool.wait_ge(s["c_mst"], 16 * 4 * HC)
            reload(0)
            out_product(1, res_d[1], res_d[2])
            reload(1)
            for j in range(2):
                pool.wait_ge(yst_s[j], 16 * 16)
            out_product(2, res_d[2], None)
            for j in range(2):
                pool.wait_ge(ost_s[j], 32 * 8)
            for b in range(4):
                pool.wait_ge(sst[b], 32 * HC)
            pool.wait_ge(s["b_pst"], 16 * HB)
            pool.wait_ge(s["b_stf"], 16 * HB)
            pool.wait_ge(s["swa_st"], 32)
            pool.wait_ge(s["kv_st"], 64)
            pool.wait_ge(s["c_pst"], 32 * HC)
            pool.wait_ge(s["c_tab"], 16 * HC + 16)
            pool.wait_ge(s["res_st"], 16)

        @block.scalar
        def _(act):
            link = Chain(act, s["a_chain"])
            A = nc.scalar.activation

            def wait_for(sm, value):
                act.wait_ge(sm, value)
                act.sem_inc(s["act_passed"], 1)

            def split_hi(n, par):
                if isinstance(n, int) and n >= N_END:
                    return
                act.wait_ge(wld[par], (n - par) * 8 + 16)
                if not (isinstance(n, int) and n < 2):
                    act.wait_ge(s["half"], n * 2 - 2)
                A(WH[:, par], slot[par], ACT.Copy).then_inc(s["hi"], 1)

            def evac(n, c, dst, rows=128):
                (act.wait_ge if isinstance(n, int) else wait_for)(s["half"], n * 2 + (c + 1))
                return A(dst, PJ[0:rows, c, 0:HALF], ACT.Copy).then_inc(s["ev"], 1)

            def halves(v):
                return v.rearrange("p (c t) -> p c t", c=2)

            def rsqrt_mean(dst, count, n):
                link(A(halves(dst), X[:, 0:2, 0:HALF], ACT.Ln, bias=eps[:, 0:1], scale=1.0 / n))
                return A(dst, dst, ACT.Exp, scale=-0.5)

            act.wait_ge(s["vec_sb"], 1)
            A(cexp, craw, ACT.Exp, scale=-1.0).then_inc(s["c_exp"], 1)
            for t in range(5):
                w = 128 if t < 4 else NS
                for q in (0, 2):
                    act.wait_ge(s["xT_ready"], 4 * t + q + 1)
                    A(R3[:, 4 * q:4 * q + 4, t * 128:t * 128 + w], X[:, q, 0:4 * w].rearrange("p (a b) -> p a b", a=4),
                      ACT.Copy).then_inc(s["xa"], 1)
            act.wait_ge(s["xa"], 10)
            act.wait_ge(s["xd"], 10)
            for k in range(KT):
                if k >= 2:
                    act.wait_ge(s["sqd"], k)
                A(sq[:, k % 2], R3[:, k], ACT.Square).then_inc(s["xa"], 1)
                act.wait_ge(s["ad_done"], k + 1)
                if k >= 2:
                    act.wait_ge(s["ad_sel"], k - 1)
                A(arow0[:, k % 2], AD[:, 0:256] if k % 2 == 0 else X[:, 4, 0:256], ACT.Copy).then_inc(s["ad_rows"], 1)

            def ada_rows(unit):
                act.wait_ge(s["ad_done"], unit)
                A(arow, AD[:, 0:256], ACT.Copy).then_inc(s["ad_rows"], 1)


            def norm(l):
                act.wait_ge(s["ms"], l + 1)
                rsqrt_mean(rstd, 0, D).then_inc(s["rb"], 1)
                for k in range(KT):
                    act.wait_ge(s["tset"], KT * l + k + 1)
                    A(AH[:, k, 0:SEQ], tk[:, k % 2], ACT.Identity, bias=mod[l][:, k, 0:1]).then_inc(s["hi_t"], 1)
                    if k == 0:
                        act.wait_ge(s["sset"], l + 1)
                        A(AH[:, :, SEQ:T], hs, ACT.Copy).then_inc(s["hi_t"], 1)

            split_hi(0, 0)
            norm(0)
            split_hi(1, 1)
            for c in range(2):
                evac(0, c, QT[:, c * HALF:(c + 1) * HALF])
            split_hi(2, 0)
            act.wait_ge(s["ev"], 2)
            A(E, QT, ACT.Square).then_inc(s["kv_rb"], 1)
            for c in range(2):
                evac(1, c, QN[:, c * HALF:(c + 1) * HALF])
            split_hi(3, 1)
            act.wait_ge(s["kv_ms"], 1)
            rsqrt_mean(E, 0, 64).then_inc(s["kv_rb"], 1)
            act.wait_ge(s["kn_ready"], 2)
            for kv in range(2):
                for e in range(2):
                    A(kdup[kv][64 * e:64 * e + 64], kn[64 * kv:64 * kv + 64], ACT.Copy).then_inc(s["kdup_ready"], 1)
            act.wait_ge(s["kct_ps"], 2)
            A(KCT, X[:, 0:2, :].rearrange("p a (b c) -> p (a b) c", c=128), ACT.Copy).then_inc(s["kct_sb"], 1)
            for c in range(2):
                act.wait_ge(s["half"], 5 + c)
                A(LR[0:RANK, c * HALF:(c + 1) * HALF], PJ[0:RANK, c, 0:HALF], ACT.Copy).then_inc(s["ev"], 1)

            def pair_of_heads(i, kv, i0):
                n = i * 2 + N_A
                split_hi(n + 1, 0)
                ada_rows(i * 1 + 17)
                for c in range(2):
                    evac(n, c, QT[:, c * HALF:(c + 1) * HALF])
                act.wait_ge(s["ev"], n * 2 + 2)
                act.wait_ge(s["a_gate"], i * 1 + 1)
                A(E, QT, ACT.Square).then_inc(s["a_rb"], 1)
                split_hi(n + 2, 1)
                act.wait_ge(s["a_ms"], i * 1 + 1)
                rsqrt_mean(E, 0, 64).then_inc(s["a_rb"], 1)
                wait_for(s["a_qn"], i * 1 + 1)
                for e in range(2):
                    A(qsT[64 * kv:64 * kv + 64, :, ds(i * 2 + (e - 2 * i0), 1), :].rearrange("p b g t -> p b (g t)"),
                      QN[64 * e:64 * e + 64, SEQ:T].rearrange("p (b t) -> p b t", t=NQ), ACT.Copy).then_inc(s["a_qs"], 1)
                for e in range(2):
                    act.wait_ge(s["a_mxd"], i * 2 + (e + 1))
                    for b in range(4):
                        A(S[:, b], S[:, b], ACT.Exp, bias=nm[:, b:b + 1], accum_out=den[:, b:b + 1]).then_inc(s["a_exp"], 1)
                    A(es, nm, ACT.Exp, bias=sk2[:, e:e + 1]).then_inc(s["a_exp"], 1)
                    act.wait_ge(s["a_tp"], i * 2 + (e + 1))
                    A(PT[:, 2:4].rearrange("p b h q -> p (b h q)"), X[:, 3, :], ACT.Copy).then_inc(s["a_ptA"], 1)
                for c in range(2):
                    evac(n + 1, c, R3[:, ds(i, 1), c * HALF:(c + 1) * HALF].rearrange("p a t -> p (a t)"))
                wait_for(s["ev"], n * 2 + 4)
                A(E, R3[:, ds(i, 1), :].rearrange("p a t -> p (a t)"), ACT.Exp, scale=-1.0).then_inc(s["a_eg"], 1)

            act.wait_ge(s["kv_st"], 64)
            for kv in range(2):
                with act.Fori(4 * kv, 4 * kv + 4) as i:
                    link.loop(i - 4 * kv, 1)
                    pair_of_heads(i, kv, 4 * kv)
                    link.end(4)
            act.wait_ge(s["s_mx"], 1)
            for p in range(4):
                A(SS[:, p], SS[:, p], ACT.Exp, bias=nm[:, p:p + 1], accum_out=den[:, p:p + 1]).then_inc(s["s_exp"], 1)
            A(es, nm, ACT.Exp, bias=skrow).then_inc(s["s_exp"], 1)
            act.wait_ge(s["s_tp"], 2)
            A(PTs.rearrange("p a b -> p (a b)"), X[:, 2, :], ACT.Copy).then_inc(s["s_pt"], 1)
            A(PTn[0:NS].rearrange("p a b -> p (a b)"), X[0:NS, 3, :], ACT.Copy).then_inc(s["s_pt"], 1)
            act.wait_ge(s["s_pv"], 1)
            for kv in range(2):
                for e in range(2):
                    for b in range(NB):
                        A(OSm[64 * e:64 * e + 64, 4 * kv:4 * kv + 4, NQ * b:NQ * b + NQ],
                          X[64 * kv:64 * kv + 64, 4, 32 * b:32 * b + 32].rearrange("p (g u t) -> p g u t", u=2, t=NQ)[:, :, e],
                          ACT.Copy).then_inc(s["s_os"], 1)

            with act.Fori(0, HB) as h:
                link.loop(h, 5)
                n = h * 6 + N_B
                act.wait_ge(s["b_z"], h * 2 + 2)
                link(A(T1[:, 0:SEQ], X[:, 0, :], ACT.Abs))
                link(A(T2[0:NS, 0:128], X[0:NS, 1, 0:128], ACT.Abs))
                link(A(T1[:, 0:SEQ], T1[:, 0:SEQ], ACT.Exp, scale=-1.0))
                link(A(T2[0:NS, 0:128], T2[0:NS, 0:128], ACT.Exp, scale=-1.0))
                A(T1[:, 0:SEQ], T1[:, 0:SEQ], ACT.Ln, bias=1.0).then_inc(s["b_ln"], 1)
                A(T2[0:NS, 0:128], T2[0:NS, 0:128], ACT.Ln, bias=1.0).then_inc(s["b_ln"], 1)
                split_hi(n + 1, 0)
                ada_rows(h * 6 + 25)
                act.wait_ge(s["b_bc"], h * 1 + 1)
                A(EBP[:, 0:SEQ], X[:, 2, :], ACT.Exp, scale=1.0 / 16).then_inc(s["b_eb"], 1)
                A(EBP[:, SEQ:T], X[:, 3, 0:NS], ACT.Exp, scale=1.0 / 16).then_inc(s["b_eb"], 1)
                A(T2[:, 0:SEQ], X[:, 2, :], ACT.Exp, scale=-1.0 / 16).then_inc(s["b_eb"], 1)
                A(T2[:, SEQ:T], X[:, 3, 0:NS], ACT.Exp, scale=-1.0 / 16).then_inc(s["b_eb"], 1)
                act.wait_ge(s["b_dif"], h * 1 + 1)
                A(T1, T1, ACT.Exp, scale=1.0 / 16).then_inc(s["b_kdx"], 1)
                for j in range(4):
                    if j > 0:
                        ada_rows(h * 6 + (25 + j))
                    for c in range(2):
                        evac(n + j, c, BP[:, j, c * HALF:(c + 1) * HALF])
                    split_hi(n + j + 2, (j + 1) % 2)
                    if j == 2:
                        act.wait_ge(s["b_kt"], h * 1 + 1)
                        A(KDT.rearrange("p a b -> p (a b)"), X[:, 2, :], ACT.Copy).then_inc(s["b_kta"], 1)
                        A(KDTs[0:NS], X[0:NS, 3, 0:128], ACT.Copy).then_inc(s["b_kta"], 1)
                act.wait_ge(s["b_vt"], h * 1 + 1)
                A(VTB.rearrange("p (x a) e -> p x (a e)", x=2), X[:, 0:2, :], ACT.Copy).then_inc(s["b_vta"], 1)
                A(VTBs[0:NS], X[0:NS, 2, 0:256], ACT.Copy).then_inc(s["b_vta"], 1)
                for j in range(4, 6):
                    ada_rows(h * 6 + (25 + j))
                    for c in range(2):
                        evac(n + j, c, R3[:, ds(h * 2 + (4 + j), 1), c * HALF:(c + 1) * HALF].rearrange("p a t -> p (a t)"))
                    if j < 5:
                        split_hi(n + j + 2, (j + 1) % 2)
                act.wait_ge(s["b_o"], h * 2 + 2)
                A(BP[:, 2:4, 0:SEQ], X[:, 0:2, :], ACT.Copy).then_inc(s["b_oe"], 1)
                act.wait_ge(s["b_so"], h * 1 + 1)
                A(BP[:, 2:4, SEQ:T], X[:, 4, 0:2 * NS].rearrange("p (e t) -> p e t", e=2), ACT.Copy).then_inc(s["b_oe"], 1)
                act.wait_ge(s["b_oe"], h * 2 + 2)
                A(T1, BP[:, 2], ACT.Square).then_inc(s["b_rb"], 1)
                A(sq1, BP[:, 3], ACT.Square).then_inc(s["b_rb"], 1)
                act.wait_ge(s["b_ms"], h * 1 + 1)
                rsqrt_mean(T1, 0, 256).then_inc(s["b_rb"], 1)
                wait_for(s["ev"], n * 2 + 12)
                for e in range(2):
                    if e == 1:
                        wait_for(s["b_gate"], h * 2 + 1)
                    A(sq1, R3[:, ds(h * 2 + (8 + e), 1), :].rearrange("p a t -> p (a t)"), ACT.Exp, scale=-1.0).then_inc(s["b_eg"], 1)
                link.end(HB)

            def out_product(w, base):
                def tiles(m, last=False):
                    for j in range(2):
                        if not (last and j == 1):
                            split_hi(m * 2 + (base + j + 1), (base + j + 1) % 2)
                        if w == 0:
                            wait_for(s["wy"], m * 2 + (j + 1))
                            A(wsq, R3[:, ds(m * 2 + j, 1), :].rearrange("p a t -> p (a t)"), ACT.Square).then_inc(s["wsqa"], 1)
                            act.wait_ge(s["wssq"], m * 2 + (j + 1))
                        if w == 2:
                            act.wait_ge(s["wtp"], m * 2 + (j + 3))
                            act.wait_ge(s["ost_free"], m * 2 + (j + 1))
                            A(ost[:, j, 0:4].rearrange("p a b -> p (a b)"), X[:, j, :], ACT.Copy).then_inc(s["wotp"], 1)
                            A(ost[0:NS, j, 4], X[0:NS, 2 + j, 0:128], ACT.Copy).then_inc(s["wotp"], 1)

                with act.Fori(0, KT // 2 - 1) as m:
                    tiles(m)
                tiles(KT // 2 - 1, last=(w == 2))

            def split_mixed(w):
                for k in range(KT):
                    if w > 0:
                        act.wait_ge(raw[k // 4], 16 * w)
                    if w == 2:
                        act.wait_ge(s["half"], 2 * (N_WA + KT))
                    if w == 0:
                        act.wait_ge(s["b_gate"], 2 * HB)
                        act.wait_ge(s["s_gate"], 1)
                    A(AH[:, k], R3[:, k], ACT.Copy).then_inc(s["m_hi"], 1)

            split_mixed(0)
            out_product(0, N_W0)
            norm(1)
            def squares(h):
                act.wait_ge(s["c_os"], h * 1 + 1)
                A(R3[:, 12:16, SEQ:T], AD[:, 0:4 * NS].rearrange("p (e t) -> p e t", e=4), ACT.Copy).then_inc(s["c_oe"], 1)
                act.wait_ge(s["c_oe"], h * 4 + 4)
                for e in range(4):
                    if e >= 2:
                        act.wait_ge(s["c_ssq"], h * 4 + (e - 1))
                    A((r1, r2)[e % 2], R3[:, 12 + e], ACT.Square).then_inc(s["c_rb"], 1)

            def gate_exps(h, part):
                if part == 0:
                    act.wait_ge(s["c_ms"], h * 1 + 1)
                    A(halves(r1), X[:, 2:4, 0:HALF], ACT.Ln, bias=eps[:, 0:1], scale=1.0 / 512).then_inc(s["c_rb"], 1)
                    act.wait_ge(s["c_rb"], h * 6 + 5)
                    A(r1, r1, ACT.Exp, scale=-0.5).then_inc(s["c_rb"], 1)
                    act.wait_ge(s["ev"], h * 24 + (2 * N_C + 24))
                for e in (2 * part, 2 * part + 1):
                    if e >= 1:
                        act.wait_ge(s["c_gate"], h * 4 + e)
                    A(r2, R3[:, 8 + e], ACT.Exp, scale=-1.0).then_inc(s["c_eg"], 1)

            def retention_head(h, first):
                n = h * 12 + N_C
                for j in range(12):
                    split_hi(n + (j + 1), (N_C + j + 1) % 2)
                    if j == 6:
                        act.wait_ge(s["c_tab"], h * 16 + 32)
                        act.wait_ge(s["c_kt"], h * 1 + 1)
                        for t in range(4):
                            A(KTK[:, t], X[:, 3 + t // 2, (t % 2) * 256:(t % 2) * 256 + 256], ACT.Copy,
                              scale=RT[:, T + NS + NB + t:T + NS + NB + t + 1]).then_inc(s["c_kta"], 1)
                        A(KTKs[0:NS], AD[0:NS, 0:256], ACT.Copy,
                          scale=RT[0:NS, T + NS + NB + 5:T + NS + NB + 6]).then_inc(s["c_kta"], 1)
                    if j == 8:
                        act.wait_ge(s["c_vt"], h * 1 + 1)
                        A(CT[:, 0:2], X[:, 0:2, :], ACT.Copy).then_inc(s["c_vta"], 1)
                        A(CTs[0:NS], X[0:NS, 4, :], ACT.Copy).then_inc(s["c_vta"], 1)
                        act.wait_ge(s["c_vta"], h * 4 + 2)
                        act.wait_ge(s["c_kta"], h * 8 + 5)
                        for g in (0, 2):
                            A(VS[NS * g:NS * g + NS], CTs[0:NS], ACT.Copy).then_inc(s["c_vta"], 1)
                        for g in (0, 1):
                            A(KS[NS * g:NS * g + NS], KTKs[0:NS], ACT.Copy).then_inc(s["c_kta"], 1)
                        A(KM[0:NS], KTKs[0:NS], ACT.Copy).then_inc(s["c_kta"], 1)
                    if j in (9, 10):
                        act.wait_ge(s["c_o"], h * 3 + (j - 8))
                        if not first:
                            act.wait_ge(s["c_mfree"], h * 1 + 1)
                        A(R3[:, 12 + 2 * (j - 9):14 + 2 * (j - 9), 0:SEQ], X[:, 2:4, :], ACT.Copy).then_inc(s["c_oe"], 1)
                    if j == 11:
                        act.wait_ge(s["c_o"], h * 3 + 3)
                        A(SR, X[:, 4, :], ACT.Copy).then_inc(s["c_oe"], 1)
                    if j == 8 and not first:
                        act.wait_ge(s["c_gate"], h * 4)
                    for c in range(2):
                        evac(n + j, c, R3[:, j, c * HALF:(c + 1) * HALF])
                    if j == 0 and not first:
                        squares(h - 1)
                    if j in (1, 2) and not first:
                        gate_exps(h - 1, j - 1)

            retention_head(0, True)
            with act.Fori(1, HC) as h:
                retention_head(h, False)
            squares(HC - 1)
            gate_exps(HC - 1, 0)
            gate_exps(HC - 1, 1)
            split_mixed(1)
            out_product(1, N_WA)
            split_mixed(2)
            out_product(2, N_WB)

        @block.vector
        def _(dve):
            link = Chain(dve, s["v_chain"])
            V = nc.vector
            TT, TS, STT = V.tensor_tensor, V.tensor_scalar, V.scalar_tensor_tensor

            def split_lo(n, par):
                dve.wait_ge(s["hi"], n + 1)
                TT(WL[:, par], slot[par], WH[:, par].bitcast(F32), ALU.subtract).then_inc(s["lo"], 1)

            link(V.memset(eps[:, :], EPS))
            V.memset(ssum, 0.0).then_inc(s["sqd"], 1)
            dve.wait_ge(s["vec_ps"], 3)
            link(V.tensor_copy(vecT[:, :], X[:, 0, 0:128]))
            link(V.tensor_copy(vecT2[:, :], X[:, 0, 128:152]))
            link(V.tensor_copy(craw[:, :, 0], X[:, 0, 128:144]))
            V.tensor_copy(craw[:, :, 1:9], X[:, 0, 256:384].rearrange("p (b k) -> p k b", b=NB)).then_inc(s["vec_sb"], 1)
            dve.wait_ge(s["c_exp"], 1)
            link(V.tensor_scalar_add(cexp, cexp, 1.0))
            link(V.reciprocal(cexp, cexp))
            link(V.memset(cs[:, KT * 9:], 0.0))
            TT(cs[:, 0:KT * 9].rearrange("p (k b) -> p k b", b=9), craw, cexp, ALU.mult).then_inc(s["vec_sb"], 1)
            for t in range(5):
                w = 128 if t < 4 else NS
                for q in (1, 3):
                    dve.wait_ge(s["xT_ready"], 4 * t + q + 1)
                    V.tensor_copy(R3[:, 4 * q:4 * q + 4, t * 128:t * 128 + w],
                                  X[:, q, 0:4 * w].rearrange("p (a b) -> p a b", a=4)).then_inc(s["xd"], 1)
            for k in range(KT):
                dve.wait_ge(s["xa"], k + 11)
                dve.wait_ge(s["sqd"], k + 1)
                TT(ssum, ssum, sq[:, k % 2], ALU.add).then_inc(s["sqd"], 1)
                dve.wait_ge(s["ad_sel"], k + 1)
                src = (AD[:, 256:288] if k % 2 == 0 else X[:, 4, 256:288]).rearrange("p (a b) -> p a b", b=16)[:, :, 0:9]
                TT(mod[0][:, 2 * k:2 * k + 2, :], src,
                   vecT[:, 2 * k:2 * k + 2].unsqueeze(2).to_broadcast([128, 2, 9]), ALU.add).then_inc(s["ad_ev"], 1)

            def norm(l):
                if l == 0:
                    dve.wait_ge(s["ad_ev"], 16)
                else:
                    dve.wait_ge(s["ad_ev"], 48)
                link(V.tensor_scalar_add(G, mod[l][:, KT:2 * KT, :], 1.0))
                link(TT(G, G, vecT[:, 96 + 16 * l:112 + 16 * l].unsqueeze(2).to_broadcast([128, KT, 9]), ALU.mult))
                dve.wait_ge(s["rb"], l + 1)

                def low(k):
                    dve.wait_ge(s["hi_t"], 17 * l + k + 1 + (k > 0))
                    STT(AL[:, k, 0:SEQ], tk[:, k % 2], mod[l][:, k, 0:1], AH[:, k, 0:SEQ].bitcast(F32),
                        ALU.add, ALU.subtract).then_inc(s["nl"], 1)

                for k in range(KT):
                    if k >= 2:
                        dve.wait_ge(s["nl"], 2 * KT * l + k - 1)
                    STT(tk[:, k % 2], R3[:, k, 0:SEQ], G[:, k, 0:1], rstd[:, 0:SEQ], ALU.mult, ALU.mult).then_inc(s["tset"], 1)
                    if k == 0:
                        link(TT(ts, R3[:, :, SEQ:T], rstd[:, SEQ:T].unsqueeze(1).to_broadcast([128, KT, NS]), ALU.mult))
                        t4 = ts.rearrange("p k (b t) -> p k b t", t=NQ)
                        h4 = hs.rearrange("p k (b t) -> p k b t", t=NQ)
                        link(TT(t4, t4, G[:, :, 1:9].unsqueeze(3).to_broadcast([128, KT, NB, NQ]), ALU.mult))
                        TT(h4, t4, mod[l][:, 0:KT, 1:9].unsqueeze(3).to_broadcast([128, KT, NB, NQ]), ALU.add).then_inc(s["sset"], 1)
                        dve.wait_ge(s["hi_t"], 17 * l + 2)
                        TT(AL[:, :, SEQ:T], hs, AH[:, :, SEQ:T].bitcast(F32), ALU.subtract).then_inc(s["nls"], 1)
                    if k > 0:
                        low(k - 1)
                low(KT - 1)

            norm(0)
            split_lo(0, 0)
            split_lo(1, 1)
            dve.wait_ge(s["res_st"], 16)
            link(V.memset(relb[32:33], 1.0))
            V.memset(LR[0:32], 1.0).then_inc(s["kn_ready"], 1)
            split_lo(2, 0)
            link(TS(qg8, vecT2[:, 22:23], 0.125, None, ALU.mult))
            dve.wait_ge(s["kv_ms"], 2)
            V.tensor_copy(relS[0:HA], X[0:HA, 2, 0:384]).then_inc(s["rel_sb"], 1)
            dve.wait_ge(s["kv_rb"], 2)
            STT(kn, QT, vecT2[:, 23:24], E, ALU.mult, ALU.mult).then_inc(s["kn_ready"], 1)
            dve.wait_ge(s["kv_ps"], 1)
            link(V.tensor_copy(vtok.rearrange("p a b -> p (a b)"), X[:, 3, :]))
            V.tensor_copy(vtok_s[0:NS], X[0:NS, 4, 0:128]).then_inc(s["kv_out_sb"], 1)
            dve.wait_ge(s["kv_ps"], 2)
            link(V.tensor_copy(E[:, 0:128], X[:, 2, 0:128]))
            V.tensor_copy(E[0:NS, 128:256], X[0:NS, 2, 128:256]).then_inc(s["kv_out_sb"], 1)
            split_lo(3, 1)
            dve.wait_ge(s["kdup_ready"], 4)
            dve.wait_ge(s["kv_ps"], 2)
            link(V.memset(S[:, 0, 0:128], NEG))
            dve.sem_inc(s["a_gate"], 1)
            dve.wait_ge(s["kv_st"], 64)

            def ada_sum(unit, dst, bias):
                dve.wait_ge(s["ad_sel"], unit)
                TT(dst, AD[:, 256:288].rearrange("p (a b) -> p a b", b=16)[:, :, 0:9],
                   vecT[:, bias].unsqueeze(2).to_broadcast([128, 2, 9]), ALU.add).then_inc(s["ad_ev"], 1)

            def pair_of_heads(i, kv):
                n = i * 2 + N_A
                split_lo(n + 1, 0)
                ada_sum(i * 1 + 17, mod[0][:, ds(i * 2 + 32, 2), :], ds(i * 2 + 32, 2))
                dve.wait_ge(s["a_rb"], i * 2 + 2)
                STT(QN, QT, qg8, E, ALU.mult, ALU.mult).then_inc(s["a_qn"], 1)
                link(V.tensor_copy(sk2, sk[:, ds(i * 2, 2)]))
                split_lo(n + 2, 1)
                dve.wait_ge(s["bias_ld"], i * 16 + 16)
                for e in range(2):
                    dve.wait_ge(s["a_sc"], i * 2 + (e + 1))
                    link(TT(S[:, 0, 128:256], X[:, 0, 128:256], biasT[:, e, 128:256], ALU.add))
                    link(TT(S[:, 1], X[:, 0, 256:512], biasT[:, e], ALU.add))
                    TT(S[:, 2:4], X[:, 1, :].rearrange("p (a b) -> p a b", a=2),
                       biasT[:, e].unsqueeze(1).to_broadcast([128, 2, 256]), ALU.add).then_inc(s["a_sadd"], 1)
                    dve.wait_ge(s["a_sadd"], i * 2 + (e + 1))
                    link(V.tensor_reduce(mx, S, AX, ALU.max))
                    TS(nm, mx, sk2[:, e:e + 1], -1.0, ALU.max, ALU.mult).then_inc(s["a_mxd"], 1)
                    dve.wait_ge(s["a_exp"], i * 10 + (5 * e + 5))
                    link(TT(rec, den, es, ALU.add))
                    link(V.reciprocal(rec, rec))
                    TT(S, S, rec.unsqueeze(2).to_broadcast([128, 4, 256]), ALU.mult).then_inc(s["a_p"], 1)
                    dve.wait_ge(s["a_tp"], i * 2 + (e + 1))
                    V.tensor_copy(PT[:, 0:2].rearrange("p b h q -> p (b h q)")[:, 128:512], X[:, 2, 128:512]).then_inc(s["a_ptV"], 1)
                    if e == 0:
                        link(V.memset(S[:, 0, 0:128], NEG))
                dve.wait_ge(s["a_eg"], i * 1 + 1)
                g = R3[:, ds(i, 1), :].rearrange("p a t -> p (a t)")
                link(V.tensor_scalar_add(E, E, 1.0))
                link(V.reciprocal(E, E))
                link(TT(g, g, E, ALU.mult))
                dve.wait_ge(s["a_pv"], i * 2 + 2)
                TT(g[:, 0:SEQ], g[:, 0:SEQ], X[:, 4, :], ALU.mult).then_inc(s["a_gate"], 1)
                link(V.memset(S[:, 0, 0:128], NEG))

            for kv in range(2):
                with dve.Fori(4 * kv, 4 * kv + 4) as i:
                    link.loop(i - 4 * kv, 16)
                    pair_of_heads(i, kv)
                    link.end(4)
            dve.wait_ge(s["a_qn"], 8)
            dve.wait_ge(s["a_qs"], 16)
            V.memset(biasS, NEG).then_inc(s["bs_ld"], 1)
            dve.wait_ge(s["rel_st"], 16 * 18)
            dve.wait_ge(s["s_sc"], 1)
            dve.wait_ge(s["bs_ld"], 1)
            link(TT(SS.rearrange("p (x a) b -> p x (a b)", x=2), X[:, 0:2, 0:320],
                    biasS.rearrange("p (x a) b -> p x (a b)", x=2), ALU.add))
            link(V.tensor_reduce(mx, SS, AX, ALU.max))
            TS(nm, mx, skrow, -1.0, ALU.max, ALU.mult).then_inc(s["s_mx"], 1)
            dve.wait_ge(s["s_exp"], 5)
            link(TT(rec, den, es, ALU.add))
            link(V.reciprocal(rec, rec))
            TT(SS, SS, rec.unsqueeze(2).to_broadcast([128, 4, 160]), ALU.mult).then_inc(s["s_p"], 1)
            dve.wait_ge(s["s_os"], 4 * NB)
            TT(R3[:, 0:8, SEQ:T], R3[:, 0:8, SEQ:T], OSm, ALU.mult).then_inc(s["s_gate"], 1)

            dve.wait_ge(s["vld2"], 16 * 12)
            with dve.Fori(0, HB) as h:
                link.loop(h, 14)
                n = h * 6 + N_B
                V.tensor_copy(WLH[0:RANK + 1], WLR[0:RANK + 1, ds(h * 128, 128)]).then_inc(s["b_wl"], 1)
                split_lo(n + 1, 0)
                dve.wait_ge(s["b_ln"], h * 2 + 2)
                STT(LAt.rearrange("p a b -> p (a b)"), X[:, 0, :], 0.0, T1[:, 0:SEQ], ALU.min, ALU.subtract).then_inc(s["b_la"], 1)
                STT(LAs[0:NS], X[0:NS, 1, 0:128], 0.0, T2[0:NS, 0:128], ALU.min, ALU.subtract).then_inc(s["b_la"], 1)
                ada_sum(h * 6 + 25, mod[1][:, ds(h * 12, 2), :], ds(h * 12 + 48, 2))
                dve.wait_ge(s["b_bc"], h * 1 + 1)
                dve.wait_ge(s["b_eb"], h * 4 + 4)
                dve.wait_ge(s["b_la"], h * 2 + 2)
                bl = X[:, 2, :].rearrange("p (c t) -> p c t", t=64)
                bs = X[:, 3, 0:NS].rearrange("p (b t) -> p b t", t=NQ)
                link(V.tensor_copy(blast[:, 0:8], bl[:, :, 63]))
                link(V.tensor_copy(blast[:, 8:16], bs[:, :, NQ - 1]))
                link(TT(T1[:, 0:SEQ].rearrange("p (c t) -> p c t", t=64), blast[:, 0:8].unsqueeze(2).to_broadcast([128, 8, 64]),
                        bl, ALU.subtract))
                TT(T1[:, SEQ:T].rearrange("p (b t) -> p b t", t=NQ), blast[:, 8:16].unsqueeze(2).to_broadcast([128, NB, NQ]),
                   bs, ALU.subtract).then_inc(s["b_dif"], 1)
                link(V.tensor_copy(ebl[:, 0:8], EBP[:, 0:SEQ].rearrange("p (c t) -> p c t", t=64)[:, :, 63]))
                link(V.tensor_copy(ebl[:, 8:16], EBP[:, SEQ:T].rearrange("p (b t) -> p b t", t=NQ)[:, :, NQ - 1]))
                dve.wait_ge(s["ev"], n * 2 + 2)
                split_lo(n + 2, 1)
                STT(BP[:, 0], BP[:, 0], 128.0 ** -0.5, EBP, ALU.mult, ALU.mult).then_inc(s["b_qk"], 1)
                dve.wait_ge(s["ev"], n * 2 + 4)
                dve.wait_ge(s["b_kdx"], h * 1 + 1)
                TT(T1, T1, BP[:, 1], ALU.mult).then_inc(s["b_kd"], 1)
                dve.wait_ge(s["b_kd"], h * 1 + 1)
                TT(BP[:, 1], BP[:, 1], T2, ALU.mult).then_inc(s["b_qk"], 1)
                split_lo(n + 3, 0)
                ada_sum(h * 6 + 26, mod[1][:, ds(h * 12 + 2, 2), :], ds(h * 12 + 50, 2))
                split_lo(n + 4, 1)
                ada_sum(h * 6 + 27, mod[1][:, ds(h * 12 + 4, 2), :], ds(h * 12 + 52, 2))
                dve.wait_ge(s["b_at"], h * 1 + 1)
                link(TT(AT, X[:, 0, :].rearrange("p (a b) -> p a b", a=4), gmask.unsqueeze(1).to_broadcast([128, 4, 128]), ALU.mult))
                TT(ATs[0:NS], X[0:NS, 1, 0:NS], smask[0:NS, 0:NS], ALU.mult).then_inc(s["b_atm"], 1)
                split_lo(n + 5, 0)
                ada_sum(h * 6 + 28, mod[1][:, ds(h * 12 + 6, 2), :], ds(h * 12 + 54, 2))
                split_lo(n + 6, 1)
                ada_sum(h * 6 + 29, mod[1][:, ds(h * 12 + 8, 2), :], ds(h * 12 + 56, 2))
                for c in range(8):
                    dS = X[:, (c % 2) * 2 + c // 4, (c // 2 % 2) * 256:(c // 2 % 2) * 256 + 256]
                    if c == 0:
                        dve.wait_ge(s["b_dS"], h * 1 + 1)
                        dve.wait_ge(s["b_free"], h * 1 + 1)
                        V.tensor_copy(ST[:, 0], dS).then_inc(s["b_st"], 1)
                    else:
                        dve.wait_ge(s["b_st"], h * 8 + c)
                        STT(ST[:, c], ST[:, c - 1], ebl[:, c:c + 1], dS, ALU.mult, ALU.add).then_inc(s["b_st"], 1)
                ada_sum(h * 6 + 30, mod[1][:, ds(h * 12 + 10, 2), :], ds(h * 12 + 58, 2))
                dve.wait_ge(s["b_kta"], h * 2 + 2)
                for b in range(NB):
                    if b >= 2:
                        dve.wait_ge(s["b_ssb"], h * 8 + (b - 1))
                    TS(kdm[0:NS, b % 2], KDTs[0:NS], bmask[0:NS, b:b + 1], None, ALU.mult).then_inc(s["b_kdm"], 1)
                    dve.wait_ge(s["b_ssb"], h * 8 + (b + 1))
                    STT(ST[:, b], ST[:, b], ebl[:, 8 + b:9 + b], X[:, 2 + b % 2, 0:256], ALU.mult, ALU.add).then_inc(s["b_sup"], 1)
                dve.wait_ge(s["b_rb"], h * 3 + 2)
                TT(T1, T1, sq1, ALU.add).then_inc(s["b_sq1"], 1)
                dve.wait_ge(s["b_rb"], h * 3 + 3)
                for e in range(2):
                    g = R3[:, ds(h * 2 + (8 + e), 1), :].rearrange("p a t -> p (a t)")
                    dve.wait_ge(s["b_eg"], h * 2 + (e + 1))
                    link(V.tensor_scalar_add(sq1, sq1, 1.0))
                    link(V.reciprocal(sq1, sq1))
                    link(TT(g, g, sq1, ALU.mult))
                    link(STT(BP[:, 2 + e], BP[:, 2 + e], vecT2[:, 16 + e:17 + e], T1, ALU.mult, ALU.mult))
                    TT(g, g, BP[:, 2 + e], ALU.mult).then_inc(s["b_gate"], 1)
                link.end(HB)

            def split_mixed(w):
                for k in range(KT):
                    dve.wait_ge(s["m_hi"], KT * w + k + 1)
                    TT(AL[:, k], R3[:, k], AH[:, k].bitcast(F32), ALU.subtract).then_inc(s["nl"], 1)

            def out_product(w, base, l):
                if w == 0:
                    dve.wait_ge(s["b_free"], HB + 1)
                    link(V.memset(ssum, 0.0))
                if w == 2:
                    for j in range(2):
                        dve.wait_ge(yst_s[j], 256)
                def tiles(m, last=False):
                    for j in range(2):
                        n = m * 2 + (base + j)
                        if not (last and j == 1):
                            split_lo(n + 1, (base + j + 1) % 2)
                        dve.wait_ge(rld[j], m * 16 + (128 * w + 16))
                        y = R3[:, ds(m * 2 + j, 1), :].rearrange("p a t -> p (a t)") if w == 0 else yst[:, j]
                        gp = mod[l][:, ds(m * 2 + (32 + j), 1), 0:1].rearrange("p a b -> p (a b)")
                        gs = mod[l][:, ds(m * 2 + (32 + j), 1), 1:9].rearrange("p a b -> p (a b)")
                        link(V.tensor_copy(eps[:, 6:7], gp))
                        if w == 1:
                            dve.wait_ge(yst_s[j], m * 16 + 128)
                        if w == 2:
                            dve.wait_ge(s["wtp"], m * 2 + (j + 1))
                        dve.wait_ge(s["half"], n * 2 + 1)
                        STT(y[:, 0:HALF], PJ[:, 0, 0:HALF], eps[:, 6:7], resb[:, j, 0:HALF], ALU.mult, ALU.add).then_inc(s["ev"], 1)
                        dve.wait_ge(s["half"], n * 2 + 2)
                        link(STT(y[:, HALF:SEQ], PJ[:, 1, 0:SEQ - HALF], eps[:, 6:7], resb[:, j, HALF:SEQ], ALU.mult, ALU.add))
                        TT(smp.rearrange("p (b t) -> p b t", t=NQ), PJ[:, 1, SEQ - HALF:HALF].rearrange("p (b t) -> p b t", t=NQ),
                           gs.unsqueeze(2).to_broadcast([128, NB, NQ]), ALU.mult).then_inc(s["ev"], 1)
                        dve.wait_ge(s["ev"], n * 2 + 2)
                        TT(y[:, SEQ:T], smp, resb[:, j, SEQ:T], ALU.add).then_inc(s["wy"], 1)
                        if w == 0:
                            dve.wait_ge(s["wsqa"], m * 2 + (j + 1))
                            TT(ssum, ssum, wsq, ALU.add).then_inc(s["wssq"], 1)
                            dve.wait_ge(s["wssq"], m * 2 + (j + 1))

                with dve.Fori(0, KT // 2 - 1) as m:
                    link.loop(m, 4)
                    tiles(m)
                    link.end(KT // 2 - 1)
                tiles(KT // 2 - 1, last=(w == 2))

            split_mixed(0)
            out_product(0, N_W0, 0)
            norm(1)
            dve.wait_ge(s["c_tab"], 32)
            def head_squares(h):
                for e in range(4):
                    dve.wait_ge(s["c_rb"], h * 6 + (e + 1))
                    if e == 0:
                        V.tensor_copy(r3, r1).then_inc(s["c_ssq"], 1)
                    else:
                        dve.wait_ge(s["c_ssq"], h * 4 + e)
                        TT(r3, r3, (r1, r2)[e % 2], ALU.add).then_inc(s["c_ssq"], 1)

            def gates(h, part):
                dve.wait_ge(s["c_rb"], h * 6 + 6)
                for e in (2 * part, 2 * part + 1):
                    g, o = R3[:, 8 + e], R3[:, 12 + e]
                    dve.wait_ge(s["c_eg"], h * 4 + (e + 1))
                    link(V.tensor_scalar_add(r2, r2, 1.0))
                    link(V.reciprocal(r2, r2))
                    link(TT(g, g, r2, ALU.mult))
                    link(STT(o, o, vecT2[:, 18 + e:19 + e], r1, ALU.mult, ALU.mult))
                    TT(o, o, g, ALU.mult).then_inc(s["c_gate"], 1)

            def update_states(h, b0):
                for b in range(b0, b0 + 4):
                    TS(KM, KS, RT[0:3 * NS, T + NS + b:T + NS + b + 1], None, ALU.mult).then_inc(s["c_km"], 1)
                    for kk in range(2):
                        dve.wait_ge(s["c_up"], h * 16 + (2 * b + kk + 1))
                        STT(SB[:, b % 4, kk], SB[:, b % 4, kk], RT[:, T + NS + NB + 4:T + NS + NB + 5],
                            X[:, kk, :], ALU.mult, ALU.add).then_inc(s["c_upv"], 1)

            def retention_head(h, first):
                n = h * 12 + N_C
                split_lo(n + 1, (N_C + 1) % 2)
                if not first:
                    head_squares(h - 1)
                split_lo(n + 2, N_C % 2)
                if not first:
                    gates(h - 1, 0)
                split_lo(n + 3, (N_C + 1) % 2)
                if not first:
                    gates(h - 1, 1)
                for x in range(2):
                    dve.wait_ge(s["ev"], n * 2 + (4 + 4 * x))
                    x1, x2 = R3[:, 2 * x], R3[:, 2 * x + 1]
                    if x == 1:
                        dve.wait_ge(s["c_rot"], h * 2 + 1)
                    link(TT(r3, x1, sin, ALU.mult))
                    link(TT(r2, x2, sin, ALU.mult))
                    link(TT(x1, x1, cos, ALU.mult))
                    link(TT(x1, x1, r2, ALU.subtract))
                    link(TT(x2, x2, cos, ALU.mult))
                    TT(x2, x2, r3, ALU.add).then_inc(s["c_rot"], 1)
                    if x == 0:
                        split_lo(n + 4, N_C % 2)
                split_lo(n + 5, (N_C + 1) % 2)
                split_lo(n + 6, N_C % 2)
                dve.wait_ge(s["c_tab"], h * 16 + 32)
                dve.wait_ge(s["c_rot"], h * 2 + 2)
                for kk in range(2):
                    link(TT(qi[:, kk], R3[:, kk, SEQ:T], RT[:, T:T + NS], ALU.mult))
                dve.wait_ge(s["c_sc"], h * 1 + 1)
                dve.wait_ge(s["c_kt"], h * 1 + 1)
                for t, src in enumerate((X[:, 0, 0:512], X[:, 1, 0:384], X[:, 2, 0:256], X[:, 1, 384:512])):
                    link(TT(RAT[:, RAOFF[t]:RAOFF[t] + SEQ - 128 * t], src, RT[:, 0:SEQ - 128 * t], ALU.mult))
                TT(RATs[0:NS], X[0:NS, 2, 256:256 + NS], RT[0:NS, SEQ:T], ALU.mult).then_inc(s["c_scv"], 1)
                link(V.memset(qk_flat[:, 1632:2144], 0.0))
                for kk in range(2):
                    at = 1632 + 256 * kk
                    V.tensor_copy(qk_flat[:, at:at + NB * (NS + NQ)].rearrange("p (b u) -> p b u", b=NB)[:, :, 0:NQ],
                                  qi[:, kk].rearrange("p (b t) -> p b t", t=NQ)).then_inc(s["c_scv"], 1)
                split_lo(n + 7, (N_C + 1) % 2)
                split_lo(n + 8, N_C % 2)
                dve.wait_ge(s["c_vt"], h * 1 + 1)
                V.tensor_copy(CT[:, 2:4], X[:, 2:4, :]).then_inc(s["c_vtv"], 1)
                dve.wait_ge(s["c_vta"], h * 4 + 4)
                TT(VS[NS:2 * NS], CTs[0:NS], VS[0:NS].bitcast(F32), ALU.subtract).then_inc(s["c_vtv"], 1)
                dve.wait_ge(s["c_kta"], h * 8 + 8)
                TT(KS[2 * NS:3 * NS], KTKs[0:NS], KM[0:NS].bitcast(F32), ALU.subtract).then_inc(s["c_vtv"], 1)
                split_lo(n + 9, (N_C + 1) % 2)
                dve.wait_ge(s["c_vtv"], h * 3 + 3)
                if not first:
                    dve.wait_ge(s["c_pfree"], h * 1 + 1)
                for kk in range(2):
                    dve.wait_ge(s["c_st"], h * 2 + (kk + 1))
                    V.tensor_copy(CST[:, kk], X[:, kk, :]).then_inc(s["c_stv"], 1)
                split_lo(n + 10, N_C % 2)
                update_states(h, 0)
                split_lo(n + 11, (N_C + 1) % 2)
                split_lo(n + 12, N_C % 2)
                update_states(h, 4)

            link.loop(0, 17)
            retention_head(0, True)
            link.end(1)
            with dve.Fori(1, HC) as h:
                link.loop(h - 1, 33)
                retention_head(h, False)
                link.end(HC - 1)
            head_squares(HC - 1)
            gates(HC - 1, 0)
            gates(HC - 1, 1)
            split_mixed(1)
            out_product(1, N_WA, 1)
            split_mixed(2)
            out_product(2, N_WB, 1)

        @block.tensor
        def _(pe):
            mm = nc.tensor.matmul

            def tr(out, in_, rows=128):
                return nc.tensor.transpose(out, in_, ident[0:rows, 0:rows])

            def product(n, par, ready=None, between=()):
                for c in range(2):
                    product_half(n, par, c, ready, between[2 * c:2 * c + 2])

            def product_half(n, par, c, ready=None, between=()):
                if c == 0:
                    pe.wait_ge(s["lo"], n + 1)
                if not (isinstance(n, int) and n == 0):
                    pe.wait_ge(s["ev"], n * 2 + (c - 1))
                for k in range(KT):
                    if ready is not None and c == 0:
                        pe.wait_ge(s["nl"], ready + k + 1)
                    for a, (w, x) in enumerate(((WH, AH), (WH, AL), (WL, AH))):
                        last = mm(PJ[:, c, 0:HALF], w[:, par, k], x[:, k, c * HALF:(c + 1) * HALF],
                                  start=(k == 0 and a == 0), stop=(k == KT - 1 and a == 2))
                    if k == KT // 2 - 1 and between:
                        between[0]()
                last.then_inc(s["half"], 1)
                if between:
                    between[1]()

            def sum_rows(lhs, src, banks=(0, 1)):
                for c in range(2):
                    last = mm(X[:, banks[c], 0:HALF], lhs, src[:, c * HALF:(c + 1) * HALF], start=True, stop=True)
                return last

            def ada_rows(w, bank):
                for k in range(KT):
                    g = 32 * (k % 4)
                    last = mm(bank[g:g + 32, 0:256], cs[:, 9 * k:9 * k + 32], w[:, k], start=(k < 4), stop=(k >= KT - 4),
                              tile_position=(0, g))
                last.then_inc(s["ad_done"], 1)

            def ada_select(unit, rows, bank):
                pe.wait_ge(s["ad_rows"], unit)
                for e in range(2):
                    last = mm(bank[:, 256 + 16 * e:256 + 16 * e + 9], rows[:, 128 * e:128 * e + 128], sel[:, 0:9],
                              start=True, stop=True)
                last.then_inc(s["ad_sel"], 1)

            pe.wait_ge(s["vld"], 16 * 15)
            tr(X[:, 0, 0:128], vr).then_inc(s["vec_ps"], 1)
            tr(X[:, 0, 128:152], vr2[0:24], 24).then_inc(s["vec_ps"], 1)
            tr(X[:, 0, 256:384], vc).then_inc(s["vec_ps"], 1)
            pe.wait_ge(s["vec_sb"], 1)
            for t in range(5):
                w = 128 if t < 4 else NS
                pe.wait_ge(xld[t % 2], 16 * (t // 2 + 1))
                for q in range(4):
                    if t > 0:
                        pe.wait_ge(s["xa" if q % 2 == 0 else "xd"], 2 * (t - 1) + q // 2 + 1)
                    for a in range(4):
                        last = tr(X[:, q, a * w:(a + 1) * w], xs[0:w, t % 2, (4 * q + a) * 128:(4 * q + a + 1) * 128], w)
                    last.then_inc(s["xT_ready"], 1)
            pe.wait_ge(s["vec_sb"], 2)

            def ada_slab(i, sl):
                pe.wait_ge(adl[sl], i * 16 + 16)
                ada_rows(slab[sl], AD if sl == 0 else X[:, 4])

            def ada_slabs_select(i):
                for sl in range(2):
                    ada_select(i * 2 + (sl + 1), arow0[:, sl], AD if sl == 0 else X[:, 4])

            ada_slab(0, 0)
            ada_slab(0, 1)
            ada_slabs_select(0)
            with pe.Fori(1, 8) as i:
                for sl in range(2):
                    pe.wait_ge(s["ad_ev"], i * 2 + (sl - 1))
                    ada_slab(i, sl)
                ada_slabs_select(i)
            pe.wait_ge(s["sqd"], KT + 1)
            pe.wait_ge(s["xa"], 10)
            pe.wait_ge(s["xd"], 10)
            sum_rows(ones[:, :], ssum).then_inc(s["ms"], 1)
            pe.wait_ge(s["nls"], 1)
            product(0, 0, ready=0)
            product(1, 1)
            pe.wait_ge(s["vld2"], 16 * 10)
            pe.wait_ge(s["kv_rb"], 1)
            sum_rows(blk64, E).then_inc(s["kv_ms"], 1)
            pe.wait_ge(s["kn_ready"], 1)
            mm(X[0:HA, 2, 0:384], relb[0:33], hot[0:33], start=True, stop=True).then_inc(s["kv_ms"], 1)
            pe.wait_ge(s["ev"], 4)
            for t in range(4):
                tr(X[:, 3, 128 * t:128 * t + 128], QN[:, 128 * t:128 * t + 128])
            tr(X[0:NS, 4, 0:128], QN[:, SEQ:T]).then_inc(s["kv_ps"], 1)
            product(2, 0)
            pe.wait_ge(s["kn_ready"], 2)
            pe.wait_ge(s["rel_sb"], 1)
            tr(X[:, 2, 0:128], kn[:, SEQ - 128:SEQ])
            tr(X[0:NS, 2, 128:256], kn[:, SEQ:T]).then_inc(s["kv_ps"], 1)
            pe.wait_ge(s["kv_rb"], 2)
            for b in range(NB):
                last = tr(X[:, b // 4, (b % 4) * 128:(b % 4) * 128 + 128], KC[:, b])
                if b % 4 == 3:
                    last.then_inc(s["kct_ps"], 1)
            pe.wait_ge(s["kdup_ready"], 4)
            pe.wait_ge(s["kv_out_sb"], 2)
            pe.wait_ge(s["kct_sb"], 1)

            def product_and_ada(n, par, unit, loaded):
                pe.wait_ge(s["ad_ev"], unit)
                pe.wait_ge(adl[1], loaded)
                ada_rows(slab[1], AD)
                product_half(n, par, 0)
                ada_select(unit + 1, arow, AD)
                product_half(n, par, 1)

            def pair_of_heads(i, kv):
                n = i * 2 + N_A
                product_and_ada(n, 1, i * 1 + 16, i * 16 + 144)
                pe.wait_ge(s["a_rb"], i * 2 + 1)
                sum_rows(blk64, E).then_inc(s["a_ms"], 1)
                pe.wait_ge(s["a_qn"], i * 1 + 1)
                for e in range(2):
                    r = slice(64 * e, 64 * e + 64)
                    if e == 1:
                        pe.wait_ge(s["a_mxd"], i * 2 + 1)
                    for b in range(4):
                        bank = X[:, b // 2, (b % 2) * 256:(b % 2) * 256 + 256]
                        if b == 0:
                            last = mm(bank[:, 128:256], QN[r, 0:128], kdup[kv][r, 0:128], start=True, stop=True)
                        else:
                            last = mm(bank, QN[r, 128 * b:128 * b + 128], kdup[kv][r, 128 * b - 128:128 * b + 128],
                                      start=True, stop=True)
                    last.then_inc(s["a_sc"], 1)
                    product_half(n + 1, 0, e)
                    pe.wait_ge(s["a_p"], i * 2 + (e + 1))
                    for b in range(4):
                        for f in range(2):
                            if b == 0 and f == 0:
                                continue
                            last = tr(X[:, 2 + b // 2, (b % 2) * 256 + f * 128:(b % 2) * 256 + f * 128 + 128],
                                      S[:, b, f * 128:f * 128 + 128])
                    last.then_inc(s["a_tp"], 1)
                    pe.wait_ge(s["a_ptA"], i * 2 + (e + 1))
                    pe.wait_ge(s["a_ptV"], i * 2 + (e + 1))
                    if e == 0:
                        pe.wait_ge(s["a_gate"], i * 1 + 1)
                    for b in range(4):
                        out = X[r, 4, 128 * b:128 * b + 128]
                        if b > 0:
                            mm(out, vtok[:, b - 1, 64 * kv:64 * kv + 64], PT[:, b, 0], start=True, stop=False)
                        last = mm(out, vtok[:, b, 64 * kv:64 * kv + 64], PT[:, b, 1], start=(b == 0), stop=True)
                    last.then_inc(s["a_pv"], 1)

            for kv in range(2):
                with pe.Fori(4 * kv, 4 * kv + 4) as i:
                    pair_of_heads(i, kv)
            pe.wait_ge(s["a_gate"], 9)
            pe.wait_ge(s["a_qs"], 16)
            for p in range(4):
                for e in range(2):
                    for kv in range(2):
                        b = 2 * p + e
                        r = slice(64 * kv, 64 * kv + 64)
                        rows = slice(64 * e + 32 * kv, 64 * e + 32 * kv + 32)
                        q = qsT[r, b].rearrange("p g t -> p (g t)")
                        at = (p % 2) * 160
                        mm(X[rows, p // 2, at:at + 128], q, KCT[r, b], start=True, stop=True)
                        last = mm(X[rows, p // 2, at + 128:at + 160], q, kdup[kv][r, SEQ:T], start=True, stop=True)
            last.then_inc(s["s_sc"], 1)
            pe.wait_ge(s["s_p"], 1)
            for p in range(4):
                last = tr(X[:, 2, 128 * p:128 * p + 128], SS[:, p, 0:128])
            last.then_inc(s["s_tp"], 1)
            for p in range(4):
                last = tr(X[0:NS, 3, 128 * p:128 * p + 128], SS[:, p, 128:160])
            last.then_inc(s["s_tp"], 1)
            pe.wait_ge(s["s_pt"], 2)
            for b in range(NB):
                for kv in range(2):
                    cols = slice(64 * (b % 2) + 32 * kv, 64 * (b % 2) + 32 * kv + 32)
                    out = X[64 * kv:64 * kv + 64, 4, 32 * b:32 * b + 32]
                    mm(out, VCc[:, b, 64 * kv:64 * kv + 64], PTs[:, b // 2, cols], start=True, stop=False)
                    last = mm(out, vtok_s[0:NS, 64 * kv:64 * kv + 64], PTn[0:NS, b // 2, cols], start=False, stop=True)
            last.then_inc(s["s_pv"], 1)

            pe.wait_ge(s["s_gate"], 1)
            pe.wait_ge(s["vld2"], 16 * 12)
            pe.wait_ge(s["ev"], 6)
            with pe.Fori(0, HB) as h:
                n = h * 6 + N_B

                def product_ada(j):
                    product_and_ada(n + j, (N_B + j) % 2, h * 6 + (24 + j), h * 96 + (272 + 16 * j))

                pe.wait_ge(s["b_wl"], h * 1 + 1)
                for t in range(4):
                    last = mm(X[:, 0, 128 * t:128 * t + 128], LR[0:RANK + 1, 128 * t:128 * t + 128],
                              WLH[0:RANK + 1], start=True, stop=True)
                last.then_inc(s["b_z"], 1)
                mm(X[0:NS, 1, 0:128], LR[0:RANK + 1, SEQ:T], WLH[0:RANK + 1],
                   start=True, stop=True).then_inc(s["b_z"], 1)
                product_ada(0)
                pe.wait_ge(s["b_la"], h * 2 + 2)
                for t in range(4):
                    mm(X[:, 2, 128 * t:128 * t + 128], LAt[:, t], gmask, start=True, stop=True)
                mm(X[:, 3, 0:NS], LAs[0:NS], smask[0:NS, 0:NS], start=True, stop=True).then_inc(s["b_bc"], 1)
                product_ada(1)
                product_ada(2)
                pe.wait_ge(s["b_qk"], h * 2 + 2)
                for t in range(4):
                    mm(X[:, 0, 128 * t:128 * t + 128], BP[:, 1, 128 * t:128 * t + 128], BP[:, 0, 128 * t:128 * t + 128],
                       start=True, stop=True)
                mm(X[0:NS, 1, 0:NS], BP[:, 1, SEQ:T], BP[:, 0, SEQ:T], start=True, stop=True).then_inc(s["b_at"], 1)
                pe.wait_ge(s["b_kd"], h * 1 + 1)
                for t in range(4):
                    tr(X[:, 2, 128 * t:128 * t + 128], T1[:, 128 * t:128 * t + 128])
                tr(X[0:NS, 3, 0:128], T1[:, SEQ:T]).then_inc(s["b_kt"], 1)
                product_ada(3)
                pe.wait_ge(s["ev"], n * 2 + 8)
                pe.wait_ge(s["b_atm"], h * 1 + 1)
                pe.wait_ge(s["b_kta"], h * 2 + 2)
                for t in range(4):
                    for e in range(2):
                        tr(X[:, t // 2, (t % 2) * 256 + 128 * e:(t % 2) * 256 + 128 * e + 128],
                           BP[:, 2 + e, 128 * t:128 * t + 128])
                tr(X[0:NS, 2, 0:128], BP[:, 2, SEQ:T])
                tr(X[0:NS, 2, 128:256], BP[:, 3, SEQ:T]).then_inc(s["b_vt"], 1)
                product_ada(4)
                pe.wait_ge(s["b_vta"], h * 2 + 2)
                for c in range(8):
                    r = slice(64 * (c % 2), 64 * (c % 2) + 64)
                    last = mm(X[:, (c % 2) * 2 + c // 4, (c // 2 % 2) * 256:(c // 2 % 2) * 256 + 256], KDT[r, c // 2], VTB[r, c // 2],
                              start=True, stop=True)
                last.then_inc(s["b_dS"], 1)
                product_ada(5)
                pe.wait_ge(s["b_st"], h * 8 + 8)
                for e in range(2):
                    ec = slice(128 * e, 128 * e + 128)
                    for t in range(4):
                        mm(X[:, e, 128 * t:128 * t + 128], VTB[:, t, ec], AT[:, t], start=True, stop=False)
                        for c in (2 * t, 2 * t + 1):
                            if c > 0:
                                last = mm(X[:, e, 64 * c:64 * c + 64], ST[:, c - 1, ec], BP[:, 0, 64 * c:64 * c + 64],
                                          start=False, stop=(c % 2 == 1))
                    last.then_inc(s["b_o"], 1)
                pe.wait_ge(s["b_sld"], h * 16 + 16)
                for e in range(2):
                    ec = slice(128 * e, 128 * e + 128)
                    mm(X[:, 4, NS * e:NS * e + NS], VTBs[0:NS, ec], ATs[0:NS], start=True, stop=False)
                    for b in range(NB):
                        last = mm(X[:, 4, NS * e + NQ * b:NS * e + NQ * b + NQ], ST[:, b, ec],
                                  BP[:, 0, SEQ + NQ * b:SEQ + NQ * b + NQ], start=False, stop=(b == NB - 1))
                last.then_inc(s["b_so"], 1)
                for b in range(NB):
                    pe.wait_ge(s["b_kdm"], h * 8 + (b + 1))
                    if b >= 2:
                        pe.wait_ge(s["b_sup"], h * 8 + (b - 1))
                    mm(X[:, 2 + b % 2, 0:256], kdm[0:NS, b % 2], VTBs[0:NS], start=True, stop=True).then_inc(s["b_ssb"], 1)
                pe.wait_ge(s["b_sq1"], h * 1 + 1)
                sum_rows(ones[:, :], T1).then_inc(s["b_ms"], 1)
                pe.wait_ge(s["b_gate"], h * 2 + 2)
                pe.wait_ge(s["b_sup"], h * 8 + 8)

            def transposed(r, j):
                pe.wait_ge(s["wy"], r + 33)
                if not (isinstance(r, int) and r == 0):
                    pe.wait_ge(s["wotp"], r * 2)
                for t in range(4):
                    tr(X[:, j, 128 * t:128 * t + 128], yst[:, j, 128 * t:128 * t + 128])
                tr(X[0:NS, 2 + j, 0:128], yst[:, j, SEQ:T]).then_inc(s["wtp"], 1)

            def out_product(w, base, ready):
                p0, p1 = base % 2, (base + 1) % 2
                product(base, p0, ready=ready)
                product(base + 1, p1)
                if w == 2:
                    transposed(0, 0)
                with pe.Fori(1, KT // 2) as m:
                    product(m * 2 + base, p0)
                    if w == 2:
                        transposed(m * 2 - 1, 1)
                    product(m * 2 + (base + 1), p1)
                    if w == 2:
                        transposed(m * 2, 0)
                if w == 2:
                    transposed(KT - 1, 1)

            out_product(0, N_W0, KT)
            pe.wait_ge(s["wssq"], KT)
            sum_rows(ones[:, :], ssum).then_inc(s["ms"], 1)
            pe.wait_ge(s["nls"], 2)
            pe.wait_ge(s["nl"], 3 * KT)
            def head_norm(h):
                pe.wait_ge(s["c_oe"], h * 4 + 2)
                pe.wait_ge(s["c_ssq"], h * 4 + 4)
                sum_rows(ones[:, :], r3, banks=(2, 3)).then_inc(s["c_ms"], 1)

            def sample_outputs(h, b0):
                for b in range(b0, b0 + 4):
                    pe.wait_ge(sld[b % 4], h * 32 + (16 * (b // 4) + 16))
                for kk in range(2):
                    for b in range(b0, b0 + 4):
                        g = 32 * (b % 4)
                        last = mm(X[g:g + 32, 4, :], Qpad[:, kk, b], SB[:, b % 4, kk], start=(b < 4 and kk == 0),
                                  stop=(b >= 4 and kk == 1), tile_position=(0, g))
                return last

            def state_update(h, b):
                pe.wait_ge(s["c_km"], h * 8 + (b + 1))
                for kk in range(2):
                    if b >= 1:
                        pe.wait_ge(s["c_upv"], h * 16 + (2 * b - 1 + kk))
                    mm(X[:, kk, :], KM[:, 128 * kk:128 * kk + 128], VS, start=True, stop=True)\
                        .then_inc(s["c_up"], 1)

            def retention_head(h, first):
                n = h * 12 + N_C
                product(n, N_C % 2)
                product(n + 1, (N_C + 1) % 2)
                if not first:
                    head_norm(h - 1)
                for j in range(2, 6):
                    product(n + j, (N_C + j) % 2)
                pe.wait_ge(s["c_rot"], h * 2 + 2)
                if not first:
                    pe.wait_ge(s["c_rb"], h * 6 - 1)
                for t, out in enumerate((X[:, 0, 0:512], X[:, 1, 0:384], X[:, 2, 0:256], X[:, 1, 384:512])):
                    for kk in range(2):
                        mm(out, R3[:, 2 + kk, 128 * t:128 * t + 128], R3[:, kk, 128 * t:SEQ], start=(kk == 0), stop=(kk == 1))
                for kk in range(2):
                    last = mm(X[0:NS, 2, 256:256 + NS], R3[:, 2 + kk, SEQ:T], R3[:, kk, SEQ:T], start=(kk == 0), stop=(kk == 1))
                last.then_inc(s["c_sc"], 1)
                for t in range(4):
                    for kk in range(2):
                        tr(X[:, 3 + t // 2, (t % 2) * 256 + 128 * kk:(t % 2) * 256 + 128 * kk + 128],
                           R3[:, 2 + kk, 128 * t:128 * t + 128])
                for kk in range(2):
                    last = tr(AD[0:NS, 128 * kk:128 * kk + 128], R3[:, 2 + kk, SEQ:T])
                last.then_inc(s["c_kt"], 1)
                product(n + 6, N_C % 2)
                product(n + 7, (N_C + 1) % 2)
                pe.wait_ge(s["ev"], n * 2 + 16)
                pe.wait_ge(s["c_scv"], h * 3 + 3)
                pe.wait_ge(s["c_kta"], h * 8 + 5)
                for t in range(4):
                    for e in range(4):
                        tr(X[:, t, 128 * e:128 * e + 128], R3[:, 4 + e, 128 * t:128 * t + 128])
                for e in range(4):
                    last = tr(X[0:NS, 4, 128 * e:128 * e + 128], R3[:, 4 + e, SEQ:T])
                last.then_inc(s["c_vt"], 1)
                product(n + 8, N_C % 2)
                pe.wait_ge(s["c_vta"], h * 4 + 4)
                pe.wait_ge(s["c_vtv"], h * 3 + 3)
                for kk in range(2):
                    for t in range(4):
                        last = mm(X[:, kk, :], KTK[:, t, 128 * kk:128 * kk + 128], CT[:, t], start=(t == 0), stop=(t == 3))
                    last.then_inc(s["c_st"], 1)

                def outputs(g):
                    for e in (2 * g, 2 * g + 1):
                        for t in range(4):
                            last = mm(X[:, 2 + e % 2, 128 * t:SEQ], CT[:, t, 128 * e:128 * e + 128],
                                      RAT[:, RAOFF[t]:RAOFF[t] + SEQ - 128 * t], start=(t == 0), stop=(t == 3))
                    last.then_inc(s["c_o"], 1)

                outputs(0)
                sample_outputs(h, 0)
                pe.wait_ge(s["c_stv"], h * 2 + 2)
                product(n + 9, (N_C + 1) % 2, between=[lambda b=b: state_update(h, b) for b in range(4)])
                pe.wait_ge(s["c_oe"], h * 4 + 1)
                outputs(1)
                product(n + 10, N_C % 2)
                sample_outputs(h, 4).then_inc(s["c_o"], 1)
                product(n + 11, (N_C + 1) % 2, between=[lambda b=b: state_update(h, b) for b in range(4, 8)])
                pe.wait_ge(s["c_oe"], h * 4 + 3)
                for e in range(4):
                    mm(AD[:, NS * e:NS * e + NS], CTs[0:NS, 128 * e:128 * e + 128], RATs[0:NS], start=True, stop=False)
                    last = mm(AD[:, NS * e:NS * e + NS], SR[:, 128 * e:128 * e + 128], sel[:, :], start=False, stop=True)
                last.then_inc(s["c_os"], 1)

            retention_head(0, True)
            with pe.Fori(1, HC) as h:
                retention_head(h, False)
            head_norm(HC - 1)
            pe.wait_ge(s["c_upv"], 16 * HC)
            pe.wait_ge(s["c_rb"], 6 * HC - 1)
            out_product(1, N_WA, 3 * KT)
            pe.sem_inc(s["wtp"], 2)
            out_product(2, N_WB, 4 * KT)


_OUTS = [(1, SEQ, D), (NB, NQ, D), (1, 1, WIN, 2, 64), (1, 1, WIN, 2, 64), (1, 1, HB, 128, 256), (1, 1, HC, 256, 512),
         (1, NB, WIN, 2, 64), (1, NB, WIN, 2, 64), (1, NB, HB, 128, 256), (1, NB, HC, 256, 512)]


def kernel(**inputs):
    import concourse.bacc as _bacc
    from concourse.bass_utils import run_bass_kernel_spmd as _run

    nc = _bacc.Bacc("TRN2", target_bir_lowering=False, num_devices=1)
    arrays, ins, consts = {}, {}, {}
    for name in inputs:
        a = np.ascontiguousarray(inputs[name])
        arrays[f"in_{name}"] = a
        ins[name] = nc.dram_tensor(f"in_{name}", a.shape, mybir.dt.from_np(a.dtype), kind="ExternalInput").ap()
    for name, a in shape_constants().items():
        arrays[f"const_{name}"] = a
        consts[name] = nc.dram_tensor(f"const_{name}", a.shape, F32, kind="ExternalInput").ap()
    outs = [nc.dram_tensor(f"out_{i}", shape, F32, kind="ExternalOutput").ap() for i, shape in enumerate(_OUTS)]
    build(nc, ins, outs, consts)
    r = _run(nc, [arrays], core_ids=[0])
    return tuple(r.results[0][f"out_{i}"] for i in range(len(_OUTS)))
```

```python
from contextlib import ExitStack
import math

import numpy as np
import concourse.bass as bass
from concourse import mybir

ALU = mybir.AluOpType
ACT = mybir.ActivationFunctionType
AX = mybir.AxisListType.X
F32 = mybir.dt.float32
F32R = mybir.dt.float32r

D = 2048
KT = D // 128
SEQ, NB, NQ = 512, 8, 4
NS = NB * NQ
T = SEQ + NS
HALF = T // 2
WIN = 128
NEG = -1.0e30
EPS = 1e-6

C_QA, C_KA, C_VA, C_GA = 0, 1024, 1152, 1280
C_QB, C_KB, C_VB, C_GB, C_LR = 2304, 2816, 3328, 4352, 5376
C_QC, C_KC, C_VC, C_GC = 0, 2048, 4096, 8192
HA, HB, HC = 16, 4, 8
RANK = 16

N_KV = 0
N_A = 3
N_B = N_A + 2 * 8
N_W0 = N_B + 6 * HB
N_C = N_W0 + KT
N_WA = N_C + 12 * HC
N_WB = N_WA + KT
N_END = N_WB + KT

RT_W = T + NS + NB + 6


def shape_constants():
    c = {}
    c["ident"] = np.eye(128, dtype=np.float32)
    c["ones"] = np.ones((128, 128), np.float32)
    i = np.arange(128)
    c["blk64"] = (i[:, None] // 64 == i[None, :] // 64).astype(np.float32)
    same = i[:, None] // 64 == i[None, :] // 64
    c["gmask"] = (same & (i[:, None] <= i[None, :])).astype(np.float32)
    j = np.arange(NS)
    sm = (j[:, None] // NQ == j[None, :] // NQ) & (j[:, None] <= j[None, :])
    smask = np.zeros((128, NS + NB), np.float32)
    smask[:NS, :NS] = sm
    smask[:3 * NS, NS:] = np.tile(j[:, None] // NQ == np.arange(NB)[None, :], (3, 1))
    c["smask"] = smask
    dist = 255 - np.arange(384)
    ok = (dist >= 0) & (dist <= WIN)
    dd = np.clip(dist, 0, WIN)
    ratio = np.log(np.maximum(dd, 1).astype(np.float32) / np.float32(16)) / math.log(128 / 16)
    large = np.minimum(16 + (ratio * 16).astype(np.int32), 31)
    bucket = np.where(dd < 16, dd, large)
    hot = np.zeros((33, 384), np.float32)
    hot[bucket[ok], np.nonzero(ok)[0]] = 1.0
    hot[32, ~ok] = NEG
    c["hot"] = hot
    pos = np.concatenate([np.arange(SEQ), 1024 + np.tile(np.arange(NQ), NB)]).astype(np.float32)
    inv = (np.float32(10000.0) ** (-np.arange(128, dtype=np.float32) / np.float32(128))).astype(np.float32)
    ang = (inv[:, None] * pos[None, :]).astype(np.float32).astype(np.float64)
    c["rope"] = np.stack([np.cos(ang), np.sin(ang)], 1).astype(np.float32)
    ret = np.zeros((HC, 128, RT_W), np.float32)
    p = np.arange(128)[:, None].astype(np.float64)
    for h in range(HC):
        lg = math.log1p(-2.0 ** (-5.0 - h))
        dcol = np.arange(SEQ)[None, :] - p
        ret[h, :, :SEQ] = np.where(dcol >= 0, np.exp(np.maximum(dcol, 0) * lg), 0) / 16
        ds = j[None, :] - j[:, None]
        ret[h, :NS, SEQ:T] = np.where(sm, np.exp(np.maximum(ds, 0) * lg), 0) / 16
        ret[h, :, T:T + NS] = np.exp((j % NQ + 1.0) * lg)[None, :]
        ret[h, :3 * NS, T + NS:T + NS + NB] = np.tile(smask[:NS, NS:], (3, 1))
        for t in range(4):
            ret[h, :, T + NS + NB + t] = np.exp((SEQ - 1.0 - 128 * t - p[:, 0]) * lg) / 16
        ret[h, :, T + NS + NB + 4] = math.exp(NQ * lg)
        ret[h, :NS, T + NS + NB + 5] = np.exp((NQ - 1.0 - j % NQ) * lg) / 16
    c["ret"] = ret
    c["sel"] = (i[:, None] % 32 == np.arange(32)[None, :]).astype(np.float32)
    return c


def build(nc, I, O, C):
    ctx = ExitStack()
    with ctx:
        def sb(name, shape, dt=F32):
            return ctx.enter_context(nc.sbuf_tensor(name, shape, dt))

        def sem(name):
            return ctx.enter_context(nc.semaphore(name))

        ds = bass.ds
        ident, ones = sb("ident", [128, 128]), sb("ones", [128, 128])
        vecT = sb("vecT", [128, 128])
        vecT2 = sb("vecT2", [128, 24])
        eps = sb("eps", [128, 8])
        mod = [sb("mod_even", [128, 48, 9]), sb("mod_odd", [128, 48, 9])]
        cs = sb("cs", [128, KT * 9 + 23])
        sel = sb("sel", [128, 32])
        WR = sb("W_raw", [128, 4 * KT * 128])
        WH = sb("W_hi", [128, 2, KT, 128], F32R)
        WL = sb("W_lo", [128, 2, KT, 128], F32R)
        AH = sb("act_hi", [128, KT, T], F32R)
        AL = sb("act_lo", [128, KT, T], F32R)
        R3 = sb("tiles", [128, KT, T])
        U = sb("work", [128, 8424])
        STK = sb("row_stacks", [128, 768], F32R)
        U2 = WR[:, 2 * KT * 128:4 * KT * 128]
        slot = [WR[:, s * 2048:(s + 1) * 2048].rearrange("p (k n) -> p k n", k=KT) for s in range(4)]
        slab = [WR[:, s * 4096:(s + 1) * 4096].rearrange("p (k n) -> p k n", k=KT) for s in range(2)]

        def u(at, *shape, base=None):
            n = int(np.prod(shape))
            v = (U if base is None else base)[:, at:at + n]
            if len(shape) == 2:
                v = v.rearrange("p (a b) -> p a b", a=shape[0])
            elif len(shape) == 3:
                v = v.rearrange("p (a b c) -> p a b c", a=shape[0], b=shape[1])
            return v

        PJ = ctx.enter_context(nc.psum_tensor("PJ", [128, 2, 512], F32))
        AD = ctx.enter_context(nc.psum_tensor("AD", [128, 512], F32))
        X = ctx.enter_context(nc.psum_tensor("X", [128, 5, 512], F32))

        def dram(name, shape):
            return nc.dram_tensor(name, shape, F32).ap()

        res_d = [dram("resid0", (KT, 128, T)), dram("resid1", (KT, 128, T)), dram("resid2", (KT, 128, T))]
        mix_d = dram("mixed_odd", (2 * KT, 128, T))
        rel_d = dram("rel_rows", (HA, 384))
        bias_d = dram("bias_tiles", (HA, 128, 256))

        xs = u(0, 2, 2048)
        ssum, sq, rstd = u(4096, T), u(4640, 2, T), u(5728, T)
        tk, ts, hs = u(6272, 2, 512), u(0, KT, NS), u(512, KT, NS)
        vr, vr2, vc = u(7296, 128), u(7424, 128), u(7552, 128)
        craw, cexp = u(7680, KT, 9), u(7824, KT, 9)
        G = u(7680, KT, 9)
        arow0 = u(6272, 2, 256)
        arow = R3[:, 15, 288:544]
        KC, PT, PTs, PTn = u(0, NB, 128), u(0, 4, 2, 128), u(0, 4, 128), u(512, 4, 128)
        VCc, KCT = u(1024, NB, 128), u(2048, NB, 128)
        kdup = [u(3072, T), u(3616, T)]
        vtok, vtok_s = u(4160, 4, 128), u(4672, 128)
        blk64, LR, smask = u(4800, 128), u(4928, T), u(5472, NS + NB)
        gmask = R3[:, 15, 0:128]
        bmask = smask[:, NS:NS + NB]
        qsT = u(5640, NB, 8, NQ)
        sk, skrow, sk2 = u(5896, 16), u(5912, 1), u(5914, 2)
        mx, nm, den, es, rec = (u(5920 + 4 * n, 4) for n in range(5))
        qg8 = u(5944, 1)
        QT, QN, E = u(5952, T), u(6496, T), u(7040, T)
        tiles8 = R3[:, 8:10].rearrange("p a b -> p (a b)")
        S, SS = (tiles8[:, 0:4 * w].rearrange("p (a b) -> p a b", a=4) for w in (256, 160))
        kn, biasT = R3[:, 8], R3[:, 10, 0:512].rearrange("p (a b) -> p a b", a=2)
        biasS = R3[:, 12:14].rearrange("p a b -> p (a b)")[:, 0:640].rearrange("p (a b) -> p a b", a=4)
        OSm = u(7040, 8, NS)
        relS, relb, hot = R3[:, 11, 0:384], R3[:, 11, 384:400], u(2048, 384)
        BP = u(0, 4, T)
        ST = u(2176, 8, 256)
        LAt, LAs, AT, ATs = u(4224, 4, 128), u(4736, 128), u(4224, 4, 128), u(4736, NS)
        sq1 = u(4224, T)
        WLR = R3[:, 14, 0:512]
        WLH = u(8168, 128)
        EBP, T1, T2 = u(5512, T), u(6056, T), u(6600, T)
        KDT, KDTs = u(5512, 4, 128), u(6600, 128)
        BVS, BKM = STK[0:3 * NS, 0:256], STK[0:3 * NS, 512:768].rearrange("p (a b) -> p a b", a=2)
        BKS = u(6728, 128)[0:3 * NS]
        VTB, VTBs = u(7144, 4, 256), u(8168, 256)
        ebl, blast = u(4864, 16), u(4880, 16)
        rel8 = u(0, 8, T)
        resb, yst, wsq = u(0, 2, T), u(1088, 2, T), u(2176, T)
        smp = u(2720, NS)
        ost = u(2760, 2, 5, 128)
        cos, sin = u(0, T), u(544, T)
        CT, CTs, KTK, KTKs = u(1088, 4, 512), u(3136, 512), u(3648, 4, 256), u(4672, 256)
        RT = u(4928, RT_W)
        r1, r2 = u(5520, T), u(6064, T)
        qi = u(6608, 2, NS)
        CST = u(6672, 2, 512)
        r3 = u(7696, T)
        SB = u(0, 4, 2, 512, base=U2)
        qk_flat = R3[:, 0:4, :].rearrange("p a b -> p (a b)")
        RAT, RATs = qk_flat[:, 0:1280], qk_flat[:, 1280:1280 + NS]
        Qpad = qk_flat[:, 1632:2144].rearrange("p (k b t) -> p k b t", k=2, b=NB)
        VS, KM = STK[0:3 * NS, 0:512], STK[0:3 * NS, 512:768]
        SR = R3[:, 5, 0:512]
        KS = R3[0:3 * NS, 6, 0:256]
        RAOFF = [0, 512, 896, 1152]

        names = ("vld vld2 xT_ready vec_ps vec_sb xa xd sqd ms rb tset sset hi_t nl nls "
                 "ad_done ad_ev hi lo half ev "
                 "c_exp v_chain a_chain res_st "
                 "kv_ps kv_ms kv_rb kn_ready kdup_ready kv_out_sb kv_st kct_ps kct_sb rel_sb "
                 "rel_st bias_ld "
                 "a_ms a_rb a_qn a_qs a_sc a_sadd a_mxd a_exp a_p a_tp a_ptA a_ptV a_pv a_eg a_gate "
                 "bs_ld s_sc s_mx s_exp s_p s_tp s_pt s_pv s_os s_gate swa_st "
                 "b_wl b_z b_ln b_la b_bc b_eb b_dif b_kdx b_qk b_kd b_at b_vt b_vta b_kt b_kta b_atm b_dS b_st "
                 "b_o b_oe b_so b_sld b_stf b_sup b_ssb b_ms b_rb b_eg b_gate b_kdm b_pst b_sq1 "
                 "wy wssq wsqa wtp wotp "
                 "c_tab c_rot c_sc c_scv c_kt c_kta c_vt c_vta c_vtv c_st c_stv c_o c_oe c_os "
                 "c_km c_up c_upv c_ms c_rb c_eg c_gate c_mst c_ssq c_pst m_hi pool_passed act_passed ad_rows ad_sel b_free c_mfree c_pfree ost_free ")
        s = {}
        for n in names.split():
            s[n] = sem(n)
        wld = [sem(f"w_loaded{n}") for n in range(2)]
        adl = [sem(f"ada_tile_loaded{n}") for n in range(2)]
        xld = [sem(f"x_loaded{n}") for n in range(2)]
        rld = [sem(f"resid_loaded{n}") for n in range(2)]
        sld = [sem(f"state_loaded{n}") for n in range(4)]
        sst = [sem(f"state_stored{n}") for n in range(4)]
        yst_s = [sem(f"y_stored{n}") for n in range(2)]
        ost_s = [sem(f"out_stored{n}") for n in range(2)]
        raw = [sem(f"mixed_loaded{n}") for n in range(4)]

        class Chain:

            def __init__(self, eng, sm):
                self.eng, self.sm, self.base, self.total, self.k, self.per = eng, sm, 0, 0, 0, None

            def loop(self, i, per):
                assert self.per is None
                self.total += self.k
                self.base, self.k, self.per = i * per + self.total, 0, per

            def end(self, trips):
                assert self.k == self.per, f"{self.sm}: {self.k} links in the loop, {self.per} declared"
                self.total += self.per * trips
                self.base, self.k, self.per = self.total, 0, None

            def __call__(self, ins):
                self.k += 1
                ins.then_inc(self.sm, 1)
                self.eng.wait_ge(self.sm, self.base + self.k)

        block = ctx.enter_context(nc.Block())

        @block.sync
        def _(sp):
            def load(n, par, src, cols=128):
                if not isinstance(n, int) or n >= 2:
                    sp.wait_ge(s["lo"], n - 1)
                sp.dma_start(slot[par][:, :, 0:cols], src).then_inc(wld[par], 16)

            wie = I["w_in_even"][0].rearrange("(k p) n -> p k n", p=128)
            woe = I["w_out_even"][0].rearrange("(k p) n -> p k n", p=128)
            wio = I["w_in_odd"][0].rearrange("(k p) n -> p k n", p=128)
            woo = I["w_out_odd"][0].rearrange("(k p) n -> p k n", p=128)
            ae = I["ada_w_even"][0].rearrange("(k p) n -> p k n", p=128)
            ao = I["ada_w_odd"][0].rearrange("(k p) n -> p k n", p=128)
            xp = I["x_prompt"][0]
            xsm = I["x_sample"].rearrange("b t d -> (b t) d")
            for t in range(5):
                if t >= 2:
                    sp.wait_ge(s["xT_ready"], 4 * (t - 1))
                if t < 4:
                    sp.dma_start(xs[:, t % 2], xp[t * 128:(t + 1) * 128, :]).then_inc(xld[t % 2], 16)
                else:
                    sp.dma_start(xs[0:NS, 0], xsm).then_inc(xld[0], 16)
                if t == 1:
                    for sl in range(2):
                        sp.dma_start(slab[sl], ae[:, :, sl * 256:(sl + 1) * 256]).then_inc(adl[sl], 16)
            with sp.Fori(1, 8) as i:
                for sl in range(2):
                    sp.wait_ge(s["ad_done"], i * 2 + (sl - 1))
                    sp.dma_start(slab[sl], ae[:, :, ds(i * 512 + sl * 256, 256)]).then_inc(adl[sl], 16)
            sp.wait_ge(s["ad_done"], 15)
            load(0, 0, wie[:, :, C_KA:C_KA + 128])
            load(1, 1, wie[:, :, C_VA:C_VA + 128])
            load(2, 0, wie[:, :, C_LR:C_LR + RANK], RANK)

            def ada_pair(unit, w, col):
                sp.wait_ge(s["ad_done"], unit)
                sp.dma_start(slab[1], w[:, :, ds(col, 256)]).then_inc(adl[1], 16)

            with sp.Fori(0, 8) as i:
                load(i * 2 + N_A, N_A % 2, wie[:, :, ds(i * 128 + C_QA, 128)])
                ada_pair(i * 1 + 16, ae, i * 256 + 4096)
                load(i * 2 + (N_A + 1), (N_A + 1) % 2, wie[:, :, ds(i * 128 + C_GA, 128)])
            with sp.Fori(0, HB) as h:
                src = (ds(h * 128 + C_QB, 128), ds(h * 128 + C_KB, 128), ds(h * 256 + C_VB, 128),
                       ds(h * 256 + (C_VB + 128), 128), ds(h * 256 + C_GB, 128), ds(h * 256 + (C_GB + 128), 128))
                for j in range(6):
                    load(h * 6 + (N_B + j), (N_B + j) % 2, wie[:, :, src[j]])
                    ada_pair(h * 6 + (24 + j), ao, h * 1536 + 256 * j)

            def out_product(base, w):
                with sp.Fori(0, KT // 2) as m:
                    for j in range(2):
                        load(m * 2 + (base + j), (base + j) % 2, w[:, :, ds(m * 256 + 128 * j, 128)])

            out_product(N_W0, woe)
            with sp.Fori(0, HC) as h:
                src = [ds(h * 256 + (c + 128 * e), 128) for c in (C_QC, C_KC) for e in range(2)] + \
                    [ds(h * 512 + (c + 128 * e), 128) for c in (C_VC, C_GC) for e in range(4)]
                for j in range(12):
                    load(h * 12 + (N_C + j), (N_C + j) % 2, wio[:, :, src[j]])
            out_product(N_WA, woo[:, 0:KT, :])
            out_product(N_WB, woo[:, KT:2 * KT, :])

        @block.gpsimd
        def _(pool):
            def wait_for(sm, value, tell="pool_passed"):
                pool.wait_ge(sm, value)
                pool.sem_inc(s[tell], 1)

            pool.sem_inc(s["b_free"], 1)
            pool.sem_inc(s["c_mfree"], 1)
            pool.sem_inc(s["c_pfree"], 1)
            pool.sem_inc(s["ost_free"], 2)
            for dst, src in ((ident[:, :], C["ident"]), (ones[:, :], C["ones"]), (sel[:, :], C["sel"])):
                pool.dma_start(dst, src).then_inc(s["vld"], 16)
            be, bo = (I[k][0].rearrange("(r c) -> r c", c=128) for k in ("ada_b_even", "ada_b_odd"))
            ge, go = (I[k][0].rearrange("(r c) -> r c", c=128) for k in ("norm_g_even", "norm_g_odd"))
            for a, b, src in ((0, 48, be), (48, 96, bo), (96, 112, ge), (112, 128, go)):
                pool.dma_start(vr[a:b, :], src).then_inc(s["vld"], 16)
            for a, b, src in ((0, 16, I["c_prompt"][0].rearrange("(r c) -> r c", c=128)),
                              (16, 18, I["gla_g_even"][0].rearrange("(r c) -> r c", c=128)),
                              (18, 22, I["ret_g_odd"][0].rearrange("(r c) -> r c", c=128))):
                pool.dma_start(vr2[a:b, :], src).then_inc(s["vld"], 16)
            for e in range(2):
                pool.dma_start(vr2[22:23, 64 * e:64 * e + 64], I["qn_g_even"]).then_inc(s["vld"], 16)
                pool.dma_start(vr2[23:24, 64 * e:64 * e + 64], I["kn_g_even"]).then_inc(s["vld"], 16)
            pool.dma_start(vc[:, :], I["c_sample"].rearrange("b (r c) -> (b r) c", c=128)).then_inc(s["vld"], 16)
            pool.wait_ge(s["xa"], 10)
            pool.wait_ge(s["xd"], 10)
            pool.dma_start(res_d[0].rearrange("k p t -> p k t"), R3[:, :, :]).then_inc(s["res_st"], 16)
            pool.wait_ge(s["res_st"], 16)
            pool.wait_ge(s["nl"], KT)
            pool.wait_ge(s["nls"], 1)
            kc = I["cache_swa_k"][0].rearrange("b s k d -> s b (k d)")
            vcc = I["cache_swa_v"][0].rearrange("b s k d -> s b (k d)")
            pool.dma_start(KC, kc).then_inc(s["vld2"], 16)
            pool.dma_start(VCc, vcc).then_inc(s["vld2"], 16)
            pool.dma_start(blk64, C["blk64"]).then_inc(s["vld2"], 16)
            pool.dma_start(gmask, C["gmask"]).then_inc(s["vld2"], 16)
            pool.dma_start(smask, C["smask"]).then_inc(s["vld2"], 16)
            pool.dma_start(hot[0:33], C["hot"]).then_inc(s["vld2"], 16)
            pool.dma_start(relb[0:32], I["rel_bias"]).then_inc(s["vld2"], 16)
            sinks = I["sinks_even"]
            pool.dma_start(sk[:, :], bass.AP(sinks.tensor, 0, [[0, 128], [1, HA]])).then_inc(s["vld2"], 16)
            with nc.allow_non_contiguous_dma(reason="one sink per row"):
                for e in range(2):
                    pool.dma_start(skrow[64 * e:64 * e + 64, :],
                                   bass.AP(sinks.tensor, 0, [[1, HA], [0, NQ], [1, 1]])).then_inc(s["vld2"], 16)
            pool.dma_start(WLR[0:RANK], I["w_lr_even"][0]).then_inc(s["vld2"], 16)
            pool.dma_start(WLR[RANK:RANK + 1], I["b_lr_even"]).then_inc(s["vld2"], 16)
            for k, src in ((6, I["cache_swa_k"]), (7, I["cache_swa_v"])):
                pool.dma_start(O[k][0][:, 0:WIN - NQ], src[0][:, NQ:WIN]).then_inc(s["swa_st"], 16)
            pool.wait_ge(s["rel_sb"], 1)
            pool.dma_start(rel_d, relS[0:HA, :]).then_inc(s["rel_st"], 16)
            pool.wait_ge(s["rel_st"], 16)
            pool.dma_start(bias_d, bass.AP(rel_d.tensor, 127, [[384, HA], [-1, 128], [1, 256]])).then_inc(s["rel_st"], 16)
            pool.wait_ge(s["kv_out_sb"], 2)
            pool.dma_start(O[2][0, 0].rearrange("s k d -> s (k d)"), E[:, 0:128]).then_inc(s["kv_st"], 16)
            pool.dma_start(O[6][0][:, WIN - NQ:WIN].rearrange("b t k d -> b t (k d)"), E[0:NS, 128:256]).then_inc(s["kv_st"], 16)
            pool.dma_start(O[3][0, 0].rearrange("s k d -> s (k d)"), vtok[:, 3]).then_inc(s["kv_st"], 16)
            pool.dma_start(O[7][0][:, WIN - NQ:WIN].rearrange("b t k d -> b t (k d)"), vtok_s[0:NS]).then_inc(s["kv_st"], 16)
            pool.wait_ge(s["rel_st"], 32)
            pool.wait_ge(s["kv_st"], 64)

            def load_bias(i):
                pool.dma_start(biasT, bias_d[ds(i * 2, 2)].rearrange("h i s -> i h s")).then_inc(s["bias_ld"], 16)

            load_bias(0)
            pool.wait_ge(s["bs_ld"], 1)
            with nc.allow_non_contiguous_dma(reason="small bias rows"):
                for e in range(2):
                    for p in range(4):
                        r = slice(64 * e, 64 * e + 64)
                        pool.dma_start(biasS[r, p, 0:128],
                                       bass.AP(rel_d.tensor, 127, [[384, HA], [-1, NQ], [1, 128]])).then_inc(s["rel_st"], 16)
                        b = 2 * p + e
                        pool.dma_start(biasS[r, p, 128 + NQ * b:128 + NQ * b + NQ],
                                       bass.AP(rel_d.tensor, 255, [[384, HA], [-1, NQ], [1, NQ]])).then_inc(s["rel_st"], 16)
            with pool.Fori(1, 8) as i:
                wait_for(s["a_sadd"], i * 2)
                load_bias(i)
            with pool.Fori(0, HB) as h:
                wait_for(s["b_st"], h * 8 + 8)
                pool.dma_start(O[4][0, 0, ds(h, 1)].rearrange("h p e -> p (h e)"), ST[:, 7]).then_inc(s["b_pst"], 16)
                wait_for(s["b_pst"], h * 16 + 16)
                wait_for(s["b_o"], h * 2 + 2)
                pool.dma_start(ST, I["state_gla"][0][:, ds(h, 1)].rearrange("b h p e -> p (b h) e")).then_inc(s["b_sld"], 16)
                wait_for(s["b_sup"], h * 8 + 8)
                pool.dma_start(O[8][0][:, ds(h, 1)].rearrange("b h p e -> p (b h) e"), ST).then_inc(s["b_stf"], 16)
                wait_for(s["b_stf"], h * 16 + 16, "b_free")

            def reload(w, q):
                pool.dma_start(R3[:, 4 * q:4 * q + 4] if w or q < 2 else rel8[:, 4 * q - 8:4 * q - 4],
                               mix_d[KT * w + 4 * q:KT * w + 4 * q + 4].rearrange("k p t -> p k t")).then_inc(raw[q], 16)

            def out_product(w, src, dst):
                def load(m, j):
                    pool.dma_start(resb[:, j], src[ds(m * 2 + j, 1)].rearrange("k p t -> p (k t)")).then_inc(rld[j], 16)

                def store(m, j):
                    if w < 2:
                        wait_for(s["wy"], m * 2 + (16 * w + j + 1))
                        y = R3[:, ds(m * 2 + j, 1), :].rearrange("p k t -> p (k t)") if w == 0 else yst[:, j]
                        pool.dma_start(dst[ds(m * 2 + j, 1)].rearrange("k p t -> p (k t)"), y).then_inc(yst_s[j], 16)
                    else:
                        wait_for(s["wotp"], m * 4 + (2 * j + 2))
                        pool.dma_start(O[0][0].rearrange("(t p) n -> p t n", p=128)[:, :, ds(m * 256 + 128 * j, 128)],
                                       ost[:, j, 0:4]).then_inc(ost_s[j], 16)
                        pool.dma_start(O[1].rearrange("b t n -> (b t) n")[:, ds(m * 256 + 128 * j, 128)],
                                       ost[0:NS, j, 4]).then_inc(ost_s[j], 16)
                        wait_for(ost_s[j], m * 32 + 32, "ost_free")

                if w == 1:
                    pool.wait_ge(s["nl"], 4 * KT)
                load(0, 0)
                load(0, 1)

                def steps(m):
                    for j in range(2):
                        wait_for(s["wy"], m * 2 + (16 * w + j + 1))
                        load(m + 1, j)
                        store(m, j)

                start = 0
                if w == 1:
                    start = 3
                    for m in range(start):
                        steps(m)
                    store_mixed(HC - 1)
                    for q in range(4):
                        reload(1, q)
                with pool.Fori(start, KT // 2 - 1) as m:
                    steps(m)
                for j in range(2):
                    store(KT // 2 - 1, j)

            pool.wait_ge(s["b_gate"], 2 * HB)
            pool.wait_ge(s["nl"], 2 * KT)
            pool.wait_ge(s["res_st"], 16)
            out_product(0, res_d[0], res_d[1])
            pool.wait_ge(s["nl"], 3 * KT)
            pool.wait_ge(s["nls"], 2)

            def load_table(h):
                pool.dma_start(RT, C["ret"][ds(h, 1)].rearrange("h p w -> p (h w)")).then_inc(s["c_tab"], 16)

            load_table(0)
            pool.dma_start(u(0, 2 * T), C["rope"].rearrange("p a t -> p (a t)")).then_inc(s["c_tab"], 16)

            def load_state(h, b):
                pool.dma_start(SB[:, b % 4], I["state_ret"][0][b, ds(h, 1)].rearrange(
                    "h (k p) e -> p (h k) e", p=128)).then_inc(sld[b % 4], 16)

            def store_state(h, b):
                wait_for(s["c_upv"], h * 16 + (2 * b + 2))
                pool.dma_start(O[9][0][b, ds(h, 1)].rearrange("h (k p) e -> p (h k) e", p=128),
                               SB[:, b % 4]).then_inc(sst[b % 4], 16)

            def store_mixed(h):
                for e in range(4):
                    wait_for(s["c_gate"], h * 4 + (e + 1))
                    pool.dma_start(mix_d[ds(h * 4 + e, 1)].rearrange("k p t -> p (k t)"), R3[:, 12 + e]).then_inc(s["c_mst"], 16)
                wait_for(s["c_mst"], h * 64 + 64, "c_mfree")

            def head_transfers(h, first, last):
                if not first:
                    store_mixed(h - 1)
                for kk in range(2):
                    wait_for(s["c_stv"], h * 2 + (kk + 1))
                    pool.dma_start(O[5][0, 0, ds(h, 1), 128 * kk:128 * kk + 128].rearrange("h p e -> p (h e)"),
                                   CST[:, kk]).then_inc(s["c_pst"], 16)
                for b in range(4):
                    store_state(h, b)
                for b in range(4):
                    wait_for(sst[b], h * 32 + 16)
                    load_state(h, b + 4)
                wait_for(s["c_pst"], h * 32 + 32, "c_pfree")
                for b in range(4, NB):
                    store_state(h, b)
                for b in range(4):
                    wait_for(sst[b], h * 32 + 32)
                    if not last:
                        load_state(h + 1, b)
                if not last:
                    load_table(h + 1)

            for b in range(4):
                load_state(0, b)
            head_transfers(0, True, False)
            with pool.Fori(1, HC - 1) as h:
                head_transfers(h, False, False)
            head_transfers(HC - 1, False, True)
            pool.wait_ge(s["c_os"], HC)
            pool.wait_ge(s["c_km"], NB * HC)
            for q in range(4):
                reload(0, q)
            out_product(1, res_d[1], res_d[2])
            for j in range(2):
                pool.wait_ge(yst_s[j], 16 * 16)
            out_product(2, res_d[2], None)
            for j in range(2):
                pool.wait_ge(ost_s[j], 32 * 8)
            for b in range(4):
                pool.wait_ge(sst[b], 32 * HC)
            pool.wait_ge(s["b_pst"], 16 * HB)
            pool.wait_ge(s["b_stf"], 16 * HB)
            pool.wait_ge(s["swa_st"], 32)
            pool.wait_ge(s["kv_st"], 64)
            pool.wait_ge(s["c_pst"], 32 * HC)
            pool.wait_ge(s["c_tab"], 16 * HC + 16)
            pool.wait_ge(s["res_st"], 16)

        @block.scalar
        def _(act):
            link = Chain(act, s["a_chain"])
            A = nc.scalar.activation

            def wait_for(sm, value):
                act.wait_ge(sm, value)
                act.sem_inc(s["act_passed"], 1)

            def split_hi(n, par):
                if isinstance(n, int) and n >= N_END:
                    return
                act.wait_ge(wld[par], (n - par) * 8 + 16)
                if not (isinstance(n, int) and n < 2):
                    act.wait_ge(s["half"], n * 2 - 2)
                A(WH[:, par], slot[par], ACT.Copy).then_inc(s["hi"], 1)

            def evac(n, c, dst):
                (act.wait_ge if isinstance(n, int) else wait_for)(s["half"], n * 2 + (c + 1))
                return A(dst, PJ[:, c, 0:HALF], ACT.Copy).then_inc(s["ev"], 1)

            def halves(v):
                return v.rearrange("p (c t) -> p c t", c=2)

            def rsqrt_mean(dst, n):
                link(A(halves(dst), X[:, 0:2, 0:HALF], ACT.Ln, bias=eps[:, 0:1], scale=1.0 / n))
                return A(dst, dst, ACT.Exp, scale=-0.5)

            def sigmoid(dst, src):
                link(A(dst, src, ACT.Exp, scale=-1.0))
                link(A(dst, dst, ACT.Ln, bias=1.0))
                return A(dst, dst, ACT.Exp, scale=-1.0)

            act.wait_ge(s["vec_sb"], 1)
            A(cexp, craw, ACT.Exp, scale=-1.0).then_inc(s["c_exp"], 1)
            for t in range(5):
                w = 128 if t < 4 else NS
                for q in (0, 2):
                    act.wait_ge(s["xT_ready"], 4 * t + q + 1)
                    A(R3[:, 4 * q:4 * q + 4, t * 128:t * 128 + w], X[:, q, 0:4 * w].rearrange("p (a b) -> p a b", a=4),
                      ACT.Copy).then_inc(s["xa"], 1)
            act.wait_ge(s["xa"], 10)
            act.wait_ge(s["xd"], 10)
            for k in range(KT):
                if k >= 2:
                    act.wait_ge(s["sqd"], k)
                A(sq[:, k % 2], R3[:, k], ACT.Square).then_inc(s["xa"], 1)
                act.wait_ge(s["ad_done"], k + 1)
                if k >= 2:
                    act.wait_ge(s["ad_sel"], k - 1)
                A(arow0[:, k % 2], AD[:, 0:256] if k % 2 == 0 else X[:, 4, 0:256], ACT.Copy).then_inc(s["ad_rows"], 1)

            def ada_rows(unit):
                act.wait_ge(s["ad_done"], unit)
                A(arow, AD[:, 0:256], ACT.Copy).then_inc(s["ad_rows"], 1)


            def norm(l):
                act.wait_ge(s["ms"], l + 1)
                rsqrt_mean(rstd, D).then_inc(s["rb"], 1)
                for k in range(KT):
                    act.wait_ge(s["tset"], KT * l + k + 1)
                    A(AH[:, k, 0:SEQ], tk[:, k % 2], ACT.Identity, bias=mod[l][:, k, 0:1]).then_inc(s["hi_t"], 1)
                    if k == 0:
                        act.wait_ge(s["sset"], l + 1)
                        A(AH[:, :, SEQ:T], hs, ACT.Copy).then_inc(s["hi_t"], 1)

            split_hi(0, 0)
            split_hi(1, 1)
            norm(0)
            for c in range(2):
                evac(0, c, QT[:, c * HALF:(c + 1) * HALF])
            split_hi(2, 0)
            act.wait_ge(s["ev"], 2)
            A(E, QT, ACT.Square).then_inc(s["kv_rb"], 1)
            for c in range(2):
                evac(1, c, QN[:, c * HALF:(c + 1) * HALF])
            split_hi(3, 1)
            act.wait_ge(s["kv_ms"], 1)
            rsqrt_mean(E, 64).then_inc(s["kv_rb"], 1)
            act.wait_ge(s["kn_ready"], 2)
            for kv in range(2):
                for e in range(2):
                    A(kdup[kv][64 * e:64 * e + 64], kn[64 * kv:64 * kv + 64], ACT.Copy).then_inc(s["kdup_ready"], 1)
            act.wait_ge(s["kct_ps"], 2)
            A(KCT, X[:, 0:2, :].rearrange("p a (b c) -> p (a b) c", c=128), ACT.Copy).then_inc(s["kct_sb"], 1)
            for c in range(2):
                act.wait_ge(s["half"], 5 + c)
                A(LR[0:RANK, c * HALF:(c + 1) * HALF], PJ[0:RANK, c, 0:HALF], ACT.Copy).then_inc(s["ev"], 1)

            def probs_copied(i, e):
                act.wait_ge(s["a_tp"], i * 2 + (e + 1))
                A(PT[:, 2:4].rearrange("p b h q -> p (b h q)"), X[:, 3, :], ACT.Copy).then_inc(s["a_ptA"], 1)

            def pair_of_heads(i, kv, i0, first=False):
                n = i * 2 + N_A
                split_hi(n + 1, 0)
                ada_rows(i * 1 + 17)
                evac(n, 0, QT[:, 0:HALF])
                if not first:
                    probs_copied(i - 1, 1)
                evac(n, 1, QT[:, HALF:T])
                act.wait_ge(s["ev"], n * 2 + 2)
                act.wait_ge(s["a_gate"], i * 1 + 1)
                A(E, QT, ACT.Square).then_inc(s["a_rb"], 1)
                split_hi(n + 2, 1)
                act.wait_ge(s["a_ms"], i * 1 + 1)
                rsqrt_mean(E, 64).then_inc(s["a_rb"], 1)
                gate = R3[:, i:i + 1] if isinstance(i, int) else R3[:, ds(i, 1)]
                gate = gate.rearrange("p a t -> p (a t)")
                evac(n + 1, 0, gate[:, 0:HALF])
                wait_for(s["a_qn"], i * 1 + 1)
                for e in range(2):
                    g = i * 2 + (e - 2 * i0)
                    q = qsT[64 * kv:64 * kv + 64, :, g:g + 1, :] if isinstance(i, int) else qsT[64 * kv:64 * kv + 64, :, ds(g, 1), :]
                    A(q.rearrange("p b g t -> p b (g t)"),
                      QN[64 * e:64 * e + 64, SEQ:T].rearrange("p (b t) -> p b t", t=NQ), ACT.Copy).then_inc(s["a_qs"], 1)
                for e in range(2):
                    act.wait_ge(s["a_mxd"], i * 2 + (e + 1))
                    for b in range(4):
                        A(S[:, b], S[:, b], ACT.Exp, bias=nm[:, b:b + 1], accum_out=den[:, b:b + 1]).then_inc(s["a_exp"], 1)
                    A(es, nm, ACT.Exp, bias=sk2[:, e:e + 1]).then_inc(s["a_exp"], 1)
                    if e == 0:
                        evac(n + 1, 1, gate[:, HALF:T])
                        probs_copied(i, 0)
                wait_for(s["ev"], n * 2 + 4)
                sigmoid(E, gate).then_inc(s["a_eg"], 1)

            act.wait_ge(s["kv_st"], 64)
            for kv in range(2):
                pair_of_heads(4 * kv, kv, 4 * kv, first=(kv == 0))
                with act.Fori(4 * kv + 1, 4 * kv + 4) as i:
                    link.loop(i - (4 * kv + 1), 3)
                    pair_of_heads(i, kv, 4 * kv)
                    link.end(3)
            probs_copied(7, 1)
            act.wait_ge(s["s_mx"], 1)
            for p in range(4):
                A(SS[:, p], SS[:, p], ACT.Exp, bias=nm[:, p:p + 1], accum_out=den[:, p:p + 1]).then_inc(s["s_exp"], 1)
            A(es, nm, ACT.Exp, bias=skrow).then_inc(s["s_exp"], 1)
            act.wait_ge(s["s_tp"], 2)
            A(PTs.rearrange("p a b -> p (a b)"), X[:, 2, :], ACT.Copy).then_inc(s["s_pt"], 1)
            A(PTn[0:NS].rearrange("p a b -> p (a b)"), X[0:NS, 3, :], ACT.Copy).then_inc(s["s_pt"], 1)
            act.wait_ge(s["s_pv"], 1)
            for kv in range(2):
                for e in range(2):
                    for b in range(NB):
                        A(OSm[64 * e:64 * e + 64, 4 * kv:4 * kv + 4, NQ * b:NQ * b + NQ],
                          X[64 * kv:64 * kv + 64, 4, 32 * b:32 * b + 32].rearrange("p (g u t) -> p g u t", u=2, t=NQ)[:, :, e],
                          ACT.Copy).then_inc(s["s_os"], 1)

            def gla_sigmoid(h, e):
                wait_for(s["ev"], h * 12 + (2 * N_B + 12))
                if e == 1:
                    wait_for(s["b_gate"], h * 2 + 1)
                sigmoid(sq1, R3[:, ds(h * 2 + (8 + e), 1), :].rearrange("p a t -> p (a t)")).then_inc(s["b_eg"], 1)


            def gla_head(h, first):
                n = h * 6 + N_B
                if not first:
                    gla_sigmoid(h - 1, 0)
                    ada_rows(h * 6 + 25)
                    gla_sigmoid(h - 1, 1)
                    act.wait_ge(s["b_gate"], h * 2)
                act.wait_ge(s["b_z"], h * 2 + 2)
                link(A(T1[:, 0:SEQ], X[:, 0, :], ACT.Abs))
                link(A(T2[0:NS, 0:128], X[0:NS, 1, 0:128], ACT.Abs))
                link(A(T1[:, 0:SEQ], T1[:, 0:SEQ], ACT.Exp, scale=-1.0))
                link(A(T2[0:NS, 0:128], T2[0:NS, 0:128], ACT.Exp, scale=-1.0))
                A(T1[:, 0:SEQ], T1[:, 0:SEQ], ACT.Ln, bias=1.0).then_inc(s["b_ln"], 1)
                A(T2[0:NS, 0:128], T2[0:NS, 0:128], ACT.Ln, bias=1.0).then_inc(s["b_ln"], 1)
                split_hi(n + 1, 0)
                if first:
                    ada_rows(h * 6 + 25)
                for j in range(4):
                    if j > 0:
                        ada_rows(h * 6 + (25 + j))
                    for c in range(2):
                        evac(n + j, c, BP[:, j, c * HALF:(c + 1) * HALF])
                    split_hi(n + j + 2, (j + 1) % 2)
                    if j == 0:
                        act.wait_ge(s["b_bc"], h * 1 + 1)
                        A(EBP[:, 0:SEQ], X[:, 2, :], ACT.Exp, scale=1.0 / 16).then_inc(s["b_eb"], 1)
                        A(EBP[:, SEQ:T], X[:, 3, 0:NS], ACT.Exp, scale=1.0 / 16).then_inc(s["b_eb"], 1)
                        A(T2[:, 0:SEQ], X[:, 2, :], ACT.Exp, scale=-1.0 / 16).then_inc(s["b_eb"], 1)
                        A(T2[:, SEQ:T], X[:, 3, 0:NS], ACT.Exp, scale=-1.0 / 16).then_inc(s["b_eb"], 1)
                        act.wait_ge(s["b_dif"], h * 1 + 1)
                        A(T1, T1, ACT.Exp, scale=1.0 / 16).then_inc(s["b_kdx"], 1)
                    if j == 2:
                        act.wait_ge(s["b_kt"], h * 1 + 1)
                        A(KDT.rearrange("p a b -> p (a b)"), X[:, 2, :], ACT.Copy).then_inc(s["b_kta"], 1)
                        for rows in (KDTs[0:NS], BKS[0:NS], BKS[NS:2 * NS], BKM[0:NS, 0]):
                            A(rows, X[0:NS, 3, 0:128], ACT.Copy).then_inc(s["b_kta"], 1)
                act.wait_ge(s["b_vt"], h * 1 + 1)
                A(VTB.rearrange("p (x a) e -> p x (a e)", x=2), X[:, 0:2, :], ACT.Copy).then_inc(s["b_vta"], 1)
                for rows in (VTBs[0:NS], BVS[0:NS], BVS[2 * NS:3 * NS]):
                    A(rows, X[0:NS, 2, 0:256], ACT.Copy).then_inc(s["b_vta"], 1)
                for j in range(4, 6):
                    ada_rows(h * 6 + (25 + j))
                    for c in range(2):
                        evac(n + j, c, R3[:, ds(h * 2 + (4 + j), 1), c * HALF:(c + 1) * HALF].rearrange("p a t -> p (a t)"))
                    if j < 5:
                        split_hi(n + j + 2, (j + 1) % 2)
                act.wait_ge(s["b_o"], h * 2 + 2)
                A(BP[:, 2:4, 0:SEQ], X[:, 0:2, :], ACT.Copy).then_inc(s["b_oe"], 1)
                act.wait_ge(s["b_so"], h * 1 + 1)
                A(BP[:, 2:4, SEQ:T], X[:, 4, 0:2 * NS].rearrange("p (e t) -> p e t", e=2), ACT.Copy).then_inc(s["b_oe"], 1)
                act.wait_ge(s["b_oe"], h * 2 + 2)
                A(T1, BP[:, 2], ACT.Square).then_inc(s["b_rb"], 1)
                A(sq1, BP[:, 3], ACT.Square).then_inc(s["b_rb"], 1)
                act.wait_ge(s["b_ms"], h * 1 + 1)
                rsqrt_mean(T1, 256).then_inc(s["b_rb"], 1)

            gla_head(0, True)
            with act.Fori(1, HB) as h:
                link.loop(h - 1, 9)
                gla_head(h, False)
                link.end(HB - 1)

            def out_product(w, base):
                def rows_out(r, j):
                    act.wait_ge(s["wtp"], r + 3)
                    act.wait_ge(s["ost_free"], r + 1)
                    A(ost[:, j, 0:4].rearrange("p a b -> p (a b)"), X[:, j, :], ACT.Copy).then_inc(s["wotp"], 1)
                    A(ost[0:NS, j, 4], X[0:NS, 2 + j, 0:128], ACT.Copy).then_inc(s["wotp"], 1)

                def tiles(m, first=False, last=False):
                    for j in range(2):
                        if not (last and j == 1):
                            split_hi(m * 2 + (base + j + 1), (base + j + 1) % 2)
                        if w == 2 and not (first and j == 0):
                            rows_out(m * 2 + (j - 1), 1 - j)
                        if w == 1 and first:
                            if j == 0:
                                squares(HC - 1)
                            else:
                                head_rstd(HC - 1)
                                for e in range(4):
                                    head_sigmoid(HC - 1, e)
                        if w == 0:
                            wait_for(s["wy"], m * 2 + (j + 1))
                            A(wsq, R3[:, ds(m * 2 + j, 1), :].rearrange("p a t -> p (a t)"), ACT.Square).then_inc(s["wsqa"], 1)
                            act.wait_ge(s["wssq"], m * 2 + (j + 1))

                tiles(0, first=True)
                with act.Fori(1, KT // 2 - 1) as m:
                    tiles(m)
                tiles(KT // 2 - 1, last=(w == 2))
                if w == 2:
                    rows_out(KT - 1, 1)

            def split_mixed(w):
                for k in range(KT):
                    if w > 0:
                        act.wait_ge(raw[k // 4], 16 * w)
                    if w > 0:
                        act.wait_ge(s["half"], 2 * (N_WA + KT * (w - 1)))
                    if w == 0:
                        if k in (0, 7):
                            gla_sigmoid(HB - 1, k // 7)
                        act.wait_ge(s["b_gate"], 2 * HB - 2 + (2 if k >= KT - 2 else 0))
                        act.wait_ge(s["s_gate"], 1)
                    A(AH[:, k], rel8[:, k - 8] if w == 1 and k >= 8 else R3[:, k], ACT.Copy).then_inc(s["m_hi"], 1)

            split_mixed(0)
            out_product(0, N_W0)
            norm(1)
            def squares(h):
                act.wait_ge(s["c_os"], h * 1 + 1)
                A(R3[:, 12:16, SEQ:T], AD[:, 0:4 * NS].rearrange("p (e t) -> p e t", e=4), ACT.Copy).then_inc(s["c_oe"], 1)
                act.wait_ge(s["c_oe"], h * 4 + 4)
                for e in range(4):
                    if e >= 2:
                        act.wait_ge(s["c_ssq"], h * 4 + (e - 1))
                    A((r1, r2)[e % 2], R3[:, 12 + e], ACT.Square).then_inc(s["c_rb"], 1)

            def head_rstd(h):
                act.wait_ge(s["c_ms"], h * 1 + 1)
                A(halves(r1), X[:, 2:4, 0:HALF], ACT.Ln, bias=eps[:, 0:1], scale=1.0 / 512).then_inc(s["c_rb"], 1)
                act.wait_ge(s["c_rb"], h * 6 + 5)
                A(r1, r1, ACT.Exp, scale=-0.5).then_inc(s["c_rb"], 1)

            def head_sigmoid(h, e):
                act.wait_ge(s["ev"], h * 24 + (2 * N_C + 24))
                if e >= 1:
                    act.wait_ge(s["c_gate"], h * 4 + e)
                sigmoid(r2, R3[:, 8 + e]).then_inc(s["c_eg"], 1)

            def retention_head(h, first):
                n = h * 12 + N_C
                for j in range(12):
                    split_hi(n + (j + 1), (N_C + j + 1) % 2)
                    if j == 2 and not first:
                        head_rstd(h - 1)
                    if j in (2, 3) and not first:
                        head_sigmoid(h - 1, 2 * j - 4)
                    if j == 6:
                        act.wait_ge(s["c_tab"], h * 16 + 32)
                        act.wait_ge(s["c_kt"], h * 1 + 1)
                        for t in range(4):
                            A(KTK[:, t], X[:, 3 + t // 2, (t % 2) * 256:(t % 2) * 256 + 256], ACT.Copy,
                              scale=RT[:, T + NS + NB + t:T + NS + NB + t + 1]).then_inc(s["c_kta"], 1)
                        A(KTKs[0:NS], AD[0:NS, 0:256], ACT.Copy,
                          scale=RT[0:NS, T + NS + NB + 5:T + NS + NB + 6]).then_inc(s["c_kta"], 1)
                    if j == 8:
                        act.wait_ge(s["c_vt"], h * 1 + 1)
                        A(CT[:, 0:2], X[:, 0:2, :], ACT.Copy).then_inc(s["c_vta"], 1)
                        A(CTs[0:NS], X[0:NS, 4, :], ACT.Copy).then_inc(s["c_vta"], 1)
                        act.wait_ge(s["c_vta"], h * 4 + 2)
                        act.wait_ge(s["c_kta"], h * 8 + 5)
                        for g in (0, 2):
                            A(VS[NS * g:NS * g + NS], CTs[0:NS], ACT.Copy).then_inc(s["c_vta"], 1)
                        for g in (0, 1):
                            A(KS[NS * g:NS * g + NS], KTKs[0:NS], ACT.Copy).then_inc(s["c_kta"], 1)
                        A(KM[0:NS], KTKs[0:NS], ACT.Copy).then_inc(s["c_kta"], 1)
                    if j in (9, 10):
                        act.wait_ge(s["c_o"], h * 3 + (j - 8))
                        if not first:
                            act.wait_ge(s["c_mfree"], h * 1 + 1)
                        A(R3[:, 12 + 2 * (j - 9):14 + 2 * (j - 9), 0:SEQ], X[:, 2:4, :], ACT.Copy).then_inc(s["c_oe"], 1)
                    if j == 11:
                        act.wait_ge(s["c_o"], h * 3 + 3)
                        A(SR, X[:, 4, :], ACT.Copy).then_inc(s["c_oe"], 1)
                    if j == 8 and not first:
                        act.wait_ge(s["c_gate"], h * 4)
                    for c in range(2):
                        evac(n + j, c, R3[:, j, c * HALF:(c + 1) * HALF])
                    if j == 0 and not first:
                        squares(h - 1)
                    if j in (2, 3) and not first:
                        head_sigmoid(h - 1, 2 * j - 3)

            retention_head(0, True)
            with act.Fori(1, HC) as h:
                link.loop(h - 1, 8)
                retention_head(h, False)
                link.end(HC - 1)
            split_mixed(1)
            out_product(1, N_WA)
            split_mixed(2)
            out_product(2, N_WB)

        @block.vector
        def _(dve):
            link = Chain(dve, s["v_chain"])
            V = nc.vector
            TT, TS, STT = V.tensor_tensor, V.tensor_scalar, V.scalar_tensor_tensor

            def split_lo(n, par):
                dve.wait_ge(s["hi"], n + 1)
                TT(WL[:, par], slot[par], WH[:, par].bitcast(F32), ALU.subtract).then_inc(s["lo"], 1)

            link(V.memset(eps[:, :], EPS))
            V.memset(ssum, 0.0).then_inc(s["sqd"], 1)
            dve.wait_ge(s["vec_ps"], 3)
            link(V.tensor_copy(vecT[:, :], X[:, 0, 0:128]))
            link(V.tensor_copy(vecT2[:, :], X[:, 0, 128:152]))
            link(V.tensor_copy(craw[:, :, 0], X[:, 0, 128:144]))
            V.tensor_copy(craw[:, :, 1:9], X[:, 0, 256:384].rearrange("p (b k) -> p k b", b=NB)).then_inc(s["vec_sb"], 1)
            dve.wait_ge(s["c_exp"], 1)
            link(V.tensor_scalar_add(cexp, cexp, 1.0))
            link(V.reciprocal(cexp, cexp))
            link(V.memset(cs[:, KT * 9:], 0.0))
            TT(cs[:, 0:KT * 9].rearrange("p (k b) -> p k b", b=9), craw, cexp, ALU.mult).then_inc(s["vec_sb"], 1)
            for t in range(5):
                w = 128 if t < 4 else NS
                for q in (1, 3):
                    dve.wait_ge(s["xT_ready"], 4 * t + q + 1)
                    V.tensor_copy(R3[:, 4 * q:4 * q + 4, t * 128:t * 128 + w],
                                  X[:, q, 0:4 * w].rearrange("p (a b) -> p a b", a=4)).then_inc(s["xd"], 1)
            for k in range(KT):
                dve.wait_ge(s["xa"], k + 11)
                dve.wait_ge(s["sqd"], k + 1)
                TT(ssum, ssum, sq[:, k % 2], ALU.add).then_inc(s["sqd"], 1)
                dve.wait_ge(s["ad_sel"], k + 1)
                src = (AD[:, 256:288] if k % 2 == 0 else X[:, 4, 256:288]).rearrange("p (a b) -> p a b", b=16)[:, :, 0:9]
                TT(mod[0][:, 2 * k:2 * k + 2, :], src,
                   vecT[:, 2 * k:2 * k + 2].unsqueeze(2).to_broadcast([128, 2, 9]), ALU.add).then_inc(s["ad_ev"], 1)

            def norm(l):
                if l == 0:
                    dve.wait_ge(s["ad_ev"], 16)
                else:
                    dve.wait_ge(s["ad_ev"], 48)
                link(V.tensor_scalar_add(G, mod[l][:, KT:2 * KT, :], 1.0))
                link(TT(G, G, vecT[:, 96 + 16 * l:112 + 16 * l].unsqueeze(2).to_broadcast([128, KT, 9]), ALU.mult))
                if l == 0:
                    split_lo(0, 0)
                    split_lo(1, 1)
                dve.wait_ge(s["rb"], l + 1)

                def low(k):
                    dve.wait_ge(s["hi_t"], 17 * l + k + 1 + (k > 0))
                    STT(AL[:, k, 0:SEQ], tk[:, k % 2], mod[l][:, k, 0:1], AH[:, k, 0:SEQ].bitcast(F32),
                        ALU.add, ALU.subtract).then_inc(s["nl"], 1)

                for k in range(KT):
                    if k >= 2:
                        dve.wait_ge(s["nl"], 2 * KT * l + k - 1)
                    STT(tk[:, k % 2], R3[:, k, 0:SEQ], G[:, k, 0:1], rstd[:, 0:SEQ], ALU.mult, ALU.mult).then_inc(s["tset"], 1)
                    if k == 0:
                        link(TT(ts, R3[:, :, SEQ:T], rstd[:, SEQ:T].unsqueeze(1).to_broadcast([128, KT, NS]), ALU.mult))
                        t4 = ts.rearrange("p k (b t) -> p k b t", t=NQ)
                        h4 = hs.rearrange("p k (b t) -> p k b t", t=NQ)
                        link(TT(t4, t4, G[:, :, 1:9].unsqueeze(3).to_broadcast([128, KT, NB, NQ]), ALU.mult))
                        TT(h4, t4, mod[l][:, 0:KT, 1:9].unsqueeze(3).to_broadcast([128, KT, NB, NQ]), ALU.add).then_inc(s["sset"], 1)
                        dve.wait_ge(s["hi_t"], 17 * l + 2)
                        TT(AL[:, :, SEQ:T], hs, AH[:, :, SEQ:T].bitcast(F32), ALU.subtract).then_inc(s["nls"], 1)
                    if k > 0:
                        low(k - 1)
                low(KT - 1)

            norm(0)
            dve.wait_ge(s["res_st"], 16)
            link(V.memset(relb[32:33], 1.0))
            V.memset(biasS, NEG).then_inc(s["bs_ld"], 1)
            V.memset(LR[0:32], 1.0).then_inc(s["kn_ready"], 1)
            split_lo(2, 0)
            link(TS(qg8, vecT2[:, 22:23], 0.125, None, ALU.mult))
            dve.wait_ge(s["kv_ms"], 2)
            V.tensor_copy(relS[0:HA], X[0:HA, 2, 0:384]).then_inc(s["rel_sb"], 1)
            dve.wait_ge(s["kv_rb"], 2)
            STT(kn, QT, vecT2[:, 23:24], E, ALU.mult, ALU.mult).then_inc(s["kn_ready"], 1)
            dve.wait_ge(s["kv_ps"], 1)
            link(V.tensor_copy(vtok.rearrange("p a b -> p (a b)"), X[:, 3, :]))
            V.tensor_copy(vtok_s[0:NS], X[0:NS, 4, 0:128]).then_inc(s["kv_out_sb"], 1)
            dve.wait_ge(s["kv_ps"], 2)
            link(V.tensor_copy(E[:, 0:128], X[:, 2, 0:128]))
            V.tensor_copy(E[0:NS, 128:256], X[0:NS, 2, 128:256]).then_inc(s["kv_out_sb"], 1)
            split_lo(3, 1)
            dve.wait_ge(s["kdup_ready"], 4)
            dve.wait_ge(s["kv_ps"], 2)
            link(V.memset(S[:, 0, 0:128], NEG))
            dve.sem_inc(s["a_gate"], 1)
            dve.wait_ge(s["kv_st"], 64)

            def ada_sum(unit, dst, bias):
                dve.wait_ge(s["ad_sel"], unit)
                TT(dst, AD[:, 256:288].rearrange("p (a b) -> p a b", b=16)[:, :, 0:9],
                   vecT[:, bias].unsqueeze(2).to_broadcast([128, 2, 9]), ALU.add).then_inc(s["ad_ev"], 1)

            def tile_of(i):
                return (R3[:, i:i + 1] if isinstance(i, int) else R3[:, ds(i, 1)]).rearrange("p a t -> p (a t)")

            def probs_copied(i, e):
                dve.wait_ge(s["a_tp"], i * 2 + (e + 1))
                V.tensor_copy(PT[:, 0:2].rearrange("p b h q -> p (b h q)")[:, 128:512], X[:, 2, 128:512]).then_inc(s["a_ptV"], 1)
                link(V.memset(S[:, 0, 0:128], NEG))

            def gated(i):
                dve.wait_ge(s["a_pv"], i * 2 + 2)
                g = tile_of(i)
                TT(g[:, 0:SEQ], g[:, 0:SEQ], X[:, 4, :], ALU.mult).then_inc(s["a_gate"], 1)

            def pair_of_heads(i, first=False):
                n = i * 2 + N_A
                split_lo(n + 1, 0)
                if not first:
                    probs_copied(i - 1, 1)
                ada_sum(i * 1 + 17, mod[0][:, ds(i * 2 + 32, 2), :], ds(i * 2 + 32, 2))
                if not first:
                    gated(i - 1)
                dve.wait_ge(s["a_rb"], i * 2 + 2)
                STT(QN, QT, qg8, E, ALU.mult, ALU.mult).then_inc(s["a_qn"], 1)
                link(V.tensor_copy(sk2, sk[:, ds(i * 2, 2)]))
                split_lo(n + 2, 1)
                dve.wait_ge(s["bias_ld"], i * 16 + 16)
                for e in range(2):
                    dve.wait_ge(s["a_sc"], i * 2 + (e + 1))
                    link(TT(S[:, 0, 128:256], X[:, 0, 128:256], biasT[:, e, 128:256], ALU.add))
                    link(TT(S[:, 1], X[:, 0, 256:512], biasT[:, e], ALU.add))
                    TT(S[:, 2:4], X[:, 1, :].rearrange("p (a b) -> p a b", a=2),
                       biasT[:, e].unsqueeze(1).to_broadcast([128, 2, 256]), ALU.add).then_inc(s["a_sadd"], 1)
                    dve.wait_ge(s["a_sadd"], i * 2 + (e + 1))
                    link(V.tensor_reduce(mx, S, AX, ALU.max))
                    TS(nm, mx, sk2[:, e:e + 1], -1.0, ALU.max, ALU.mult).then_inc(s["a_mxd"], 1)
                    dve.wait_ge(s["a_exp"], i * 10 + (5 * e + 5))
                    link(TT(rec, den, es, ALU.add))
                    link(V.reciprocal(rec, rec))
                    TT(S, S, rec.unsqueeze(2).to_broadcast([128, 4, 256]), ALU.mult).then_inc(s["a_p"], 1)
                    if e == 0:
                        probs_copied(i, 0)
                dve.wait_ge(s["a_eg"], i * 1 + 1)
                g = tile_of(i)
                link(TT(g, g, E, ALU.mult))

            for i0, trips in ((1, 3), (5, 3)):
                pair_of_heads(i0 - 1, first=(i0 == 1))
                with dve.Fori(i0, i0 + trips) as i:
                    link.loop(i - i0, 14)
                    pair_of_heads(i)
                    link.end(trips)
            probs_copied(7, 1)
            gated(7)
            dve.wait_ge(s["rel_st"], 16 * 18)
            dve.wait_ge(s["s_sc"], 1)
            dve.wait_ge(s["bs_ld"], 1)
            link(TT(SS.rearrange("p (x a) b -> p x (a b)", x=2), X[:, 0:2, 0:320],
                    biasS.rearrange("p (x a) b -> p x (a b)", x=2), ALU.add))
            link(V.tensor_reduce(mx, SS, AX, ALU.max))
            TS(nm, mx, skrow, -1.0, ALU.max, ALU.mult).then_inc(s["s_mx"], 1)
            dve.wait_ge(s["s_exp"], 5)
            link(TT(rec, den, es, ALU.add))
            link(V.reciprocal(rec, rec))
            TT(SS, SS, rec.unsqueeze(2).to_broadcast([128, 4, 160]), ALU.mult).then_inc(s["s_p"], 1)
            dve.wait_ge(s["s_os"], 4 * NB)
            TT(R3[:, 0:8, SEQ:T], R3[:, 0:8, SEQ:T], OSm, ALU.mult).then_inc(s["s_gate"], 1)

            dve.wait_ge(s["vld2"], 16 * 12)
            def gla_gate(h, e):
                dve.wait_ge(s["b_rb"], h * 3 + 3)
                g = R3[:, ds(h * 2 + (8 + e), 1), :].rearrange("p a t -> p (a t)")
                dve.wait_ge(s["b_eg"], h * 2 + (e + 1))
                link(TT(g, g, sq1, ALU.mult))
                link(STT(BP[:, 2 + e], BP[:, 2 + e], vecT2[:, 16 + e:17 + e], T1, ALU.mult, ALU.mult))
                TT(g, g, BP[:, 2 + e], ALU.mult).then_inc(s["b_gate"], 1)


            def gla_head(h, first):
                n = h * 6 + N_B
                V.tensor_copy(WLH[0:RANK + 1], WLR[0:RANK + 1, ds(h * 128, 128)]).then_inc(s["b_wl"], 1)
                if not first:
                    gla_gate(h - 1, 0)
                    gla_gate(h - 1, 1)
                split_lo(n + 1, 0)
                dve.wait_ge(s["b_ln"], h * 2 + 2)
                STT(LAt.rearrange("p a b -> p (a b)"), X[:, 0, :], 0.0, T1[:, 0:SEQ], ALU.min, ALU.subtract).then_inc(s["b_la"], 1)
                STT(LAs[0:NS], X[0:NS, 1, 0:128], 0.0, T2[0:NS, 0:128], ALU.min, ALU.subtract).then_inc(s["b_la"], 1)
                ada_sum(h * 6 + 25, mod[1][:, ds(h * 12, 2), :], ds(h * 12 + 48, 2))
                dve.wait_ge(s["ev"], n * 2 + 2)
                split_lo(n + 2, 1)
                dve.wait_ge(s["b_bc"], h * 1 + 1)
                dve.wait_ge(s["b_eb"], h * 4 + 4)
                dve.wait_ge(s["b_la"], h * 2 + 2)
                bl = X[:, 2, :].rearrange("p (c t) -> p c t", t=64)
                bs = X[:, 3, 0:NS].rearrange("p (b t) -> p b t", t=NQ)
                link(V.tensor_copy(blast[:, 0:8], bl[:, :, 63]))
                link(V.tensor_copy(blast[:, 8:16], bs[:, :, NQ - 1]))
                link(TT(T1[:, 0:SEQ].rearrange("p (c t) -> p c t", t=64), blast[:, 0:8].unsqueeze(2).to_broadcast([128, 8, 64]),
                        bl, ALU.subtract))
                TT(T1[:, SEQ:T].rearrange("p (b t) -> p b t", t=NQ), blast[:, 8:16].unsqueeze(2).to_broadcast([128, NB, NQ]),
                   bs, ALU.subtract).then_inc(s["b_dif"], 1)
                link(V.tensor_copy(ebl[:, 0:8], EBP[:, 0:SEQ].rearrange("p (c t) -> p c t", t=64)[:, :, 63]))
                link(V.tensor_copy(ebl[:, 8:16], EBP[:, SEQ:T].rearrange("p (b t) -> p b t", t=NQ)[:, :, NQ - 1]))
                STT(BP[:, 0], BP[:, 0], 128.0 ** -0.5, EBP, ALU.mult, ALU.mult).then_inc(s["b_qk"], 1)
                ada_sum(h * 6 + 26, mod[1][:, ds(h * 12 + 2, 2), :], ds(h * 12 + 50, 2))
                dve.wait_ge(s["ev"], n * 2 + 4)
                dve.wait_ge(s["b_kdx"], h * 1 + 1)
                TT(T1, T1, BP[:, 1], ALU.mult).then_inc(s["b_kd"], 1)
                dve.wait_ge(s["b_kd"], h * 1 + 1)
                TT(BP[:, 1], BP[:, 1], T2, ALU.mult).then_inc(s["b_qk"], 1)
                split_lo(n + 3, 0)
                ada_sum(h * 6 + 27, mod[1][:, ds(h * 12 + 4, 2), :], ds(h * 12 + 52, 2))
                split_lo(n + 4, 1)
                dve.wait_ge(s["b_at"], h * 1 + 1)
                link(TT(AT, X[:, 0, :].rearrange("p (a b) -> p a b", a=4), gmask.unsqueeze(1).to_broadcast([128, 4, 128]), ALU.mult))
                TT(ATs[0:NS], X[0:NS, 1, 0:NS], smask[0:NS, 0:NS], ALU.mult).then_inc(s["b_atm"], 1)
                ada_sum(h * 6 + 28, mod[1][:, ds(h * 12 + 6, 2), :], ds(h * 12 + 54, 2))
                split_lo(n + 5, 0)
                ada_sum(h * 6 + 29, mod[1][:, ds(h * 12 + 8, 2), :], ds(h * 12 + 56, 2))
                split_lo(n + 6, 1)
                for c in range(8):
                    dS = X[:, (c % 2) * 2 + c // 4, (c // 2 % 2) * 256:(c // 2 % 2) * 256 + 256]
                    if c == 0:
                        dve.wait_ge(s["b_dS"], h * 1 + 1)
                        dve.wait_ge(s["b_free"], h * 1 + 1)
                        V.tensor_copy(ST[:, 0], dS).then_inc(s["b_st"], 1)
                    else:
                        dve.wait_ge(s["b_st"], h * 8 + c)
                        STT(ST[:, c], ST[:, c - 1], ebl[:, c:c + 1], dS, ALU.mult, ALU.add).then_inc(s["b_st"], 1)
                ada_sum(h * 6 + 30, mod[1][:, ds(h * 12 + 10, 2), :], ds(h * 12 + 58, 2))
                dve.wait_ge(s["b_kta"], h * 5 + 5)
                dve.wait_ge(s["b_vta"], h * 4 + 4)
                link(TT(BKS[2 * NS:3 * NS], KDTs[0:NS], BKM[0:NS, 0].bitcast(F32), ALU.subtract))
                link(TT(BVS[NS:2 * NS], VTBs[0:NS], BVS[0:NS].bitcast(F32), ALU.subtract))
                for b in range(NB):
                    if b >= 2:
                        dve.wait_ge(s["b_ssb"], h * 8 + (b - 1))
                    TS(BKM[:, b % 2], BKS, bmask[0:3 * NS, b:b + 1], None, ALU.mult).then_inc(s["b_kdm"], 1)
                    dve.wait_ge(s["b_ssb"], h * 8 + (b + 1))
                    STT(ST[:, b], ST[:, b], ebl[:, 8 + b:9 + b], X[:, 2 + b % 2, 0:256], ALU.mult, ALU.add).then_inc(s["b_sup"], 1)
                dve.wait_ge(s["b_rb"], h * 3 + 2)
                TT(T1, T1, sq1, ALU.add).then_inc(s["b_sq1"], 1)

            gla_head(0, True)
            with dve.Fori(1, HB) as h:
                link.loop(h - 1, 12)
                gla_head(h, False)
                link.end(HB - 1)

            def split_mixed(w):
                for k in range(KT):
                    if w == 0 and k in (0, 7):
                        gla_gate(HB - 1, k // 7)
                    dve.wait_ge(s["m_hi"], KT * w + k + 1)
                    TT(AL[:, k], rel8[:, k - 8] if w == 1 and k >= 8 else R3[:, k], AH[:, k].bitcast(F32), ALU.subtract).then_inc(s["nl"], 1)

            def out_product(w, base, l):
                if w == 0:
                    dve.wait_ge(s["b_free"], HB + 1)
                    link(V.memset(ssum, 0.0))
                if w == 2:
                    for j in range(2):
                        dve.wait_ge(yst_s[j], 256)
                def tiles(m, first=False, last=False):
                    for j in range(2):
                        n = m * 2 + (base + j)
                        if not (last and j == 1):
                            split_lo(n + 1, (base + j + 1) % 2)
                        if w == 1 and first and j == 0:
                            head_squares(HC - 1)
                        if w == 1 and first and j == 1:
                            gates(HC - 1, 0)
                        dve.wait_ge(rld[j], m * 16 + (128 * w + 16))
                        y = R3[:, ds(m * 2 + j, 1), :].rearrange("p a t -> p (a t)") if w == 0 else yst[:, j]
                        gp = mod[l][:, ds(m * 2 + (32 + j), 1), 0:1].rearrange("p a b -> p (a b)")
                        gs = mod[l][:, ds(m * 2 + (32 + j), 1), 1:9].rearrange("p a b -> p (a b)")
                        link(V.tensor_copy(eps[:, 6:7], gp))
                        if w == 1:
                            dve.wait_ge(yst_s[j], m * 16 + 128)
                        if w == 2:
                            dve.wait_ge(s["wtp"], m * 2 + (j + 1))
                        dve.wait_ge(s["half"], n * 2 + 1)
                        STT(y[:, 0:HALF], PJ[:, 0, 0:HALF], eps[:, 6:7], resb[:, j, 0:HALF], ALU.mult, ALU.add).then_inc(s["ev"], 1)
                        dve.wait_ge(s["half"], n * 2 + 2)
                        link(STT(y[:, HALF:SEQ], PJ[:, 1, 0:SEQ - HALF], eps[:, 6:7], resb[:, j, HALF:SEQ], ALU.mult, ALU.add))
                        TT(smp.rearrange("p (b t) -> p b t", t=NQ), PJ[:, 1, SEQ - HALF:HALF].rearrange("p (b t) -> p b t", t=NQ),
                           gs.unsqueeze(2).to_broadcast([128, NB, NQ]), ALU.mult).then_inc(s["ev"], 1)
                        dve.wait_ge(s["ev"], n * 2 + 2)
                        TT(y[:, SEQ:T], smp, resb[:, j, SEQ:T], ALU.add).then_inc(s["wy"], 1)
                        if w == 1 and first and j == 1:
                            gates(HC - 1, 1)
                        if w == 0:
                            dve.wait_ge(s["wsqa"], m * 2 + (j + 1))
                            TT(ssum, ssum, wsq, ALU.add).then_inc(s["wssq"], 1)
                            dve.wait_ge(s["wssq"], m * 2 + (j + 1))

                tiles(0, first=True)
                with dve.Fori(1, KT // 2 - 1) as m:
                    link.loop(m - 1, 4)
                    tiles(m)
                    link.end(KT // 2 - 2)
                tiles(KT // 2 - 1, last=(w == 2))

            split_mixed(0)
            out_product(0, N_W0, 0)
            norm(1)
            dve.wait_ge(s["c_tab"], 32)
            def head_squares(h):
                for e in range(4):
                    dve.wait_ge(s["c_rb"], h * 6 + (e + 1))
                    if e == 0:
                        V.tensor_copy(r3, r1).then_inc(s["c_ssq"], 1)
                    else:
                        dve.wait_ge(s["c_ssq"], h * 4 + e)
                        TT(r3, r3, (r1, r2)[e % 2], ALU.add).then_inc(s["c_ssq"], 1)

            def gates(h, part):
                dve.wait_ge(s["c_rb"], h * 6 + 6)
                for e in (2 * part, 2 * part + 1):
                    g, o = R3[:, 8 + e], R3[:, 12 + e]
                    dve.wait_ge(s["c_eg"], h * 4 + (e + 1))
                    link(TT(g, g, r2, ALU.mult))
                    link(STT(o, o, vecT2[:, 18 + e:19 + e], r1, ALU.mult, ALU.mult))
                    TT(o, o, g, ALU.mult).then_inc(s["c_gate"], 1)

            def update_states(h, b0):
                for b in range(b0, b0 + 4):
                    TS(KM, KS, RT[0:3 * NS, T + NS + b:T + NS + b + 1], None, ALU.mult).then_inc(s["c_km"], 1)
                    for kk in range(2):
                        dve.wait_ge(s["c_up"], h * 16 + (2 * b + kk + 1))
                        STT(SB[:, b % 4, kk], SB[:, b % 4, kk], RT[:, T + NS + NB + 4:T + NS + NB + 5],
                            X[:, kk, :], ALU.mult, ALU.add).then_inc(s["c_upv"], 1)

            def retention_head(h, first):
                n = h * 12 + N_C
                split_lo(n + 1, (N_C + 1) % 2)
                if not first:
                    head_squares(h - 1)
                split_lo(n + 2, N_C % 2)
                split_lo(n + 3, (N_C + 1) % 2)
                if not first:
                    gates(h - 1, 0)
                split_lo(n + 4, N_C % 2)
                if not first:
                    gates(h - 1, 1)
                split_lo(n + 5, (N_C + 1) % 2)
                for x in range(2):
                    dve.wait_ge(s["ev"], n * 2 + (4 + 4 * x))
                    x1, x2 = R3[:, 2 * x], R3[:, 2 * x + 1]
                    if x == 1:
                        dve.wait_ge(s["c_rot"], h * 2 + 1)
                    link(TT(r3, x1, sin, ALU.mult))
                    link(TT(r2, x2, sin, ALU.mult))
                    link(TT(x1, x1, cos, ALU.mult))
                    link(TT(x1, x1, r2, ALU.subtract))
                    link(TT(x2, x2, cos, ALU.mult))
                    TT(x2, x2, r3, ALU.add).then_inc(s["c_rot"], 1)
                split_lo(n + 6, N_C % 2)
                dve.wait_ge(s["c_tab"], h * 16 + 32)
                dve.wait_ge(s["c_rot"], h * 2 + 2)
                for kk in range(2):
                    link(TT(qi[:, kk], R3[:, kk, SEQ:T], RT[:, T:T + NS], ALU.mult))
                dve.wait_ge(s["c_sc"], h * 1 + 1)
                dve.wait_ge(s["c_kt"], h * 1 + 1)
                for t, src in enumerate((X[:, 0, 0:512], X[:, 1, 0:384], X[:, 2, 0:256], X[:, 1, 384:512])):
                    link(TT(RAT[:, RAOFF[t]:RAOFF[t] + SEQ - 128 * t], src, RT[:, 0:SEQ - 128 * t], ALU.mult))
                TT(RATs[0:NS], X[0:NS, 2, 256:256 + NS], RT[0:NS, SEQ:T], ALU.mult).then_inc(s["c_scv"], 1)
                link(V.memset(qk_flat[:, 1632:2144], 0.0))
                for kk in range(2):
                    at = 1632 + 256 * kk
                    V.tensor_copy(qk_flat[:, at:at + NB * (NS + NQ)].rearrange("p (b u) -> p b u", b=NB)[:, :, 0:NQ],
                                  qi[:, kk].rearrange("p (b t) -> p b t", t=NQ)).then_inc(s["c_scv"], 1)
                split_lo(n + 7, (N_C + 1) % 2)
                split_lo(n + 8, N_C % 2)
                dve.wait_ge(s["c_vt"], h * 1 + 1)
                V.tensor_copy(CT[:, 2:4], X[:, 2:4, :]).then_inc(s["c_vtv"], 1)
                dve.wait_ge(s["c_vta"], h * 4 + 4)
                TT(VS[NS:2 * NS], CTs[0:NS], VS[0:NS].bitcast(F32), ALU.subtract).then_inc(s["c_vtv"], 1)
                dve.wait_ge(s["c_kta"], h * 8 + 8)
                TT(KS[2 * NS:3 * NS], KTKs[0:NS], KM[0:NS].bitcast(F32), ALU.subtract).then_inc(s["c_vtv"], 1)
                split_lo(n + 9, (N_C + 1) % 2)
                dve.wait_ge(s["c_vtv"], h * 3 + 3)
                if not first:
                    dve.wait_ge(s["c_pfree"], h * 1 + 1)
                for kk in range(2):
                    dve.wait_ge(s["c_st"], h * 2 + (kk + 1))
                    V.tensor_copy(CST[:, kk], X[:, kk, :]).then_inc(s["c_stv"], 1)
                split_lo(n + 10, N_C % 2)
                update_states(h, 0)
                split_lo(n + 11, (N_C + 1) % 2)
                split_lo(n + 12, N_C % 2)
                update_states(h, 4)

            retention_head(0, True)
            with dve.Fori(1, HC) as h:
                link.loop(h - 1, 25)
                retention_head(h, False)
                link.end(HC - 1)
            split_mixed(1)
            out_product(1, N_WA, 1)
            split_mixed(2)
            out_product(2, N_WB, 1)

        @block.tensor
        def _(pe):
            mm = nc.tensor.matmul

            def nothing():
                pass

            def tr(out, in_, rows=128):
                return nc.tensor.transpose(out, in_, ident[0:rows, 0:rows])

            def product(n, par, ready=None, between=()):
                for c in range(2):
                    product_half(n, par, c, ready, between[2 * c:2 * c + 2])

            def product_half(n, par, c, ready=None, between=()):
                if c == 0:
                    pe.wait_ge(s["lo"], n + 1)
                if not (isinstance(n, int) and n == 0):
                    pe.wait_ge(s["ev"], n * 2 + (c - 1))
                for k in range(KT):
                    if ready is not None and c == 0:
                        pe.wait_ge(s["nl"], ready + k + 1)
                    for a, (w, x) in enumerate(((WH, AH), (WH, AL), (WL, AH))):
                        last = mm(PJ[:, c, 0:HALF], w[:, par, k], x[:, k, c * HALF:(c + 1) * HALF],
                                  start=(k == 0 and a == 0), stop=(k == KT - 1 and a == 2))
                    if k == KT // 2 - 1 and between:
                        between[0]()
                last.then_inc(s["half"], 1)
                if between:
                    between[1]()

            def sum_rows(lhs, src, banks=(0, 1)):
                for c in range(2):
                    last = mm(X[:, banks[c], 0:HALF], lhs, src[:, c * HALF:(c + 1) * HALF], start=True, stop=True)
                return last

            def ada_rows(w, bank):
                for k in range(KT):
                    g = 32 * (k % 4)
                    last = mm(bank[g:g + 32, 0:256], cs[:, 9 * k:9 * k + 32], w[:, k], start=(k < 4), stop=(k >= KT - 4),
                              tile_position=(0, g))
                last.then_inc(s["ad_done"], 1)

            def ada_select(unit, rows, bank):
                pe.wait_ge(s["ad_rows"], unit)
                for e in range(2):
                    last = mm(bank[:, 256 + 16 * e:256 + 16 * e + 9], rows[:, 128 * e:128 * e + 128], sel[:, 0:9],
                              start=True, stop=True)
                last.then_inc(s["ad_sel"], 1)

            pe.wait_ge(s["vld"], 16 * 15)
            tr(X[:, 0, 0:128], vr).then_inc(s["vec_ps"], 1)
            tr(X[:, 0, 128:152], vr2[0:24], 24).then_inc(s["vec_ps"], 1)
            tr(X[:, 0, 256:384], vc).then_inc(s["vec_ps"], 1)
            pe.wait_ge(s["vec_sb"], 1)
            for t in range(5):
                w = 128 if t < 4 else NS
                pe.wait_ge(xld[t % 2], 16 * (t // 2 + 1))
                for q in range(4):
                    if t > 0:
                        pe.wait_ge(s["xa" if q % 2 == 0 else "xd"], 2 * (t - 1) + q // 2 + 1)
                    for a in range(4):
                        last = tr(X[:, q, a * w:(a + 1) * w], xs[0:w, t % 2, (4 * q + a) * 128:(4 * q + a + 1) * 128], w)
                    last.then_inc(s["xT_ready"], 1)
            pe.wait_ge(s["vec_sb"], 2)

            def ada_slab(i, sl):
                pe.wait_ge(adl[sl], i * 16 + 16)
                ada_rows(slab[sl], AD if sl == 0 else X[:, 4])

            def ada_slabs_select(i):
                for sl in range(2):
                    ada_select(i * 2 + (sl + 1), arow0[:, sl], AD if sl == 0 else X[:, 4])

            ada_slab(0, 0)
            ada_slab(0, 1)
            ada_slabs_select(0)
            with pe.Fori(1, 8) as i:
                for sl in range(2):
                    pe.wait_ge(s["ad_ev"], i * 2 + (sl - 1))
                    ada_slab(i, sl)
                ada_slabs_select(i)
            pe.wait_ge(s["sqd"], KT + 1)
            pe.wait_ge(s["xa"], 10)
            pe.wait_ge(s["xd"], 10)
            sum_rows(ones[:, :], ssum).then_inc(s["ms"], 1)
            pe.wait_ge(s["nls"], 1)
            product(0, 0, ready=0)
            product(1, 1)
            pe.wait_ge(s["vld2"], 16 * 12)
            pe.wait_ge(s["kv_rb"], 1)
            sum_rows(blk64, E).then_inc(s["kv_ms"], 1)
            pe.wait_ge(s["kn_ready"], 1)
            mm(X[0:HA, 2, 0:384], relb[0:33], hot[0:33], start=True, stop=True).then_inc(s["kv_ms"], 1)
            pe.wait_ge(s["ev"], 4)
            for t in range(4):
                tr(X[:, 3, 128 * t:128 * t + 128], QN[:, 128 * t:128 * t + 128])
            tr(X[0:NS, 4, 0:128], QN[:, SEQ:T]).then_inc(s["kv_ps"], 1)
            product(2, 0)
            pe.wait_ge(s["kn_ready"], 2)
            pe.wait_ge(s["rel_sb"], 1)
            tr(X[:, 2, 0:128], kn[:, SEQ - 128:SEQ])
            tr(X[0:NS, 2, 128:256], kn[:, SEQ:T]).then_inc(s["kv_ps"], 1)
            pe.wait_ge(s["kv_rb"], 2)
            for b in range(NB):
                last = tr(X[:, b // 4, (b % 4) * 128:(b % 4) * 128 + 128], KC[:, b])
                if b % 4 == 3:
                    last.then_inc(s["kct_ps"], 1)
            pe.wait_ge(s["kdup_ready"], 4)
            pe.wait_ge(s["kv_out_sb"], 2)
            pe.wait_ge(s["kct_sb"], 1)

            def product_and_ada(n, par, unit, loaded, between=()):
                pe.wait_ge(s["ad_ev"], unit)
                pe.wait_ge(adl[1], loaded)
                ada_rows(slab[1], AD)
                product_half(n, par, 0, between=between[0:2])
                ada_select(unit + 1, arow, AD)
                product_half(n, par, 1, between=between[2:4])

            def probs_transposed(i, e):
                pe.wait_ge(s["a_p"], i * 2 + (e + 1))
                for b in range(4):
                    for f in range(2):
                        if b == 0 and f == 0:
                            continue
                        last = tr(X[:, 2 + b // 2, (b % 2) * 256 + f * 128:(b % 2) * 256 + f * 128 + 128],
                                  S[:, b, f * 128:f * 128 + 128])
                last.then_inc(s["a_tp"], 1)

            def head_outputs(i, e, kv):
                r = slice(64 * e, 64 * e + 64)
                pe.wait_ge(s["a_ptA"], i * 2 + (e + 1))
                pe.wait_ge(s["a_ptV"], i * 2 + (e + 1))
                if e == 0:
                    pe.wait_ge(s["a_gate"], i * 1 + 1)
                for b in range(4):
                    out = X[r, 4, 128 * b:128 * b + 128]
                    if b > 0:
                        mm(out, vtok[:, b - 1, 64 * kv:64 * kv + 64], PT[:, b, 0], start=True, stop=False)
                    last = mm(out, vtok[:, b, 64 * kv:64 * kv + 64], PT[:, b, 1], start=(b == 0), stop=True)
                last.then_inc(s["a_pv"], 1)

            def scores(i, e, kv):
                r = slice(64 * e, 64 * e + 64)
                for b in range(4):
                    bank = X[:, b // 2, (b % 2) * 256:(b % 2) * 256 + 256]
                    if b == 0:
                        last = mm(bank[:, 128:256], QN[r, 0:128], kdup[kv][r, 0:128], start=True, stop=True)
                    else:
                        last = mm(bank, QN[r, 128 * b:128 * b + 128], kdup[kv][r, 128 * b - 128:128 * b + 128],
                                  start=True, stop=True)
                last.then_inc(s["a_sc"], 1)

            def query_norm(i):
                pe.wait_ge(s["a_rb"], i * 2 + 1)
                sum_rows(blk64, E).then_inc(s["a_ms"], 1)

            def pair_of_heads(i, kv, before):
                n = i * 2 + N_A
                if before is None:
                    product_and_ada(n, 1, i * 1 + 16, i * 16 + 144)
                else:
                    product_and_ada(n, 1, i * 1 + 16, i * 16 + 144,
                                    between=[nothing, lambda: probs_transposed(i - 1, 1),
                                             lambda: head_outputs(i - 1, 1, before), nothing])
                product_half(n + 1, 0, 0, between=[lambda: query_norm(i), nothing])
                pe.wait_ge(s["a_qn"], i * 1 + 1)
                scores(i, 0, kv)
                product_half(n + 1, 0, 1)
                probs_transposed(i, 0)
                pe.wait_ge(s["a_mxd"], i * 2 + 1)
                scores(i, 1, kv)
                head_outputs(i, 0, kv)

            for kv in range(2):
                pair_of_heads(4 * kv, kv, 0 if kv else None)
                with pe.Fori(4 * kv + 1, 4 * kv + 4) as i:
                    pair_of_heads(i, kv, kv)
            probs_transposed(7, 1)
            head_outputs(7, 1, 1)
            pe.wait_ge(s["a_gate"], 9)
            pe.wait_ge(s["a_qs"], 16)
            for p in range(4):
                for e in range(2):
                    for kv in range(2):
                        b = 2 * p + e
                        r = slice(64 * kv, 64 * kv + 64)
                        rows = slice(64 * e + 32 * kv, 64 * e + 32 * kv + 32)
                        q = qsT[r, b].rearrange("p g t -> p (g t)")
                        at = (p % 2) * 160
                        mm(X[rows, p // 2, at:at + 128], q, KCT[r, b], start=True, stop=True)
                        last = mm(X[rows, p // 2, at + 128:at + 160], q, kdup[kv][r, SEQ:T], start=True, stop=True)
            last.then_inc(s["s_sc"], 1)
            pe.wait_ge(s["s_p"], 1)
            for p in range(4):
                last = tr(X[:, 2, 128 * p:128 * p + 128], SS[:, p, 0:128])
            last.then_inc(s["s_tp"], 1)
            for p in range(4):
                last = tr(X[0:NS, 3, 128 * p:128 * p + 128], SS[:, p, 128:160])
            last.then_inc(s["s_tp"], 1)
            pe.wait_ge(s["s_pt"], 2)
            for b in range(NB):
                for kv in range(2):
                    cols = slice(64 * (b % 2) + 32 * kv, 64 * (b % 2) + 32 * kv + 32)
                    out = X[64 * kv:64 * kv + 64, 4, 32 * b:32 * b + 32]
                    mm(out, VCc[:, b, 64 * kv:64 * kv + 64], PTs[:, b // 2, cols], start=True, stop=False)
                    last = mm(out, vtok_s[0:NS, 64 * kv:64 * kv + 64], PTn[0:NS, b // 2, cols], start=False, stop=True)
            last.then_inc(s["s_pv"], 1)

            pe.wait_ge(s["s_gate"], 1)
            pe.wait_ge(s["vld2"], 16 * 12)
            pe.wait_ge(s["ev"], 6)
            with pe.Fori(0, HB) as h:
                n = h * 6 + N_B

                def product_ada(j, between=()):
                    product_and_ada(n + j, (N_B + j) % 2, h * 6 + (24 + j), h * 96 + (272 + 16 * j), between)

                pe.wait_ge(s["b_wl"], h * 1 + 1)
                for t in range(4):
                    last = mm(X[:, 0, 128 * t:128 * t + 128], LR[0:RANK + 1, 128 * t:128 * t + 128],
                              WLH[0:RANK + 1], start=True, stop=True)
                last.then_inc(s["b_z"], 1)
                mm(X[0:NS, 1, 0:128], LR[0:RANK + 1, SEQ:T], WLH[0:RANK + 1],
                   start=True, stop=True).then_inc(s["b_z"], 1)
                product_ada(0)
                def cumulated_decay():
                    pe.wait_ge(s["b_la"], h * 2 + 2)
                    for t in range(4):
                        mm(X[:, 2, 128 * t:128 * t + 128], LAt[:, t], gmask, start=True, stop=True)
                    mm(X[:, 3, 0:NS], LAs[0:NS], smask[0:NS, 0:NS], start=True, stop=True).then_inc(s["b_bc"], 1)

                product_ada(1, between=[cumulated_decay] + [nothing] * 3)
                product_ada(2)
                pe.wait_ge(s["b_qk"], h * 2 + 2)
                for t in range(4):
                    mm(X[:, 0, 128 * t:128 * t + 128], BP[:, 1, 128 * t:128 * t + 128], BP[:, 0, 128 * t:128 * t + 128],
                       start=True, stop=True)
                mm(X[0:NS, 1, 0:NS], BP[:, 1, SEQ:T], BP[:, 0, SEQ:T], start=True, stop=True).then_inc(s["b_at"], 1)
                pe.wait_ge(s["b_kd"], h * 1 + 1)
                for t in range(4):
                    tr(X[:, 2, 128 * t:128 * t + 128], T1[:, 128 * t:128 * t + 128])
                tr(X[0:NS, 3, 0:128], T1[:, SEQ:T]).then_inc(s["b_kt"], 1)
                product_ada(3)
                pe.wait_ge(s["ev"], n * 2 + 8)
                pe.wait_ge(s["b_atm"], h * 1 + 1)
                pe.wait_ge(s["b_kta"], h * 5 + 5)
                for t in range(4):
                    for e in range(2):
                        tr(X[:, t // 2, (t % 2) * 256 + 128 * e:(t % 2) * 256 + 128 * e + 128],
                           BP[:, 2 + e, 128 * t:128 * t + 128])
                tr(X[0:NS, 2, 0:128], BP[:, 2, SEQ:T])
                tr(X[0:NS, 2, 128:256], BP[:, 3, SEQ:T]).then_inc(s["b_vt"], 1)
                product_ada(4)
                pe.wait_ge(s["b_vta"], h * 4 + 4)
                for c in range(8):
                    r = slice(64 * (c % 2), 64 * (c % 2) + 64)
                    last = mm(X[:, (c % 2) * 2 + c // 4, (c // 2 % 2) * 256:(c // 2 % 2) * 256 + 256], KDT[r, c // 2], VTB[r, c // 2],
                              start=True, stop=True)
                last.then_inc(s["b_dS"], 1)
                def prompt_outputs():
                    pe.wait_ge(s["b_st"], h * 8 + 8)
                    for e in range(2):
                        ec = slice(128 * e, 128 * e + 128)
                        for t in range(4):
                            mm(X[:, e, 128 * t:128 * t + 128], VTB[:, t, ec], AT[:, t], start=True, stop=False)
                            for c in (2 * t, 2 * t + 1):
                                if c > 0:
                                    last = mm(X[:, e, 64 * c:64 * c + 64], ST[:, c - 1, ec], BP[:, 0, 64 * c:64 * c + 64],
                                              start=False, stop=(c % 2 == 1))
                        last.then_inc(s["b_o"], 1)

                product_ada(5, between=[nothing, prompt_outputs, nothing, nothing])
                pe.wait_ge(s["b_sld"], h * 16 + 16)
                for e in range(2):
                    ec = slice(128 * e, 128 * e + 128)
                    mm(X[:, 4, NS * e:NS * e + NS], VTBs[0:NS, ec], ATs[0:NS], start=True, stop=False)
                    for b in range(NB):
                        last = mm(X[:, 4, NS * e + NQ * b:NS * e + NQ * b + NQ], ST[:, b, ec],
                                  BP[:, 0, SEQ + NQ * b:SEQ + NQ * b + NQ], start=False, stop=(b == NB - 1))
                last.then_inc(s["b_so"], 1)
                for b in range(NB):
                    pe.wait_ge(s["b_kdm"], h * 8 + (b + 1))
                    if b >= 2:
                        pe.wait_ge(s["b_sup"], h * 8 + (b - 1))
                    mm(X[:, 2 + b % 2, 0:256], BKM[:, b % 2], BVS, start=True, stop=True).then_inc(s["b_ssb"], 1)
                pe.wait_ge(s["b_sq1"], h * 1 + 1)
                sum_rows(ones[:, :], T1).then_inc(s["b_ms"], 1)
                pe.wait_ge(s["b_rb"], h * 3 + 3)
                pe.wait_ge(s["b_sup"], h * 8 + 8)

            def transposed(r, j):
                pe.wait_ge(s["wy"], r + 33)
                if not (isinstance(r, int) and r == 0):
                    pe.wait_ge(s["wotp"], r * 2)
                for t in range(4):
                    tr(X[:, j, 128 * t:128 * t + 128], yst[:, j, 128 * t:128 * t + 128])
                tr(X[0:NS, 2 + j, 0:128], yst[:, j, SEQ:T]).then_inc(s["wtp"], 1)

            def out_product(w, base, ready):
                p0, p1 = base % 2, (base + 1) % 2
                def beside(r, j):
                    return [lambda: transposed(r, j)] + [lambda: None] * 3 if w == 2 else ()

                product(base, p0, ready=ready)
                if w == 1:
                    head_norm(HC - 1)
                product(base + 1, p1, between=beside(0, 0))
                with pe.Fori(1, KT // 2) as m:
                    product(m * 2 + base, p0, between=beside(m * 2 - 1, 1))
                    product(m * 2 + (base + 1), p1, between=beside(m * 2, 0))
                if w == 2:
                    transposed(KT - 1, 1)

            out_product(0, N_W0, KT)
            pe.wait_ge(s["wssq"], KT)
            sum_rows(ones[:, :], ssum).then_inc(s["ms"], 1)
            pe.wait_ge(s["nls"], 2)
            def head_norm(h):
                pe.wait_ge(s["c_oe"], h * 4 + 2)
                pe.wait_ge(s["c_ssq"], h * 4 + 4)
                sum_rows(ones[:, :], r3, banks=(2, 3)).then_inc(s["c_ms"], 1)

            def sample_outputs(h, b0):
                for b in range(b0, b0 + 4):
                    pe.wait_ge(sld[b % 4], h * 32 + (16 * (b // 4) + 16))
                for kk in range(2):
                    for b in range(b0, b0 + 4):
                        g = 32 * (b % 4)
                        last = mm(X[g:g + 32, 4, :], Qpad[:, kk, b], SB[:, b % 4, kk], start=(b < 4 and kk == 0),
                                  stop=(b >= 4 and kk == 1), tile_position=(0, g))
                return last

            def state_update(h, b):
                pe.wait_ge(s["c_km"], h * 8 + (b + 1))
                for kk in range(2):
                    if b >= 1:
                        pe.wait_ge(s["c_upv"], h * 16 + (2 * b - 1 + kk))
                    mm(X[:, kk, :], KM[:, 128 * kk:128 * kk + 128], VS, start=True, stop=True)\
                        .then_inc(s["c_up"], 1)

            def retention_head(h, first):
                n = h * 12 + N_C
                product(n, N_C % 2, ready=2 * KT if first else None)
                product(n + 1, (N_C + 1) % 2)
                if not first:
                    head_norm(h - 1)
                for j in range(2, 6):
                    product(n + j, (N_C + j) % 2)
                pe.wait_ge(s["c_rot"], h * 2 + 2)
                if not first:
                    pe.wait_ge(s["c_rb"], h * 6 - 1)
                for t, out in enumerate((X[:, 0, 0:512], X[:, 1, 0:384], X[:, 2, 0:256], X[:, 1, 384:512])):
                    for kk in range(2):
                        mm(out, R3[:, 2 + kk, 128 * t:128 * t + 128], R3[:, kk, 128 * t:SEQ], start=(kk == 0), stop=(kk == 1))
                for kk in range(2):
                    last = mm(X[0:NS, 2, 256:256 + NS], R3[:, 2 + kk, SEQ:T], R3[:, kk, SEQ:T], start=(kk == 0), stop=(kk == 1))
                last.then_inc(s["c_sc"], 1)
                for t in range(4):
                    for kk in range(2):
                        tr(X[:, 3 + t // 2, (t % 2) * 256 + 128 * kk:(t % 2) * 256 + 128 * kk + 128],
                           R3[:, 2 + kk, 128 * t:128 * t + 128])
                for kk in range(2):
                    last = tr(AD[0:NS, 128 * kk:128 * kk + 128], R3[:, 2 + kk, SEQ:T])
                last.then_inc(s["c_kt"], 1)
                product(n + 6, N_C % 2)
                product(n + 7, (N_C + 1) % 2)
                pe.wait_ge(s["ev"], n * 2 + 16)
                pe.wait_ge(s["c_scv"], h * 3 + 3)
                pe.wait_ge(s["c_kta"], h * 8 + 5)
                for t in range(4):
                    for e in range(4):
                        tr(X[:, t, 128 * e:128 * e + 128], R3[:, 4 + e, 128 * t:128 * t + 128])
                for e in range(4):
                    last = tr(X[0:NS, 4, 128 * e:128 * e + 128], R3[:, 4 + e, SEQ:T])
                last.then_inc(s["c_vt"], 1)
                product(n + 8, N_C % 2)
                pe.wait_ge(s["c_vta"], h * 4 + 4)
                pe.wait_ge(s["c_vtv"], h * 3 + 3)
                for kk in range(2):
                    for t in range(4):
                        last = mm(X[:, kk, :], KTK[:, t, 128 * kk:128 * kk + 128], CT[:, t], start=(t == 0), stop=(t == 3))
                    last.then_inc(s["c_st"], 1)

                def outputs(g):
                    for e in (2 * g, 2 * g + 1):
                        for t in range(4):
                            last = mm(X[:, 2 + e % 2, 128 * t:SEQ], CT[:, t, 128 * e:128 * e + 128],
                                      RAT[:, RAOFF[t]:RAOFF[t] + SEQ - 128 * t], start=(t == 0), stop=(t == 3))
                    last.then_inc(s["c_o"], 1)

                outputs(0)
                sample_outputs(h, 0)
                pe.wait_ge(s["c_stv"], h * 2 + 2)
                product(n + 9, (N_C + 1) % 2, between=[lambda b=b: state_update(h, b) for b in range(4)])
                pe.wait_ge(s["c_oe"], h * 4 + 1)
                outputs(1)
                product(n + 10, N_C % 2)
                sample_outputs(h, 4).then_inc(s["c_o"], 1)
                product(n + 11, (N_C + 1) % 2, between=[lambda b=b: state_update(h, b) for b in range(4, 8)])
                pe.wait_ge(s["c_oe"], h * 4 + 3)
                for e in range(4):
                    mm(AD[:, NS * e:NS * e + NS], CTs[0:NS, 128 * e:128 * e + 128], RATs[0:NS], start=True, stop=False)
                    last = mm(AD[:, NS * e:NS * e + NS], SR[:, 128 * e:128 * e + 128], sel[:, :], start=False, stop=True)
                last.then_inc(s["c_os"], 1)

            retention_head(0, True)
            with pe.Fori(1, HC) as h:
                retention_head(h, False)
            out_product(1, N_WA, 3 * KT)
            pe.sem_inc(s["wtp"], 2)
            out_product(2, N_WB, 4 * KT)


_OUTS = [(1, SEQ, D), (NB, NQ, D), (1, 1, WIN, 2, 64), (1, 1, WIN, 2, 64), (1, 1, HB, 128, 256), (1, 1, HC, 256, 512),
         (1, NB, WIN, 2, 64), (1, NB, WIN, 2, 64), (1, NB, HB, 128, 256), (1, NB, HC, 256, 512)]


def kernel(**inputs):
    import concourse.bacc as _bacc
    from concourse.bass_utils import run_bass_kernel_spmd as _run

    nc = _bacc.Bacc("TRN2", target_bir_lowering=False, num_devices=1)
    arrays, ins, consts = {}, {}, {}
    for name in inputs:
        a = np.ascontiguousarray(inputs[name])
        arrays[f"in_{name}"] = a
        ins[name] = nc.dram_tensor(f"in_{name}", a.shape, mybir.dt.from_np(a.dtype), kind="ExternalInput").ap()
    for name, a in shape_constants().items():
        arrays[f"const_{name}"] = a
        consts[name] = nc.dram_tensor(f"const_{name}", a.shape, F32, kind="ExternalInput").ap()
    outs = [nc.dram_tensor(f"out_{i}", shape, F32, kind="ExternalOutput").ap() for i, shape in enumerate(_OUTS)]
    build(nc, ins, outs, consts)
    r = _run(nc, [arrays], core_ids=[0])
    return tuple(r.results[0][f"out_{i}"] for i in range(len(_OUTS)))
```
